# Optimizing a Trainium2 kernel written in Bass

```python
import jax, jax.numpy as jnp
from jax import lax
import numpy as np

D_MODEL = 1024
BATCH = 1
SEQ = 512
DEPTH = 2

GRID_W = 64
CTX_LEN = 256
HEAD_DIM = 64
NORM_EPS = 1e-6
NA_HEADS = 8
NA_WIN_ROWS = 8
NA_WIN_COLS = 16
NA_W = NA_HEADS * HEAD_DIM
SW_HEADS = 8
SW_KV_HEADS = 2
SW_WINDOW = 128
SW_BLOCK = 128
SW_QW = SW_HEADS * HEAD_DIM
SW_KVW = SW_KV_HEADS * HEAD_DIM
ROPE_THETA = 10000.0
ROPE_FREQS = HEAD_DIM // 4
CONV_WIDTH = 512
CONV_K = 3
D_FF = -(-8 * D_MODEL // (3 * 256)) * 256
N_BRANCHES = 3
IN_SPLITS = (NA_W, NA_W, NA_W, SW_QW, SW_KVW, SW_KVW, CONV_WIDTH, CONV_WIDTH, CONV_WIDTH, N_BRANCHES * D_MODEL)
N_IN = sum(IN_SPLITS)

kernel_name = "hybrid_dit_natten_swa_shortconv"

def rms_norm(x, g):
    xf = x.astype(jnp.float32)
    y = xf * lax.rsqrt(jnp.mean(xf * xf, axis=-1, keepdims=True) + NORM_EPS)
    return (y * g.astype(jnp.float32)).astype(x.dtype)

def modulate(h, shift, scale):
    return h * (1 + scale) + shift

def split_in(z):
    idx = np.cumsum(IN_SPLITS)[:-1].tolist()
    return jnp.split(z, idx, axis=-1)

def to_heads(t, n_heads):
    b, n, _ = t.shape
    return t.reshape(b, n, n_heads, HEAD_DIM).transpose(0, 2, 1, 3)

def from_heads(o):
    b, h, n, d = o.shape
    return o.transpose(0, 2, 1, 3).reshape(b, n, h * d)

def axial_rope(n_tokens, dtype):
    t = jnp.arange(n_tokens, dtype=jnp.int32)
    row = (t // GRID_W).astype(jnp.float32)
    col = (t % GRID_W).astype(jnp.float32)
    inv = ROPE_THETA ** (-jnp.arange(ROPE_FREQS, dtype=jnp.float32) / ROPE_FREQS)
    ang = jnp.concatenate([row[:, None] * inv, col[:, None] * inv], axis=-1)
    return jnp.cos(ang).astype(dtype), jnp.sin(ang).astype(dtype)

def apply_rope(x, cos, sin):
    x1, x2 = x[..., :HEAD_DIM // 2], x[..., HEAD_DIM // 2:]
    return jnp.concatenate([x1 * cos - x2 * sin, x1 * sin + x2 * cos], axis=-1)

def softmax_sink(s, sink):
    if sink is None:
        return jax.nn.softmax(s, axis=-1)
    m = jnp.maximum(jnp.max(s, axis=-1, keepdims=True), sink)
    e = jnp.exp(s - m)
    return e / (jnp.sum(e, axis=-1, keepdims=True) + jnp.exp(sink - m))

def context_attention(qc, kc, vc, sink):
    b, hq, n, d = qc.shape
    hkv = kc.shape[1]
    rep = hq // hkv
    qg = qc.reshape(b, hkv, rep, n, d)
    s = jnp.einsum('bgrqd,bgkd->bgrqk', qg, kc).astype(jnp.float32) * (HEAD_DIM ** -0.5)
    sink_g = None if sink is None else sink.reshape(hkv, rep)[None, :, :, None, None].astype(jnp.float32)
    p = softmax_sink(s, sink_g).astype(vc.dtype)
    return jnp.einsum('bgrqk,bgkd->bgrqd', p, vc).reshape(b, hq, n, d)

def neighbourhood_attention(q, k, v, kc, vc, rpb, rows):
    b, h, s_len, d = q.shape
    kh = min(NA_WIN_ROWS, rows)
    kw = NA_WIN_COLS
    scale = HEAD_DIM ** -0.5
    qg = q.reshape(b, h, rows, GRID_W, d)
    kg_all = k.reshape(b, h, rows, GRID_W, d)
    vg_all = v.reshape(b, h, rows, GRID_W, d)
    col = jnp.arange(GRID_W)
    col_start = jnp.clip(col - kw // 2, 0, GRID_W - kw)
    col_idx = col_start[:, None] + jnp.arange(kw)[None, :]
    dcol = col_idx - col[:, None] + (NA_WIN_COLS - 1)
    rpb = rpb.astype(jnp.float32)

    def row_block(r):
        r0 = jnp.clip(r - kh // 2, 0, rows - kh)
        qr = lax.dynamic_index_in_dim(qg, r, axis=2, keepdims=False)
        k_rows = lax.dynamic_slice_in_dim(kg_all, r0, kh, axis=2)
        v_rows = lax.dynamic_slice_in_dim(vg_all, r0, kh, axis=2)
        kgat = k_rows[:, :, :, col_idx, :]
        vgat = v_rows[:, :, :, col_idx, :]
        s_nb = jnp.einsum('bhwd,bhiwjd->bhwij', qr, kgat).astype(jnp.float32) * scale
        drow = r0 + jnp.arange(kh) - r + (NA_WIN_ROWS - 1)
        bias = rpb[:, drow[:, None, None], dcol[None, :, :]]
        s_nb = (s_nb + bias.transpose(0, 2, 1, 3)[None]).reshape(b, h, GRID_W, kh * kw)
        s_cx = jnp.einsum('bhwd,bhcd->bhwc', qr, kc).astype(jnp.float32) * scale
        p = jax.nn.softmax(jnp.concatenate([s_nb, s_cx], axis=-1), axis=-1).astype(v.dtype)
        p_nb = p[..., :kh * kw].reshape(b, h, GRID_W, kh, kw)
        p_cx = p[..., kh * kw:]
        return (jnp.einsum('bhwij,bhiwjd->bhwd', p_nb, vgat)
                + jnp.einsum('bhwc,bhcd->bhwd', p_cx, vc))

    out = lax.map(row_block, jnp.arange(rows))
    return out.transpose(1, 2, 0, 3, 4).reshape(b, h, s_len, d)

def sliding_window_gqa(q, k, v, kc, vc, sink):
    b, hq, s_len, d = q.shape
    hkv = k.shape[1]
    rep = hq // hkv
    nb = s_len // SW_BLOCK
    band = 3 * SW_BLOCK
    scale = HEAD_DIM ** -0.5
    qg = q.reshape(b, hkv, rep, s_len, d)
    pad = ((0, 0), (0, 0), (SW_BLOCK, SW_BLOCK), (0, 0))
    kp = jnp.pad(k, pad)
    vp = jnp.pad(v, pad)
    rel = (jnp.arange(band) - SW_BLOCK)[None, :] - jnp.arange(SW_BLOCK)[:, None]
    in_window = jnp.abs(rel) <= SW_WINDOW
    sink_g = sink.reshape(hkv, rep)[None, :, :, None, None].astype(jnp.float32)

    def block(n):
        q0 = n * SW_BLOCK
        qb = lax.dynamic_slice_in_dim(qg, q0, SW_BLOCK, axis=3)
        kb = lax.dynamic_slice_in_dim(kp, q0, band, axis=2)
        vb = lax.dynamic_slice_in_dim(vp, q0, band, axis=2)
        kabs = q0 - SW_BLOCK + jnp.arange(band)
        mask = in_window & ((kabs >= 0) & (kabs < s_len))[None, :]
        s_loc = jnp.einsum('bgrqd,bgkd->bgrqk', qb, kb).astype(jnp.float32) * scale
        s_loc = jnp.where(mask, s_loc, -jnp.inf)
        s_cx = jnp.einsum('bgrqd,bgcd->bgrqc', qb, kc).astype(jnp.float32) * scale
        p = softmax_sink(jnp.concatenate([s_loc, s_cx], axis=-1), sink_g).astype(v.dtype)
        return (jnp.einsum('bgrqk,bgkd->bgrqd', p[..., :band], vb)
                + jnp.einsum('bgrqc,bgcd->bgrqd', p[..., band:], vc))

    out = lax.map(block, jnp.arange(nb))
    return out.transpose(1, 2, 3, 0, 4, 5).reshape(b, hq, s_len, d)

def short_conv_mixer(xin, gate_b, gate_c, conv_w):
    u = gate_c * xin
    y = lax.conv_general_dilated(
        u, conv_w[:, None, :].astype(u.dtype), window_strides=(1,),
        padding=((CONV_K // 2, CONV_K // 2),), dimension_numbers=('NWC', 'WIO', 'NWC'),
        feature_group_count=u.shape[-1])
    return gate_b * y

def merge_branches(a_out, b_out, c_out, z_gate, b_gate_l, w_br_a_l, w_br_b_l, w_br_c_l, w_o_l):
    ga, gb, gc = jnp.split(jax.nn.sigmoid(z_gate + b_gate_l), N_BRANCHES, axis=-1)
    merged = ga * (a_out @ w_br_a_l) + gb * (b_out @ w_br_b_l) + gc * (c_out @ w_br_c_l)
    return merged @ w_o_l

def swiglu(h, w_up, w_down):
    gate, up = jnp.split(h @ w_up, 2, axis=-1)
    return (jax.nn.silu(gate) * up) @ w_down

def setup_inputs(seed: int = 0) -> dict:
    key = jax.random.key(seed)
    ks = jax.random.split(key, 20)
    f32 = jnp.float32

    def nrm(k, shape, scale):
        return jax.random.normal(k, shape, f32) * scale

    return {
        "x": nrm(ks[0], (BATCH, SEQ, D_MODEL), 1.0),
        "c": nrm(ks[1], (BATCH, D_MODEL), 1.0),
        "ctx": nrm(ks[2], (BATCH, CTX_LEN, D_MODEL), 1.0),
        "c_ctx": nrm(ks[3], (D_MODEL,), 1.0),
        "w_ada": nrm(ks[4], (DEPTH, D_MODEL, 6 * D_MODEL), 0.5 * D_MODEL ** -0.5),
        "b_ada": nrm(ks[5], (DEPTH, 6 * D_MODEL), 0.02),
        "norm1_g": 1.0 + nrm(ks[6], (DEPTH, D_MODEL), 0.02),
        "norm2_g": 1.0 + nrm(ks[7], (DEPTH, D_MODEL), 0.02),
        "w_in": nrm(ks[8], (DEPTH, D_MODEL, N_IN), D_MODEL ** -0.5),
        "b_gate": nrm(ks[9], (DEPTH, N_BRANCHES * D_MODEL), 0.02),
        "na_rpb": nrm(ks[10], (DEPTH, NA_HEADS, 2 * NA_WIN_ROWS - 1, 2 * NA_WIN_COLS - 1), 0.1),
        "sw_sink": nrm(ks[11], (DEPTH, SW_HEADS), 1.0),
        "conv_w": nrm(ks[12], (DEPTH, CONV_K, CONV_WIDTH), CONV_K ** -0.5),
        "w_br_a": nrm(ks[13], (DEPTH, NA_W, D_MODEL), NA_W ** -0.5),
        "w_br_b": nrm(ks[14], (DEPTH, SW_QW, D_MODEL), SW_QW ** -0.5),
        "w_br_c": nrm(ks[15], (DEPTH, CONV_WIDTH, D_MODEL), CONV_WIDTH ** -0.5),
        "w_o": nrm(ks[16], (DEPTH, D_MODEL, D_MODEL), D_MODEL ** -0.5),
        "w_ffn_up": nrm(ks[17], (DEPTH, D_MODEL, 2 * D_FF), D_MODEL ** -0.5),
        "w_ffn_down": nrm(ks[18], (DEPTH, D_FF, D_MODEL), D_FF ** -0.5),
        "final_norm_g": 1.0 + nrm(ks[19], (D_MODEL,), 0.02),
    }

def reference(x, c, ctx, c_ctx, w_ada, b_ada, norm1_g, norm2_g, w_in, b_gate, na_rpb, sw_sink,
              conv_w, w_br_a, w_br_b, w_br_c, w_o, w_ffn_up, w_ffn_down, final_norm_g):
    b, s_len, _ = x.shape
    rows = s_len // GRID_W
    cos, sin = axial_rope(s_len, x.dtype)
    silu_c = jax.nn.silu(c)
    silu_cc = jax.nn.silu(c_ctx)
    xc = ctx
    for l in range(DEPTH):
        last = l == DEPTH - 1
        sh1, sc1, g1, sh2, sc2, g2 = jnp.split((silu_c @ w_ada[l] + b_ada[l])[:, None, :], 6, axis=-1)
        csh1, csc1, cg1, csh2, csc2, cg2 = jnp.split(silu_cc @ w_ada[l] + b_ada[l], 6, axis=-1)

        h = modulate(rms_norm(x, norm1_g[l]), sh1, sc1)
        hc = modulate(rms_norm(xc, norm1_g[l]), csh1, csc1)
        qa, ka, va, qb, kb, vb, cx, cgb, cgc, zg = split_in(h @ w_in[l])
        qa_c, ka_c, va_c, qb_c, kb_c, vb_c, cx_c, cgb_c, cgc_c, zg_c = split_in(hc @ w_in[l])
        ka_c = to_heads(ka_c, NA_HEADS)
        va_c = to_heads(va_c, NA_HEADS)
        kb_c = to_heads(kb_c, SW_KV_HEADS)
        vb_c = to_heads(vb_c, SW_KV_HEADS)

        a_out = from_heads(neighbourhood_attention(
            to_heads(qa, NA_HEADS), to_heads(ka, NA_HEADS), to_heads(va, NA_HEADS),
            ka_c, va_c, na_rpb[l], rows))
        b_out = from_heads(sliding_window_gqa(
            apply_rope(to_heads(qb, SW_HEADS), cos, sin),
            apply_rope(to_heads(kb, SW_KV_HEADS), cos, sin),
            to_heads(vb, SW_KV_HEADS), kb_c, vb_c, sw_sink[l]))
        c_out = short_conv_mixer(cx, cgb, cgc, conv_w[l])
        x = x + g1 * merge_branches(a_out, b_out, c_out, zg, b_gate[l], w_br_a[l], w_br_b[l], w_br_c[l], w_o[l])

        if not last:
            a_c = from_heads(context_attention(to_heads(qa_c, NA_HEADS), ka_c, va_c, None))
            b_c = from_heads(context_attention(to_heads(qb_c, SW_HEADS), kb_c, vb_c, sw_sink[l]))
            c_c = short_conv_mixer(cx_c, cgb_c, cgc_c, conv_w[l])
            xc = xc + cg1 * merge_branches(a_c, b_c, c_c, zg_c, b_gate[l], w_br_a[l], w_br_b[l], w_br_c[l], w_o[l])

        h2 = modulate(rms_norm(x, norm2_g[l]), sh2, sc2)
        x = x + g2 * swiglu(h2, w_ffn_up[l], w_ffn_down[l])
        if not last:
            hc2 = modulate(rms_norm(xc, norm2_g[l]), csh2, csc2)
            xc = xc + cg2 * swiglu(hc2, w_ffn_up[l], w_ffn_down[l])

    return rms_norm(x, final_norm_g)


_drawn_inputs = setup_inputs


def setup_inputs(seed=0):
    import zlib

    import numpy as np

    out = dict(_drawn_inputs(seed))
    spreads = {}
    factors = {'norm1_g': 5.477,
     'norm2_g': 26.578,
     'b_gate': 8.0,
     'na_rpb': 64.0,
     'sw_sink': 8.0,
     'final_norm_g': 7.929}
    for name, (base, spread) in spreads.items():
        noise = np.random.default_rng([zlib.crc32(name.encode()), seed]).standard_normal(out[name].shape)
        drawn = base * np.exp(spread * noise) if base else spread * noise
        out[name] = __import__('jax').numpy.asarray(drawn.astype(out[name].dtype))
    for name, factor in factors.items():
        out[name] = (out[name] * factor).astype(out[name].dtype)
    return out
```

```python
from contextlib import ExitStack

import concourse.bass as bass
from concourse import mybir

F32 = mybir.dt.float32
F32R = mybir.dt.float32r
ALU = mybir.AluOpType
ACT = mybir.ActivationFunctionType
AX = mybir.AxisListType

P = 128
D_MODEL = 1024
KC = D_MODEL // P
SEQ = 512
CTX = 256
TALL = SEQ + CTX
DEPTH = 2
GRID_W = 64
ROWS = SEQ // GRID_W
HD = 64
NA_HEADS = 8
WIN_ROWS, WIN_COLS = 8, 16
RPB = (2 * WIN_ROWS - 1) * (2 * WIN_COLS - 1)
RPB_W = 2 * WIN_COLS - 1
SW_HEADS = 8
PAIRS = 4
BR = 512
D_FF = 2816
HALF_FF = D_FF // P // 2
EPS = 1e-6
ROPE_THETA = 10000.0
NEG = -1e30
QSCALE = HD ** -0.5
RPB_PAD = 8
SEG = (WIN_ROWS - 1) * RPB_W + 32

CT_QA, CT_KA, CT_VA, CT_QB, CT_KB, CT_VB, CT_X, CT_GB, CT_GC, CT_ZG = 0, 4, 8, 12, 16, 17, 18, 22, 26, 30
V_BADA, V_N1, V_N2, V_BGATE, V_CONV, V_FINAL, V_C, V_CC, V_END = 0, 48, 56, 64, 88, 100, 108, 116, 124
SH1, SC1, G1, SH2, SC2, G2 = range(6)

BAND0, BAND_END, CTX_END, SINK = 128, 512, 768, 768


class Stage:

    def __init__(self, name, layer, trips, slots, dmas, counts):
        self.name, self.layer, self.trips = name, layer, trips
        self.slots, self.dmas, self.counts = slots, dmas, counts
        self.per = len(slots)
        self.base = {}


PRIMED = dict(ada_rows_copied=1, ada_cols_done=1, ada_cols_added=1, sq_used=2, bias_done=1, masked=1, o_lo=1,
              gate_ready=1, mix_done=1, mixed=1, u_done=1, c_done=1, x_updated=2, silu_done=1, act_done=1,
              h_lo_done=2, c_lo=1, act_lo=1)


def attention_tiles(kind, layer):
    tiles = []
    for j in range(SEQ // P):
        if kind == "A":
            tiles.append((P * j, P * j, 2 * P, [j, (j + 1) % 4], 0 if j == 0 else (2 if j == 3 else 1)))
        else:
            lo, hi = max(0, j - 1), min(3, j + 1)
            tiles.append((P * j, P * lo, P * (hi - lo + 1), list(range(lo, hi + 1)), None))
    if layer == 0:
        for j in range(CTX // P):
            tiles.append((SEQ + P * j, 0, 0, [], None))
    return tiles


def chunk_groups(tile):
    _, _, width, band, _ = tile
    cols = [(v, BAND_END - width - BAND0 + P * n) for n, v in enumerate(band)]
    cols += [(4, BAND_END - BAND0), (5, BAND_END - BAND0 + P)]
    return [cols[n:n + 2] for n in range(0, len(cols), 2)]


def plan():
    stages = []

    def add(name, layer, trips, slots=(), dmas=(), **counts):
        stages.append(Stage(name, layer, trips, list(slots), list(dmas), counts))

    add("load", 0, 1, x_cols_done=8, x_cols_copied=8)
    for l in range(DEPTH):
        nt = len(attention_tiles("A", l))
        ga = sum(len(chunk_groups(t)) for t in attention_tiles("A", l))
        gb = sum(len(chunk_groups(t)) for t in attention_tiles("B", l))
        add("ada", l, 12, [0, 1, 0, 1], [1] * 4, ada_rows_copied=1, ada_cols_done=1,
            ada_cols_added=1)
        add("norm1", l, 4, sq_ready=2, sq_used=2, normed=2, h_hi_done=2, h_lo_done=2)
        att = dict(q_hi=1, q_lo=1, scores_done=2 * nt, max_done=2 * nt, exp_done=2 * nt,
                   masked=8, inv_done=2 * nt, p_done=2 * nt, o_done=nt, o_hi=nt, o_lo=nt)
        add("A", l, PAIRS, [0, 1, 2], [1] * 3, k_hi=1, k_lo=1, v_copied=1, vt_done=1,
            v_hi=1, v_lo=1, bias_done=1, pt_done=ga, pt_hi=ga, pt_lo=ga, **att)
        add("mergeA", l, 8, [0, 1], [1, 1], gate_ready=1, mix_done=1)
        add("Bkv", l, 1, [0, 1], [1, 1], k_hi=1, k_lo=1, v_copied=1, vt_done=1, v_hi=1,
            v_lo=1, swapped=1, rope_step=3)
        add("B", l, PAIRS, [0, 1], [2, 2], pt_done=gb, pt_hi=gb, pt_lo=gb, swapped=1, rope_step=3,
            sunk=2, **att)
        add("mergeB", l, 8, [0, 1], [1, 2], gate_ready=1, mix_done=1, mixed=1)
        add("C", l, 4, [0, 1, 2], [1] * 3, cx_copied=1, u_done=1,
            y_step=3, c_done=1, c_hi=1, c_lo=1)
        add("mergeC", l, 8, [0, 1], [1, 1], gate_ready=1, mix_done=1, mixed=1)
        add("split", l, 4, h_hi_done=2, h_lo_done=2)
        add("out", l, 4, [0, 1], [1, 1], x_updated=2)
        add("norm2", l, 4, sq_ready=2, sq_used=2, normed=2, h_hi_done=2, h_lo_done=2)
        for f in range(2):
            add(f"up{f}", l, HALF_FF, [0, 1], [1, 1], silu_done=1, act_done=1,
                act_hi=1, act_lo=1)
            add(f"down{f}", l, 4, [0, 1, 0, 1], [1] * 4, x_updated=2)
    add("final", DEPTH - 1, 1, sq_ready=8, sq_used=8)

    slots = [s for st in stages for _ in range(st.trips) for s in st.slots]
    assert all(a != b for a, b in zip(slots, slots[1:]))
    totals = dict(PRIMED)
    block = 0
    for st in stages:
        st.block = block
        block += st.trips * st.per
        st.base = dict(totals)
        for name, n in st.counts.items():
            totals[name] = totals.get(name, 0) + n * st.trips
    return {(st.name, st.layer): st for st in stages}, stages, totals


def build(nc, x, c, ctx, c_ctx, w_ada, b_ada, norm1_g, norm2_g, w_in, b_gate, rpb, sw_sink, conv_w,
          w_br_a, w_br_b, w_br_c, w_o, w_up, w_down, final_g, ident_in, masks_a, masks_b, rope_in, comb_in,
          out):
    stage_of, stages, totals = plan()
    blocks = [(st, i, k) for st in stages for i in range(st.trips) for k in range(st.per)]

    landed, per_slot = [], [0, 0, 0]
    for st, i, k in blocks:
        per_slot[st.slots[k]] += 16 * st.dmas[k]
        landed.append(per_slot[st.slots[k]])

    stack = ExitStack()
    with stack:
        def sb(where, name, shape, dt=F32):
            return where.enter_context(nc.sbuf_tensor(name, shape, dt))

        def sem(name):
            return stack.enter_context(nc.semaphore(name))

        x_t = sb(stack, "x_t", [P, KC, TALL])
        h_hi = sb(stack, "h_hi", [P, KC, TALL], F32R)
        h_lo = sb(stack, "h_lo", [P, KC, TALL], F32R)
        w_raw = sb(stack, "w_raw", [P, 3, KC * P])
        w_hi = sb(stack, "w_hi", [P, 3, KC * P], F32R)
        w_lo = sb(stack, "w_lo", [P, 3, KC * P], F32R)
        ident = sb(stack, "ident", [P, P])
        ones = sb(stack, "ones", [P, P])
        mask_a = sb(stack, "mask_a", [P, 3, 2 * P])
        mask_b = sb(stack, "mask_b", [P, 2, P])
        rope = sb(stack, "rope", [P, 2, SEQ])
        comb = sb(stack, "comb", [4, 2])
        vec_rows = sb(stack, "vec_rows", [P, DEPTH, P])
        vec = sb(stack, "vec", [P, DEPTH, P])
        sink = sb(stack, "sink", [P, DEPTH, SW_HEADS])
        ada = sb(stack, "ada", [P, 2, 48])
        a_mod = sb(stack, "a_mod", [P, 2, 2, KC])
        cond = sb(stack, "cond", [P, KC, 2])
        cond4 = sb(stack, "cond4", [P, KC, 4], F32R)
        nmax = sb(stack, "nmax", [P, 2, 2])
        rsum = sb(stack, "rsum", [P, 2, 2])
        rinv = sb(stack, "rinv", [P, 2, 2])

        with ExitStack() as r:
            tok = sb(r, "tok", [P, TALL // P, D_MODEL])
        with ExitStack() as r:
            rows = sb(r, "rows", [4, 4 * P])
            sq = sb(r, "sq", [P, 2, TALL])
            rstd = sb(r, "rstd", [P, TALL])
            normed_t = sb(r, "normed_t", [P, 2, TALL])
        with ExitStack() as r:
            br_hi = sb(r, "br_hi", [P, PAIRS, TALL], F32R)
            br_lo = sb(r, "br_lo", [P, PAIRS, TALL], F32R)
            with ExitStack() as r2:
                rpb_back = sb(r2, "rpb_back", [P, NA_HEADS, SEG])
                rpb_seg = sb(r2, "rpb_seg", [P, NA_HEADS, 256])
                bias = sb(r2, "bias", [P, 3, 2, 2 * P])
            merged = sb(r, "merged", [P, KC, TALL])
            with ExitStack() as r2:
                q_hi = sb(r2, "q_hi_t", [P, TALL], F32R)
                q_lo = sb(r2, "q_lo_t", [P, TALL], F32R)
                k_hi = sb(r2, "k_hi_t", [P, 640 + CTX], F32R)
                k_lo = sb(r2, "k_lo_t", [P, 640 + CTX], F32R)
                v_hi = sb(r2, "v_hi_t", [P, TALL], F32R)
                v_lo = sb(r2, "v_lo_t", [P, TALL], F32R)
                pt_hi = sb(r2, "pt_hi_t", [P, 2, 4 * P], F32R)
                pt_lo = sb(r2, "pt_lo_t", [P, 2, 4 * P], F32R)
                with ExitStack() as r3:
                    probs = sb(r3, "probs", [P, 2, 2, 644])
                with ExitStack() as r3:
                    swap = sb(r3, "swap", [P, SEQ])
                    rc = sb(r3, "rc", [P, SEQ])
                    rs = sb(r3, "rs", [P, SEQ])
                with ExitStack() as r3:
                    v_fm = sb(r3, "v_fm", [P, TALL])
            with ExitStack() as r2:
                gate = sb(r2, "gate", [P, TALL])
                mix = sb(r2, "mix", [P, TALL])
            with ExitStack() as r2:
                cx_sb = sb(r2, "cx_sb", [P, TALL])
                u_pad = sb(r2, "u_pad", [P, TALL + 4])
                y_a = sb(r2, "y_a", [P, TALL + 2])
                y_b = sb(r2, "y_b", [P, TALL + 2])
                c_out = sb(r2, "c_out", [P, TALL])
        with ExitStack() as r:
            a_hi = sb(r, "a_hi", [P, HALF_FF, TALL], F32R)
            a_lo = sb(r, "a_lo", [P, HALF_FF, TALL], F32R)
            silu_sb = sb(r, "silu_sb", [P, TALL])
            act_sb = sb(r, "act_sb", [P, TALL])
        with ExitStack() as r:
            r.enter_context(nc.sbuf_tensor("under_sq", [P, 5 * TALL + 600], F32))
            y_fm = sb(r, "y_fm", [P, KC, SEQ])
            y_tok = sb(r, "y_tok", [P, 2, D_MODEL])

        psum = stack.enter_context(nc.psum_tensor("psum", [P, 8 * 512], F32))

        def bank(n, width=512):
            return psum[:, 512 * n:512 * n + width]

        s = {name: sem(name) for name in totals}
        s_const = sem("const_loaded")
        s_load = [sem(f"w_loaded{n}") for n in range(3)]
        s_whi = sem("w_hi_done")
        s_wlo = sem("w_lo_done")
        s_block = sem("block_done")
        s_vecT = sem("vec_transposed")
        s_vec = sem("vec_copied")
        s_ones = sem("ones_set")
        s_zero = sem("pad_zeroed")
        s_cond = sem("cond_step")
        s_mod = sem("mod_ready")
        s_ms = sem("mean_square_step")
        s_rstd = sem("rstd_ready")
        s_yfm = sem("y_ready")
        s_yT = sem("y_transposed")
        s_ytok = sem("y_copied")
        s_out = [sem(f"out_stored{n}") for n in range(2)]
        s_rpb = sem("rpb_loaded")
        s_rpbf = sem("rpb_forward")
        s_sum = sem("mix_summed")

        CONSTS = 3 + DEPTH * 9 + 4

        WI = w_in.rearrange("l (kc p) (ct f) -> l ct p kc f", p=P, f=P)
        WI64 = w_in.rearrange("l (kc p) (ct f) -> l ct p kc f", p=P, f=HD)
        WADA = w_ada.rearrange("l (kc p) (g f) -> l g p kc f", p=P, f=4 * P)
        WBR = {"A": w_br_a.rearrange("l (kc p) (d f) -> l d p kc f", p=P, f=P),
               "B": w_br_b.rearrange("l (e kc p) (d f) -> l d e p kc f", e=2, p=HD, f=P),
               "C": w_br_c.rearrange("l (kc p) (d f) -> l d p kc f", p=P, f=P)}
        WO = w_o.rearrange("l (kc p) (d f) -> l d p kc f", p=P, f=P)
        WUP = w_up.rearrange("l (kc p) (ct f) -> l ct p kc f", p=P, f=P)
        WDN = w_down.rearrange("l (kc p) (d f) -> l d p kc f", p=P, f=P)

        def block_source(st, i, k):
            l, name = st.layer, st.name
            slot = w_raw[:, st.slots[k], :]

            def cols(kc):
                return slot[:, 0:kc * P].rearrange("p (kc f) -> p kc f", f=P)

            if name == "ada":
                return [(slot.rearrange("p (kc f) -> p kc f", f=4 * P), WADA[l, i, :, 2 * k:2 * k + 2])]
            if name == "A":
                return [(cols(KC), WI[l, i + (CT_QA, CT_KA, CT_VA)[k]])]
            if name == "Bkv":
                return [(cols(KC), WI[l, (CT_KB, CT_VB)[k]])]
            if name == "B":
                d = cols(KC // 2)
                return [(d[:, :, HD * e:HD * e + HD], WI64[l, i + 2 * CT_QB + 4 * e, :, 4 * k:4 * k + 4])
                        for e in range(2)]
            if name == "C":
                return [(cols(KC), WI[l, i + (CT_X, CT_GC, CT_GB)[k]])]
            if name.startswith("merge"):
                kind = name[5]
                if k == 0:
                    return [(cols(KC), WI[l, i + CT_ZG + 8 * "ABC".index(kind)])]
                if kind == "B":
                    return [(cols(4)[HD * e:HD * e + HD], WBR["B"][l, i, e]) for e in range(2)]
                return [(cols(4), WBR[kind][l, i])]
            if name == "out":
                return [(cols(KC), WO[l, i * 2 + k])]
            if name.startswith("up"):
                f = int(name[2])
                return [(cols(KC), WUP[l, i + HALF_FF * f + 2 * HALF_FF * k])]
            f = int(name[4])
            first = HALF_FF * f + (0, KC)[k % 2]
            n = (KC, HALF_FF - KC)[k % 2]
            return [(cols(n), WDN[l, i * 2 + k // 2, :, first:first + n])]

        def block_width(st, k):
            if st.name == "B" or (st.name.startswith("merge") and k == 1):
                return 4 * P
            if st.name.startswith("down") and k % 2:
                return (HALF_FF - KC) * P
            return KC * P

        def block_at(st, i, k):
            if isinstance(i, int):
                b = st.block + i * st.per + k
                if b >= len(blocks):
                    return None
                return (*blocks[b], b)
            assert k < 2 * st.per
            return (st, i + k // st.per, k % st.per, i * st.per + (st.block + k))

        def load_value(st, i, k):
            first = landed[st.block + k]
            if isinstance(i, int):
                return landed[st.block + i * st.per + k]
            if st.trips == 1:
                return first
            return i * (landed[st.block + st.per + k] - first) + first

        def passes(eng, st, body):
            if st.trips > 1:
                with eng.Fori(0, st.trips - 1) as i:
                    body(i)
            body(st.trips - 1)

        def at(st, name, i, k):
            return i * st.counts[name] + (st.base.get(name, 0) + k)

        def wait(eng, st, name, i, k=None):
            v = at(st, name, i, st.counts[name] if k is None else k)
            if not (isinstance(v, int) and v <= 0):
                eng.wait_ge(s[name], v)

        def wait_block(eng, st, i, k):
            eng.wait_ge(s_block, block_at(st, i, k)[3] + 1)

        def prime(eng, *names):
            for name in names:
                eng.sem_inc(s[name], PRIMED[name])

        def wait_total(eng, st, name):
            v = st.base.get(name, 0)
            if v > 0:
                eng.wait_ge(s[name], v)

        def segs(width):
            return [(0, 0, SEQ)] + ([(1, SEQ, TALL)] if width == TALL else [])

        def width_of(l):
            return TALL if l == 0 else SEQ

        def perm(ap):
            return ap.rearrange("p (r c) -> p c r", c=GRID_W)

        def grid(ap):
            return ap.rearrange("p (c r) -> p c r", r=ROWS)

        def chunk(t, i, k, n=2):
            if isinstance(i, int):
                return t[:, n * i + k, :]
            return t[:, :, :].rearrange("p (c k) t -> p c k t", k=n)[:, i, k, :]

        def x_chunk(i, k, n):
            return chunk(x_t, i, k, n)

        def tile_of(t, i):
            return t[:, i, :]

        pair = tile_of

        def ada_col(e, piece, i, k):
            return ada[:, e, KC * piece:KC * piece + KC].rearrange("p (c k) -> p c k", k=2)[:, i, k:k + 1]

        def mod_col(which, e, i, k):
            return a_mod[:, which, e, :].rearrange("p (c k) -> p c k", k=2)[:, i, k:k + 1]

        def vec_col(l, first, i):
            if isinstance(i, int):
                return vec[:, l, first + i:first + i + 1]
            return vec[:, l, first:P].rearrange("p (a b) -> p a b", b=1)[:, i, :]

        def sink_col(l, e, i):
            return sink[:, l, 4 * e:4 * e + 4].rearrange("p (a b) -> p a b", b=1)[:, i, :]

        def rpb_runs(i, e):
            seg = rpb_seg[:, :, :].rearrange("p (i e) w -> p i e w", e=2)[:, i, e, :]
            return bass.AP(seg.tensor, seg.offset, [list(seg.ap[0]), [1, 32], [RPB_W, ROWS]])

        def q_pieces_a(dst, width):
            out_ = [(grid(dst[:, 0:SEQ]), perm(bank(0)))]
            return out_ + ([(dst[:, SEQ:TALL], bank(1, CTX))] if width == TALL else [])

        def k_pieces_a(dst):
            src = perm(bank(2))
            return [(grid(dst[:, 64:64 + SEQ]), src), (grid(dst[:, 0:64]), src[:, 56:64, :]),
                    (grid(dst[:, 576:640]), src[:, 0:8, :]), (dst[:, 640:640 + CTX], bank(3, CTX))]

        def v_pieces(kind):
            if kind == "B":
                return [(v_fm[:, :], psum[:, 2048:2048 + TALL])]
            src = perm(bank(4))
            return [(grid(v_fm[:, 64:SEQ]), src[:, 0:56, :]), (grid(v_fm[:, 0:64]), src[:, 56:64, :]),
                    (v_fm[:, SEQ:TALL], bank(5, CTX))]

        def out_pieces(dst, kind, i, n, q0):
            pieces = []
            for e in range(2):
                part = slice(HD * e, HD * e + HD)
                src = bank((7, 1)[n % 2])[part, P * e:P * e + P]
                d = dst[part, i, :]
                if kind == "A" and q0 < SEQ:
                    c0 = q0 // ROWS
                    pieces.append((perm(d[:, 0:SEQ])[:, c0:c0 + P // ROWS, :], grid(src)))
                else:
                    pieces.append((d[:, q0:q0 + P], src))
            return pieces

        block = stack.enter_context(nc.Block())

        @block.sync
        def _(sp):
            def const(dst, src):
                sp.dma_start(dst, src).then_inc(s_const, 16)

            const(tok[:, 0:4, :], x.rearrange("b (t p) d -> p (b t) d", p=P))
            const(tok[:, 4:6, :], ctx.rearrange("b (t p) d -> p (b t) d", p=P))
            const(ident[:], ident_in)
            for l in range(DEPTH):
                def vrow(first, src):
                    n = src.shape[0]
                    const(vec_rows[first:first + n, l, :], src)
                vrow(V_BADA, b_ada[l].rearrange("(a b) -> a b", b=P))
                vrow(V_N1, norm1_g[l].rearrange("(a b) -> a b", b=P))
                vrow(V_N2, norm2_g[l].rearrange("(a b) -> a b", b=P))
                vrow(V_BGATE, b_gate[l].rearrange("(a b) -> a b", b=P))
                vrow(V_CONV, conv_w[l].rearrange("k (a b) -> (k a) b", b=P))
                vrow(V_FINAL, final_g.rearrange("(a b) -> a b", b=P))
                vrow(V_C, c.rearrange("o (a b) -> (o a) b", b=P))
                vrow(V_CC, c_ctx.rearrange("(a b) -> a b", b=P))
                const(sink[:, l, :], bass.AP(sw_sink.tensor, l * SW_HEADS, [[0, P], [1, SW_HEADS]]))
            const(mask_a[:], masks_a)
            const(mask_b[:], masks_b)
            const(rope[:], rope_in)
            const(comb[:], comb_in)

            def load(blk):
                if blk is None:
                    return
                st, i, k, b = blk
                if not (isinstance(b, int) and b < 2):
                    sp.wait_ge(s_whi, b - 1)
                    sp.wait_ge(s_wlo, b - 1)
                for dst, src in block_source(st, i, k):
                    sp.dma_start(dst, src).then_inc(s_load[st.slots[k]], 16)

            first = stage_of["ada", 0]
            load(block_at(first, 0, 0))
            load(block_at(first, 0, 1))
            for st in stages:
                if st.name == "A":
                    wait_total(sp, st, "masked")
                    wait(sp, stage_of["norm1", st.layer], "h_lo_done", 3)
                    for h in range(NA_HEADS):
                        off = RPB_PAD + (st.layer * NA_HEADS + h) * RPB - 8
                        src = bass.AP(rpb.tensor, off, [[1, P // ROWS], [RPB_W, ROWS], [1, SEG]])
                        sp.dma_start(rpb_back[:, h, :], src).then_inc(s_rpb, 16)

                def body(i, st=st):
                    for k in range(st.per):
                        load(block_at(st, i, k + 2))
                if st.per:
                    passes(sp, st, body)

            for t in range(SEQ // P):
                sp.wait_ge(s_ytok, t + 1)
                sp.dma_start(out[0, t * P:(t + 1) * P, :], y_tok[:, t % 2, :]).then_inc(s_out[t % 2], 16)
            for n in range(2):
                sp.wait_ge(s_out[n], 16 * (SEQ // P // 2))

        @block.gpsimd
        def _(pool):
            prime(pool, "bias_done")
            pool.memset(ones[:], 1.0).then_inc(s_ones, 1)

            def split_lo(blk):
                if blk is None:
                    return
                st, i, k, b = blk
                slot, w = st.slots[k], block_width(st, k)
                pool.wait_ge(s_whi, b + 1)
                pool.tensor_tensor(w_lo[:, slot, 0:w], w_raw[:, slot, 0:w], w_hi[:, slot, 0:w].bitcast(F32),
                                   ALU.subtract).then_inc(s_wlo, 1)

            first = stage_of["ada", 0]
            split_lo(block_at(first, 0, 0))
            split_lo(block_at(first, 0, 1))
            for st in stages:
                def body(i, st=st):
                    if st.name == "A":
                        wait(pool, st, "masked", i, 0)
                        for v in range(3):
                            for e in range(2):
                                run = rpb_runs(i, e)
                                ins = pool.tensor_tensor(
                                    bias[:, v, e, :].rearrange("p (b r) -> p b r", r=8), run,
                                    mask_a[:, v, :].rearrange("p (b r) -> p b r", r=8), ALU.add)
                        ins.then_inc(s["bias_done"], 1)
                    for k in range(st.per):
                        split_lo(block_at(st, i, k + 2))
                if st.name == "A":
                    pool.wait_ge(s_const, 16 * CONSTS)
                    pool.wait_ge(s_rpb, 16 * NA_HEADS * (st.layer + 1))
                    wait(pool, stage_of["norm1", st.layer], "h_lo_done", 3)
                    back = rpb_back[:, :, :]
                    pool.tensor_copy(rpb_seg[:, :, 0:SEG],
                                     bass.AP(back.tensor, back.offset + SEG - 1,
                                             [list(back.ap[0]), [SEG, NA_HEADS], [-1, SEG]])).then_inc(s_rpbf, 1)
                    pool.wait_ge(s_rpbf, st.layer + 1)
                if st.per:
                    passes(pool, st, body)

        @block.tensor
        def _(pe):
            def project(st, i, k, dst, rhs_hi, rhs_lo, nk, width, first=True, last=True, kc0=0):
                _, _, _, b = block_at(st, i, k)
                pe.wait_ge(s_whi, b + 1)
                pe.wait_ge(s_wlo, b + 1)
                slot = st.slots[k]
                for kc in range(nk):
                    cols = slice(kc * P, kc * P + P)
                    for n, (w, r) in enumerate(((w_hi, rhs_hi), (w_hi, rhs_lo), (w_lo, rhs_hi))):
                        for _, t0, t1 in segs(width):
                            ins = pe.matmul(psum[:, dst * 512 + t0:dst * 512 + t1], w[:, slot, cols],
                                            r[:, kc0 + kc, t0:t1], start=first and kc == 0 and n == 0,
                                            stop=last and kc == nk - 1 and n == 2)
                ins.then_inc(s_block, 1)

            prime(pe, "ada_cols_done", "sq_used")
            pe.wait_ge(s_const, 16 * CONSTS)
            ld = stage_of["load", 0]
            for l in range(DEPTH):
                pe.transpose(bank(4 + l, P)[:, 0:V_END], vec_rows[0:V_END, l, :],
                             ident[0:V_END, 0:V_END]).then_inc(s_vecT, 1)
            for ch in range(KC):
                if ch >= 2:
                    wait(pe, ld, "x_cols_copied", 0, ch - 1)
                for t in range(TALL // P):
                    ins = pe.transpose(psum[:, 1024 * (ch % 2) + t * P:1024 * (ch % 2) + (t + 1) * P],
                                       tok[:, t, ch * P:(ch + 1) * P], ident[:])
                ins.then_inc(s["x_cols_done"], 1)
            wait(pe, ld, "x_cols_copied", 0)
            pe.wait_ge(s_vec, DEPTH)

            def stage_ada(st):
                pe.wait_ge(s_cond, 4)
                if st.layer:
                    wait_total(pe, st, "x_updated")

                def body(i):
                    wait(pe, st, "ada_rows_copied", i, 0)
                    for k in range(4):
                        _, _, _, b = block_at(st, i, k)
                        pe.wait_ge(s_whi, b + 1)
                        pe.wait_ge(s_wlo, b + 1)
                        for kk in range(2):
                            for w in (w_hi, w_lo):
                                ins = pe.matmul(bank(0)[0:4, :], cond4[:, 2 * k + kk, :],
                                                w[:, st.slots[k], kk * 512:kk * 512 + 512],
                                                start=(k == 0 and kk == 0 and w is w_hi),
                                                stop=(k == 3 and kk == 1 and w is w_lo))
                        ins.then_inc(s_block, 1)
                    wait(pe, st, "ada_rows_copied", i)
                    wait(pe, st, "ada_cols_added", i, 0)
                    for j in range(4):
                        ins = pe.matmul(bank(2)[:, 2 * j:2 * j + 2], rows[:, P * j:P * j + P], comb[:, :],
                                        start=True, stop=True)
                    ins.then_inc(s["ada_cols_done"], 1)
                passes(pe, st, body)

            def stage_norm(st, width):
                n = st.trips * st.counts["sq_ready"]
                for ch in range(n):
                    pe.wait_ge(s["sq_ready"], st.base.get("sq_ready", 0) + ch + 1)
                    for _, t0, t1 in segs(width):
                        ins = pe.matmul(psum[:, t0:t1], ones[:], sq[:, ch % 2, t0:t1], start=ch == 0,
                                        stop=ch == n - 1)
                    ins.then_inc(s["sq_used"], 1)

            def stage_v(st, i):
                wait(pe, st, "v_copied", i)
                for t in range(6):
                    ins = pe.transpose(psum[:, 6 * 512 + t * P:6 * 512 + (t + 1) * P], v_fm[:, t * P:(t + 1) * P],
                                       ident[:])
                ins.then_inc(s["vt_done"], 1)

            def attention(st, kind, i):
                tiles = attention_tiles(kind, st.layer)

                def scores(n):
                    q0, k0, width, _, _ = tiles[n]
                    for e in range(2):
                        base = 1024 * (1 + e)
                        rows_ = slice(HD * e, HD * e + HD)
                        if n > 0:
                            wait(pe, st, "exp_done", i, 2 * (n - 1) + e + 1)
                        for m, (q, kk) in enumerate(((q_hi, k_hi), (q_hi, k_lo), (q_lo, k_hi))):
                            if width:
                                pe.matmul(psum[:, base + BAND_END - width:base + BAND_END],
                                          q[rows_, q0:q0 + P], kk[rows_, k0:k0 + width],
                                          start=m == 0, stop=m == 2)
                            ins = pe.matmul(psum[:, base + BAND_END:base + CTX_END], q[rows_, q0:q0 + P],
                                            kk[rows_, 640:640 + CTX], start=m == 0, stop=m == 2)
                        ins.then_inc(s["scores_done"], 1)

                wait(pe, st, "q_lo", i)
                scores(0)
                g0 = 0
                for n, tile in enumerate(tiles):
                    if n + 1 < len(tiles):
                        scores(n + 1)
                    groups = chunk_groups(tile)
                    wait(pe, st, "p_done", i, 2 * n + 2)

                    def turn(g):
                        gg = g0 + g
                        if gg >= 2:
                            wait(pe, st, "pt_lo", i, gg - 1)
                        for m, (_, col) in enumerate(groups[g]):
                            for e in range(2):
                                ins = pe.transpose(bank((6, 0)[gg % 2])[:, (2 * m + e) * P:(2 * m + e + 1) * P],
                                                   probs[:, n % 2, e, col:col + P], ident[:])
                        ins.then_inc(s["pt_done"], 1)

                    def values(g):
                        gg = g0 + g
                        wait(pe, st, "pt_lo", i, gg + 1)
                        if g == 0 and n >= 2:
                            wait(pe, st, "o_lo", i, n - 1)
                        for m, (v, _) in enumerate(groups[g]):
                            cols = slice(2 * m * P, 2 * m * P + 2 * P)
                            for w, (vv, pp) in enumerate(((v_hi, pt_hi), (v_hi, pt_lo), (v_lo, pt_hi))):
                                ins = pe.matmul(bank((7, 1)[n % 2], 2 * P), vv[:, v * P:(v + 1) * P],
                                                pp[:, gg % 2, cols],
                                                start=g == 0 and m == 0 and w == 0,
                                                stop=g == len(groups) - 1 and m == len(groups[g]) - 1 and w == 2)
                        if g == len(groups) - 1:
                            ins.then_inc(s["o_done"], 1)

                    turn(0)
                    for g in range(len(groups)):
                        if g + 1 < len(groups):
                            turn(g + 1)
                        values(g)
                    g0 += len(groups)

            def stage_a(st):
                width = width_of(st.layer)
                wait(pe, stage_of["norm1", st.layer], "h_lo_done", 3)

                def body(i):
                    wait(pe, st, "o_lo", i, 0)
                    for k, w in enumerate((width, TALL, TALL)):
                        project(st, i, k, 2 * k, h_hi, h_lo, KC, w)
                    stage_v(st, i)
                    wait(pe, st, "k_lo", i)
                    wait(pe, st, "v_lo", i)
                    attention(st, "A", i)
                passes(pe, st, body)

            def stage_bkv(st):
                wait(pe, stage_of["mergeA", st.layer], "mix_done", 7)
                project(st, 0, 0, 2, h_hi, h_lo, KC, TALL)
                project(st, 0, 1, 4, h_hi, h_lo, KC, TALL)
                stage_v(st, 0)
                wait(pe, st, "k_lo", 0)
                wait(pe, st, "v_lo", 0)

            def stage_b(st):
                width = width_of(st.layer)

                def body(i):
                    wait(pe, st, "o_lo", i, 0)
                    project(st, i, 0, 0, h_hi, h_lo, 4, width, last=False)
                    project(st, i, 1, 0, h_hi, h_lo, 4, width, first=False, kc0=4)
                    attention(st, "B", i)
                passes(pe, st, body)

            def stage_merge(st):
                width = width_of(st.layer)
                kind = st.name[5]
                prev = stage_of["C" if kind == "C" else kind, st.layer]
                name = "c_lo" if kind == "C" else "o_lo"
                if kind == "C":
                    wait(pe, prev, "c_lo", 3)
                else:
                    wait(pe, prev, "o_lo", 3)

                def body(i):
                    wait(pe, st, "gate_ready", i, 0)
                    project(st, i, 0, 0, h_hi, h_lo, KC, width)
                    wait(pe, st, "mix_done", i, 0)
                    project(st, i, 1, 2, br_hi, br_lo, 4, width)
                passes(pe, st, body)

            def stage_c(st):
                width = width_of(st.layer)
                wait(pe, stage_of["mergeB", st.layer], "mix_done", 7)

                def body(i):
                    wait(pe, st, "c_done", i, 0)
                    for k in range(3):
                        project(st, i, k, 2 * k, h_hi, h_lo, KC, width)
                passes(pe, st, body)

            def stage_out(st):
                width = width_of(st.layer)
                wait(pe, stage_of["split", st.layer], "h_lo_done", 3)
                wait(pe, stage_of["mergeC", st.layer], "mix_done", 7)

                def body(i):
                    for k in range(2):
                        wait(pe, st, "x_updated", i, k - 1)
                        project(st, i, k, 2 * k, h_hi, h_lo, KC, width)
                passes(pe, st, body)

            def stage_up(st):
                width = width_of(st.layer)
                if st.name == "up0":
                    wait(pe, stage_of["norm2", st.layer], "h_lo_done", 3)
                else:
                    wait(pe, stage_of["down0", st.layer], "x_updated", 3)

                def body(i):
                    wait(pe, st, "silu_done", i, 0)
                    project(st, i, 0, 0, h_hi, h_lo, KC, width)
                    wait(pe, st, "act_done", i, 0)
                    project(st, i, 1, 2, h_hi, h_lo, KC, width)
                passes(pe, st, body)

            def stage_down(st):
                width = width_of(st.layer)
                up = stage_of[f"up{st.name[4]}", st.layer]
                wait(pe, up, "act_lo", up.trips - 1)

                def body(i):
                    for d in range(2):
                        wait(pe, st, "x_updated", i, d - 1)
                        project(st, i, 2 * d, 2 * d, a_hi, a_lo, KC, width, last=False)
                        project(st, i, 2 * d + 1, 2 * d, a_hi, a_lo, HALF_FF - KC, width, first=False,
                                kc0=KC)
                passes(pe, st, body)

            pe.wait_ge(s_ones, 1)
            for l in range(DEPTH):
                stage_ada(stage_of["ada", l])
                stage_norm(stage_of["norm1", l], TALL)
                stage_a(stage_of["A", l])
                stage_merge(stage_of["mergeA", l])
                stage_bkv(stage_of["Bkv", l])
                stage_b(stage_of["B", l])
                stage_merge(stage_of["mergeB", l])
                stage_c(stage_of["C", l])
                stage_merge(stage_of["mergeC", l])
                stage_out(stage_of["out", l])
                stage_norm(stage_of["norm2", l], width_of(l))
                for f in range(2):
                    stage_up(stage_of[f"up{f}", l])
                    stage_down(stage_of[f"down{f}", l])
            stage_norm(stage_of["final", DEPTH - 1], SEQ)
            for t in range(SEQ // P):
                pe.wait_ge(s_yfm, KC)
                if t >= 2:
                    pe.wait_ge(s_ytok, t - 1)
                for ch in range(KC):
                    ins = pe.transpose(psum[:, 1024 * (1 + t % 2) + ch * P:1024 * (1 + t % 2) + (ch + 1) * P],
                                       y_fm[:, ch, t * P:(t + 1) * P], ident[:])
                ins.then_inc(s_yT, 1)

        @block.scalar
        def _(act):
            prime(act, "ada_rows_copied", "gate_ready", "silu_done")

            def split_hi(blk):
                if blk is None:
                    return
                st, i, k, b = blk
                slot, w = st.slots[k], block_width(st, k)
                act.wait_ge(s_load[slot], load_value(st, i, k))
                if not (isinstance(b, int) and b < 2):
                    act.wait_ge(s_block, b - 1)
                act.activation(w_hi[:, slot, 0:w], w_raw[:, slot, 0:w], ACT.Identity).then_inc(s_whi, 1)

            def copy(dst, src, scale=1.0):
                return act.activation(dst, src, ACT.Identity, scale=scale)

            first = stage_of["ada", 0]
            split_hi(block_at(first, 0, 0))
            split_hi(block_at(first, 0, 1))

            act.wait_ge(s_vec, DEPTH)
            act.activation(cond[:, :, 0], vec[:, 0, V_C:V_C + KC], ACT.Silu).then_inc(s_cond, 1)
            act.activation(cond[:, :, 1], vec[:, 0, V_CC:V_CC + KC], ACT.Silu).then_inc(s_cond, 1)
            act.wait_ge(s_cond, 2)
            copy(cond4[:, :, 0:4:2], cond[:]).then_inc(s_cond, 1)

            def stage_ada(st):
                def body(i):
                    for k in range(3):
                        split_hi(block_at(st, i, k + 2))
                    wait_block(act, st, i, 3)
                    wait(act, st, "ada_cols_done", i, 0)
                    copy(rows[:, :], bank(0)[0:4, :]).then_inc(s["ada_rows_copied"], 1)
                    split_hi(block_at(st, i, 5))
                passes(act, st, body)

            def squares(st, width):
                def body(i):
                    n = st.counts["sq_ready"]
                    for k in range(n):
                        wait(act, st, "sq_used", i, k - 1)
                        ch = x_chunk(i, k, n)
                        act.activation(sq[:, k % 2, 0:width], ch[:, 0:width], ACT.Square)\
                           .then_inc(s["sq_ready"], 1)
                passes(act, st, body)

            def stage_norm(st, width, number, shift):
                squares(st, width)
                act.wait_ge(s_ms, 2 * number)
                act.activation(rstd[:, 0:width], rstd[:, 0:width], ACT.Sqrt).then_inc(s_rstd, 1)

                def body(i):
                    for k in range(2):
                        wait(act, st, "normed", i, k + 1)
                        for e, t0, t1 in segs(width):
                            ins = act.activation(chunk(h_hi, i, k)[:, t0:t1], normed_t[:, k, t0:t1], ACT.Identity,
                                                 bias=ada_col(e, shift, i, k))
                        ins.then_inc(s["h_hi_done"], 1)
                passes(act, st, body)

            def qk_hi(pieces, name, scale):
                for dst, src in pieces:
                    ins = copy(dst, src, scale)
                ins.then_inc(s[name], 1)

            def stage_vt(st, i):
                wait(act, st, "vt_done", i)
                copy(v_hi[:], psum[:, 6 * 512:6 * 512 + TALL]).then_inc(s["v_hi"], 1)

            def attention(st, kind, i):
                tiles = attention_tiles(kind, st.layer)

                def exps(n, e):
                    if n >= len(tiles):
                        return
                    wait(act, st, "max_done", i, 2 * n + e + 1)
                    c0, c1 = BAND_END - tiles[n][2], SINK + (kind == "B")
                    act.activation(probs[:, n % 2, e, c0 - BAND0:c1 - BAND0],
                                   psum[:, 1024 * (1 + e) + c0:1024 * (1 + e) + c1], ACT.Exp,
                                   bias=nmax[:, n % 2, e:e + 1],
                                   accum_out=rsum[:, n % 2, e:e + 1]).then_inc(s["exp_done"], 1)

                exps(0, 0)
                exps(0, 1)
                g0 = 0
                for n, tile in enumerate(tiles):
                    groups = chunk_groups(tile)

                    def turned(g):
                        wait(act, st, "pt_done", i, g0 + g + 1)
                        w = 2 * P * len(groups[g])
                        copy(pt_hi[:, (g0 + g) % 2, 0:w], bank((6, 0)[(g0 + g) % 2], w)).then_inc(s["pt_hi"], 1)

                    turned(0)
                    exps(n + 1, 0)
                    if len(groups) > 1:
                        turned(1)
                    exps(n + 1, 1)
                    if len(groups) > 2:
                        turned(2)
                    g0 += len(groups)
                    wait(act, st, "o_done", i, n + 1)
                    for dst, src in out_pieces(br_hi, kind, i, n, tile[0]):
                        ins = copy(dst, src)
                    ins.then_inc(s["o_hi"], 1)

            def stage_a(st):
                width = width_of(st.layer)
                wait(act, stage_of["norm1", st.layer], "h_lo_done", 3)

                def body(i):
                    split_hi(block_at(st, i, 2))
                    wait_block(act, st, i, 0)
                    qk_hi(q_pieces_a(q_hi, width), "q_hi", QSCALE)
                    split_hi(block_at(st, i, 3))
                    wait_block(act, st, i, 1)
                    qk_hi(k_pieces_a(k_hi), "k_hi", 1.0)
                    wait_block(act, st, i, 2)
                    for dst, src in v_pieces("A"):
                        ins = copy(dst, src)
                    ins.then_inc(s["v_copied"], 1)
                    split_hi(block_at(st, i, 4))
                    stage_vt(st, i)
                    attention(st, "A", i)
                passes(act, st, body)

            def swap_halves(st, i, src):
                for e in range(2):
                    for half in range(2):
                        to, frm = HD * e + 32 * half, HD * e + 32 * (1 - half)
                        ins = copy(swap[to:to + 32, :], src[frm:frm + 32, 0:SEQ])
                ins.then_inc(s["swapped"], 1)

            def stage_bkv(st):
                wait(act, stage_of["mergeA", st.layer], "mix_done", 7)
                split_hi(block_at(st, 0, 2))
                wait_block(act, st, 0, 0)
                swap_halves(st, 0, bank(2))
                wait(act, st, "rope_step", 0)
                qk_hi([(k_hi[:, 0:SEQ], rc[:]), (k_hi[:, 640:640 + CTX], bank(3, CTX))], "k_hi", 1.0)
                wait_block(act, st, 0, 1)
                wait(act, st, "k_lo", 0)
                for dst, src in v_pieces("B"):
                    ins = copy(dst, src)
                ins.then_inc(s["v_copied"], 1)
                split_hi(block_at(st, 0, 3))
                stage_vt(st, 0)

            def stage_b(st):
                width = width_of(st.layer)

                def body(i):
                    split_hi(block_at(st, i, 2))
                    wait_block(act, st, i, 1)
                    swap_halves(st, i, bank(0))
                    wait(act, st, "rope_step", i)
                    qk_hi([(q_hi[:, 0:SEQ], rc[:])] + ([(q_hi[:, SEQ:TALL], bank(1, CTX))] if width == TALL else []),
                          "q_hi", QSCALE)
                    split_hi(block_at(st, i, 3))
                    attention(st, "B", i)
                passes(act, st, body)

            def stage_merge(st):
                width = width_of(st.layer)
                number = "ABC".index(st.name[5])

                def body(i):
                    split_hi(block_at(st, i, 2))
                    wait_block(act, st, i, 0)
                    wait(act, st, "mix_done", i, 0)
                    act.activation(gate[:, 0:width], psum[:, 0:width], ACT.Sigmoid,
                                   bias=vec_col(st.layer, V_BGATE + KC * number, i)).then_inc(s["gate_ready"], 1)
                    split_hi(block_at(st, i, 3))
                passes(act, st, body)

            def stage_c(st):
                width = width_of(st.layer)
                wait(act, stage_of["mergeB", st.layer], "mixed", 7)

                def body(i):
                    split_hi(block_at(st, i, 2))
                    wait_block(act, st, i, 0)
                    wait(act, st, "u_done", i, 0)
                    copy(cx_sb[:, 0:width], psum[:, 0:width]).then_inc(s["cx_copied"], 1)
                    split_hi(block_at(st, i, 3))
                    split_hi(block_at(st, i, 4))
                    wait(act, st, "c_done", i)
                    copy(pair(br_hi, i)[:, 0:width], c_out[:, 0:width]).then_inc(s["c_hi"], 1)
                passes(act, st, body)

            def stage_split(st):
                width = width_of(st.layer)
                wait(act, stage_of["mergeC", st.layer], "mixed", 7)

                def body(i):
                    for k in range(2):
                        copy(chunk(h_hi, i, k)[:, 0:width], chunk(merged, i, k)[:, 0:width])\
                            .then_inc(s["h_hi_done"], 1)
                passes(act, st, body)

            def stage_plain(st):
                def body(i):
                    for k in range(st.per):
                        split_hi(block_at(st, i, k + 2))
                passes(act, st, body)

            def stage_up(st):
                width = width_of(st.layer)

                def body(i):
                    split_hi(block_at(st, i, 2))
                    wait_block(act, st, i, 0)
                    wait(act, st, "act_done", i, 0)
                    act.activation(silu_sb[:, 0:width], psum[:, 0:width], ACT.Silu).then_inc(s["silu_done"], 1)
                    split_hi(block_at(st, i, 3))
                    wait(act, st, "act_done", i)
                    copy(tile_of(a_hi, i)[:, 0:width], act_sb[:, 0:width]).then_inc(s["act_hi"], 1)
                passes(act, st, body)

            for l in range(DEPTH):
                stage_ada(stage_of["ada", l])
                if l == 0:
                    wait_total(act, stage_of["ada", 0], "x_cols_copied")
                else:
                    wait_total(act, stage_of["ada", l], "x_updated")
                stage_norm(stage_of["norm1", l], TALL, 2 * l + 1, SH1)
                stage_a(stage_of["A", l])
                stage_merge(stage_of["mergeA", l])
                stage_bkv(stage_of["Bkv", l])
                stage_b(stage_of["B", l])
                stage_merge(stage_of["mergeB", l])
                stage_c(stage_of["C", l])
                stage_merge(stage_of["mergeC", l])
                stage_split(stage_of["split", l])
                stage_plain(stage_of["out", l])
                wait_total(act, stage_of["norm2", l], "x_updated")
                stage_norm(stage_of["norm2", l], width_of(l), 2 * l + 2, SH2)
                for f in range(2):
                    stage_up(stage_of[f"up{f}", l])
                    stage_plain(stage_of[f"down{f}", l])
            last = stage_of["final", DEPTH - 1]
            wait_total(act, last, "x_updated")
            squares(last, SEQ)
            act.wait_ge(s_ms, 2 * (2 * DEPTH + 1))
            act.activation(rstd[:, 0:SEQ], rstd[:, 0:SEQ], ACT.Sqrt).then_inc(s_rstd, 1)
            for t in range(SEQ // P):
                act.wait_ge(s_yT, t + 1)
                if t >= 2:
                    act.wait_ge(s_out[t % 2], 16 * (t // 2))
                copy(y_tok[:, t % 2, :], psum[:, 1024 * (1 + t % 2):1024 * (2 + t % 2)]).then_inc(s_ytok, 1)

        @block.vector
        def _(dve):
            prime(dve, "ada_cols_added", "masked", "o_lo", "mix_done", "mixed", "u_done", "c_done", "x_updated",
                  "act_done", "h_lo_done", "c_lo", "act_lo")

            def rest(dst, src, hi, scale=1.0):
                return dve.scalar_tensor_tensor(dst, src, scale, hi.bitcast(F32), ALU.mult, ALU.subtract)

            for l in range(DEPTH):
                dve.wait_ge(s_vecT, l + 1)
                dve.tensor_copy(vec[:, l, 0:V_END], bank(4 + l, V_END)).then_inc(s_vec, 1)
            ld = stage_of["load", 0]
            for ch in range(KC):
                wait(dve, ld, "x_cols_done", 0, ch + 1)
                dve.tensor_copy(x_t[:, ch, :], psum[:, 1024 * (ch % 2):1024 * (ch % 2) + TALL])\
                   .then_inc(s["x_cols_copied"], 1)
            dve.wait_ge(s_cond, 3)
            dve.tensor_tensor(cond4[:, :, 1:4:2], cond[:], cond4[:, :, 0:4:2].bitcast(F32), ALU.subtract)\
               .then_inc(s_cond, 1)

            def stage_ada(st):
                ada_v = ada.rearrange("p s (g j) -> p s g j", j=4)
                add_v = vec[:, st.layer, V_BADA:V_BADA + 48].rearrange("p (g j) -> p g j", j=4)

                def body(i):
                    wait(dve, st, "ada_cols_done", i)
                    for e in range(2):
                        ins = dve.tensor_tensor(ada_v[:, e, i, :], bank(2, 8)[:, e:8:2], add_v[:, i, :], ALU.add)
                    ins.then_inc(s["ada_cols_added"], 1)
                passes(dve, st, body)
                wait(dve, st, "ada_cols_added", st.trips - 1)
                for n, (scale, g) in enumerate(((SC1, V_N1), (SC2, V_N2))):
                    for e in range(2):
                        ins = dve.scalar_tensor_tensor(a_mod[:, n, e, :], ada[:, e, KC * scale:KC * scale + KC], 1.0,
                                                       vec[:, st.layer, g:g + KC], ALU.add, ALU.mult)
                ins.then_inc(s_mod, 1)
                dve.wait_ge(s_mod, st.layer + 1)

            def inverse_mean(st, width, number):
                wait(dve, st, "sq_used", st.trips - 1)
                dve.tensor_scalar(rstd[:, 0:width], psum[:, 0:width], 1.0 / D_MODEL, EPS, ALU.mult, ALU.add)\
                   .then_inc(s_ms, 1)
                dve.wait_ge(s_ms, 2 * number - 1)
                dve.reciprocal(rstd[:, 0:width], rstd[:, 0:width]).then_inc(s_ms, 1)
                dve.wait_ge(s_rstd, number)

            def stage_norm(st, width, number, which, shift):
                inverse_mean(st, width, number)

                def body(i):
                    for k in range(2):
                        wait(dve, st, "h_lo_done", i, k - 1)
                        for e, t0, t1 in segs(width):
                            ins = dve.scalar_tensor_tensor(normed_t[:, k, t0:t1], chunk(x_t, i, k)[:, t0:t1],
                                                           mod_col(which, e, i, k), rstd[:, t0:t1], ALU.mult,
                                                           ALU.mult)
                        ins.then_inc(s["normed"], 1)
                    for k in range(2):
                        wait(dve, st, "h_hi_done", i, k + 1)
                        for e, t0, t1 in segs(width):
                            ins = dve.scalar_tensor_tensor(chunk(h_lo, i, k)[:, t0:t1], normed_t[:, k, t0:t1],
                                                           ada_col(e, shift, i, k),
                                                           chunk(h_hi, i, k)[:, t0:t1].bitcast(F32), ALU.add,
                                                           ALU.subtract)
                        ins.then_inc(s["h_lo_done"], 1)
                passes(dve, st, body)

            def qk_lo(st, i, his, pieces, name, scale):
                wait(dve, st, name + "_hi", i)
                for (dst, src), (hi, _) in zip(pieces, his):
                    ins = rest(dst, src, hi, scale)
                ins.then_inc(s[name + "_lo"], 1)

            def stage_vt(st, i):
                wait(dve, st, "v_hi", i)
                rest(v_lo[:], psum[:, 6 * 512:6 * 512 + TALL], v_hi[:]).then_inc(s["v_lo"], 1)

            def attention(st, kind, i):
                tiles = attention_tiles(kind, st.layer)
                marks = [0]

                def front(n, e):
                    if n >= len(tiles):
                        return
                    q0, _, width, band, variant = tiles[n]
                    base = 1024 * (1 + e)
                    wait(dve, st, "scores_done", i, 2 * n + e + 1)
                    if kind == "B" and n == 0:
                        dve.tensor_copy(psum[:, base + SINK:base + SINK + 1], sink_col(st.layer, e, i))\
                           .then_inc(s["sunk"], 1)
                        wait(dve, st, "sunk", i, e + 1)
                    if width:
                        if kind == "A":
                            at_ = psum[:, base + BAND_END - width:base + BAND_END]
                            by = bias[:, variant, e, :]
                        elif q0 == 0:
                            at_, by = psum[:, base + 3 * P:base + 4 * P], mask_b[:, 1, :]
                        elif q0 == SEQ - P:
                            at_, by = psum[:, base + 2 * P:base + 3 * P], mask_b[:, 0, :]
                        else:
                            at_ = psum[:, base + P:base + 5 * P].rearrange("p (a b) -> p a b", b=2 * P)[:, :, 0:P]
                            by = mask_b[:, :, :]
                        dve.tensor_tensor(at_, at_, by, ALU.add).then_inc(s["masked"], 1)
                        wait(dve, st, "masked", i, 2 * n + e + 1)
                    c0, c1 = BAND_END - width, SINK + (kind == "B")
                    dve.tensor_reduce(nmax[:, n % 2, e:e + 1], psum[:, base + c0:base + c1], AX.X, ALU.max,
                                      negate=True).then_inc(s["max_done"], 1)

                def normalise(n):
                    for e in range(2):
                        wait(dve, st, "exp_done", i, 2 * n + e + 1)
                        dve.reciprocal(rinv[:, n % 2, e:e + 1], rsum[:, n % 2, e:e + 1]).then_inc(s["inv_done"], 1)
                    for e in range(2):
                        wait(dve, st, "inv_done", i, 2 * n + e + 1)
                        c0 = BAND_END - tiles[n][2] - BAND0
                        part = probs[:, n % 2, e, c0:CTX_END - BAND0]
                        dve.tensor_scalar(part, part, rinv[:, n % 2, e:e + 1], None, ALU.mult)\
                           .then_inc(s["p_done"], 1)

                if kind == "A":
                    wait(dve, st, "bias_done", i)
                front(0, 0)
                front(0, 1)
                g0 = 0
                for n, tile in enumerate(tiles):
                    groups = chunk_groups(tile)

                    def turned(g):
                        wait(dve, st, "pt_hi", i, g0 + g + 1)
                        par, w = (g0 + g) % 2, 2 * P * len(groups[g])
                        rest(pt_lo[:, par, 0:w], bank((6, 0)[par], w), pt_hi[:, par, 0:w]).then_inc(s["pt_lo"], 1)

                    normalise(n)
                    front(n + 1, 0)
                    turned(0)
                    front(n + 1, 1)
                    for g in range(1, len(groups)):
                        turned(g)
                    g0 += len(groups)
                    wait(dve, st, "o_hi", i, n + 1)
                    for (dst, src), (hi, _) in zip(out_pieces(br_lo, kind, i, n, tile[0]),
                                                   out_pieces(br_hi, kind, i, n, tile[0])):
                        ins = rest(dst, src, hi)
                    ins.then_inc(s["o_lo"], 1)

            def stage_a(st):
                width = width_of(st.layer)

                def body(i):
                    qk_lo(st, i, q_pieces_a(q_hi, width), q_pieces_a(q_lo, width), "q", QSCALE)
                    qk_lo(st, i, k_pieces_a(k_hi), k_pieces_a(k_lo), "k", 1.0)
                    stage_vt(st, i)
                    attention(st, "A", i)
                passes(dve, st, body)

            def rotate(st, i, src):
                wait(dve, st, "swapped", i)
                dve.tensor_tensor(rc[:], src, rope[:, 0, :], ALU.mult).then_inc(s["rope_step"], 1)
                dve.tensor_tensor(rs[:], swap[:], rope[:, 1, :], ALU.mult).then_inc(s["rope_step"], 1)
                wait(dve, st, "rope_step", i, 2)
                dve.tensor_tensor(rc[:], rc[:], rs[:], ALU.add).then_inc(s["rope_step"], 1)
                wait(dve, st, "rope_step", i, 3)

            def stage_bkv(st):
                rotate(st, 0, bank(2))
                qk_lo(st, 0, [(k_hi[:, 0:SEQ], None), (k_hi[:, 640:640 + CTX], None)],
                      [(k_lo[:, 0:SEQ], rc[:]), (k_lo[:, 640:640 + CTX], bank(3, CTX))], "k", 1.0)
                stage_vt(st, 0)

            def stage_b(st):
                parts = [(0, SEQ)] + ([(SEQ, TALL)] if st.layer == 0 else [])

                def body(i):
                    rotate(st, i, bank(0))
                    qk_lo(st, i, [(q_hi[:, a:b], None) for a, b in parts],
                          [(q_lo[:, a:b], rc[:] if a == 0 else bank(1, CTX)) for a, b in parts], "q", QSCALE)
                    attention(st, "B", i)
                passes(dve, st, body)

            def stage_merge(st):
                width = width_of(st.layer)

                def body(i):
                    wait_block(dve, st, i, 1)
                    wait(dve, st, "gate_ready", i)
                    m = tile_of(merged, i)[:, 0:width]
                    if st.name == "mergeA":
                        dve.tensor_tensor(m, psum[:, 1024:1024 + width], gate[:, 0:width], ALU.mult)\
                           .then_inc(s["mix_done"], 1)
                    else:
                        wait(dve, st, "mixed", i, 0)
                        dve.tensor_tensor(mix[:, 0:width], psum[:, 1024:1024 + width], gate[:, 0:width], ALU.mult)\
                           .then_inc(s["mix_done"], 1)
                        wait(dve, st, "mix_done", i)
                        dve.tensor_tensor(m, m, mix[:, 0:width], ALU.add).then_inc(s["mixed"], 1)
                passes(dve, st, body)

            def stage_c(st):
                width = width_of(st.layer)
                span = width + (2 if width == TALL else 0)

                def body(i):
                    wait_block(dve, st, i, 1)
                    wait(dve, st, "cx_copied", i)
                    for e, t0, t1 in segs(width):
                        ins = dve.tensor_tensor(u_pad[:, t0 + 1 + 2 * e:t1 + 1 + 2 * e], psum[:, 1024 + t0:1024 + t1],
                                                cx_sb[:, t0:t1], ALU.mult)
                    ins.then_inc(s["u_done"], 1)
                    wait(dve, st, "u_done", i)
                    dve.tensor_scalar(y_a[:, 0:span], u_pad[:, 1:span + 1], vec_col(st.layer, V_CONV + 4, i), None,
                                      ALU.mult).then_inc(s["y_step"], 1)
                    wait(dve, st, "y_step", i, 1)
                    dve.scalar_tensor_tensor(y_b[:, 0:span], u_pad[:, 0:span], vec_col(st.layer, V_CONV, i),
                                             y_a[:, 0:span], ALU.mult, ALU.add).then_inc(s["y_step"], 1)
                    wait(dve, st, "y_step", i, 2)
                    dve.scalar_tensor_tensor(y_a[:, 0:span], u_pad[:, 2:span + 2], vec_col(st.layer, V_CONV + 8, i),
                                             y_b[:, 0:span], ALU.mult, ALU.add).then_inc(s["y_step"], 1)
                    wait(dve, st, "y_step", i, 3)
                    wait_block(dve, st, i, 2)
                    wait(dve, st, "c_lo", i, 0)
                    for e, t0, t1 in segs(width):
                        ins = dve.tensor_tensor(c_out[:, t0:t1], psum[:, 2048 + t0:2048 + t1],
                                                y_a[:, t0 + 2 * e:t1 + 2 * e], ALU.mult)
                    ins.then_inc(s["c_done"], 1)
                    wait(dve, st, "c_hi", i)
                    rest(pair(br_lo, i)[:, 0:width], c_out[:, 0:width], pair(br_hi, i)[:, 0:width])\
                        .then_inc(s["c_lo"], 1)

                wait(dve, stage_of["mergeB", st.layer], "mixed", 7)
                dve.memset(u_pad[:, 0:1], 0.0)
                dve.memset(u_pad[:, SEQ + 1:SEQ + 3], 0.0)
                dve.memset(u_pad[:, TALL + 3:TALL + 4], 0.0).then_inc(s_zero, 1)
                dve.wait_ge(s_zero, st.layer + 1)
                passes(dve, st, body)

            def stage_split(st):
                width = width_of(st.layer)
                wait(dve, stage_of["mergeC", st.layer], "mixed", 7)

                def body(i):
                    for k in range(2):
                        wait(dve, st, "h_hi_done", i, k + 1)
                        rest(chunk(h_lo, i, k)[:, 0:width], chunk(merged, i, k)[:, 0:width],
                             chunk(h_hi, i, k)[:, 0:width]).then_inc(s["h_lo_done"], 1)
                passes(dve, st, body)

            def stage_residual(st, piece, blocks_per_tile):
                width = width_of(st.layer)

                def body(i):
                    for k in range(2):
                        wait_block(dve, st, i, (k + 1) * blocks_per_tile - 1)
                        for e, t0, t1 in segs(width):
                            xs = chunk(x_t, i, k)[:, t0:t1]
                            ins = dve.scalar_tensor_tensor(xs, psum[:, 1024 * k + t0:1024 * k + t1],
                                                           ada_col(e, piece, i, k), xs, ALU.mult, ALU.add)
                        ins.then_inc(s["x_updated"], 1)
                passes(dve, st, body)

            def stage_up(st):
                width = width_of(st.layer)

                def body(i):
                    wait_block(dve, st, i, 1)
                    wait(dve, st, "silu_done", i)
                    wait(dve, st, "act_lo", i, 0)
                    dve.tensor_tensor(act_sb[:, 0:width], psum[:, 1024:1024 + width], silu_sb[:, 0:width], ALU.mult)\
                       .then_inc(s["act_done"], 1)
                    wait(dve, st, "act_hi", i)
                    rest(tile_of(a_lo, i)[:, 0:width], act_sb[:, 0:width], tile_of(a_hi, i)[:, 0:width])\
                        .then_inc(s["act_lo"], 1)
                passes(dve, st, body)

            for l in range(DEPTH):
                stage_ada(stage_of["ada", l])
                stage_norm(stage_of["norm1", l], TALL, 2 * l + 1, 0, SH1)
                stage_a(stage_of["A", l])
                stage_merge(stage_of["mergeA", l])
                stage_bkv(stage_of["Bkv", l])
                stage_b(stage_of["B", l])
                stage_merge(stage_of["mergeB", l])
                stage_c(stage_of["C", l])
                stage_merge(stage_of["mergeC", l])
                stage_split(stage_of["split", l])
                stage_residual(stage_of["out", l], G1, 1)
                stage_norm(stage_of["norm2", l], width_of(l), 2 * l + 2, 1, SH2)
                for f in range(2):
                    stage_up(stage_of[f"up{f}", l])
                    wait(dve, stage_of[f"up{f}", l], "act_lo", HALF_FF - 1)
                    stage_residual(stage_of[f"down{f}", l], G2, 2)
            last = stage_of["final", DEPTH - 1]
            inverse_mean(last, SEQ, 2 * DEPTH + 1)
            for ch in range(KC):
                dve.scalar_tensor_tensor(y_fm[:, ch, :], x_t[:, ch, 0:SEQ], vec[:, 0, V_FINAL + ch:V_FINAL + ch + 1],
                                         rstd[:, 0:SEQ], ALU.mult, ALU.mult).then_inc(s_yfm, 1)


_INS = ["x", "c", "ctx", "c_ctx", "w_ada", "b_ada", "norm1_g", "norm2_g", "w_in", "b_gate", "na_rpb", "sw_sink",
        "conv_w", "w_br_a", "w_br_b", "w_br_c", "w_o", "w_ffn_up", "w_ffn_down", "final_norm_g"]


def shape_constants():
    import numpy as np

    ident = np.eye(P, dtype=np.float32)
    a = np.arange(P)[:, None] // ROWS
    b = np.arange(2 * P)[None, :] // ROWS
    starts = [np.maximum(a, 8), a, np.minimum(a, 8)]
    masks_a = np.stack([np.where((b >= st) & (b < st + WIN_COLS), 0.0, NEG) for st in starts], 1)
    q, k = np.arange(P)[:, None], np.arange(P)[None, :]
    masks_b = np.stack([np.where(k >= q, 0.0, NEG), np.where(k <= q, 0.0, NEG)], 1)
    t = np.arange(SEQ)
    inv = np.float32(ROPE_THETA) ** (-np.arange(HD // 4, dtype=np.float32) / np.float32(HD // 4))
    ang = np.concatenate([(t // GRID_W).astype(np.float32)[:, None] * inv,
                          (t % GRID_W).astype(np.float32)[:, None] * inv], -1)
    f = np.arange(P) % HD
    cos = np.cos(ang).T[f % 32]
    sin = np.sin(ang).T[f % 32] * np.where(f < 32, -1.0, 1.0)[:, None]
    comb = np.array([[1, 0], [1, 0], [0, 1], [0, 1]])
    return {"ident": ident, "masks_a": masks_a.astype(np.float32), "masks_b": masks_b.astype(np.float32),
            "rope": np.stack([cos, sin], 1).astype(np.float32), "comb": comb.astype(np.float32)}


def kernel(**inputs):
    import numpy as np
    import concourse.bacc as bacc
    from concourse.bass_utils import run_bass_kernel_spmd as run

    nc = bacc.Bacc("TRN2", target_bir_lowering=False, num_devices=1)
    arrays, args = {}, []

    def give(name, a):
        a = np.ascontiguousarray(a)
        arrays[f"in_{name}"] = a
        args.append(nc.dram_tensor(f"in_{name}", a.shape, mybir.dt.from_np(a.dtype), kind="ExternalInput").ap())

    for name in _INS:
        a = np.asarray(inputs[name])
        if name == "na_rpb":
            edge = np.zeros(RPB_PAD, a.dtype)
            a = np.concatenate([edge, a[:, :, ::-1, ::-1].reshape(-1), edge])
        give(name, a)
    for name, a in shape_constants().items():
        give(name, a)
    out = nc.dram_tensor("out_0", (1, SEQ, D_MODEL), F32, kind="ExternalOutput").ap()
    build(nc, *args, out)
    r = run(nc, [arrays], core_ids=[0])
    return r.results[0]["out_0"]
```

```python
from contextlib import ExitStack

import concourse.bass as bass
from concourse import mybir

F32 = mybir.dt.float32
F32R = mybir.dt.float32r
ALU = mybir.AluOpType
ACT = mybir.ActivationFunctionType
AX = mybir.AxisListType

P = 128
D_MODEL = 1024
KC = D_MODEL // P
SEQ = 512
CTX = 256
TALL = SEQ + CTX
DEPTH = 2
GRID_W = 64
ROWS = SEQ // GRID_W
HD = 64
NA_HEADS = 8
WIN_ROWS, WIN_COLS = 8, 16
RPB = (2 * WIN_ROWS - 1) * (2 * WIN_COLS - 1)
RPB_W = 2 * WIN_COLS - 1
SW_HEADS = 8
PAIRS = 4
ADA_W = 256
ADA_FIRST = 2 * D_MODEL // ADA_W
BR = 512
D_FF = 2816
HALF_FF = D_FF // P // 2
EPS = 1e-6
ROPE_THETA = 10000.0
NEG = -1e30
QSCALE = HD ** -0.5
RPB_PAD = 8
SEG = (WIN_ROWS - 1) * RPB_W + 32

CT_QA, CT_KA, CT_VA, CT_QB, CT_KB, CT_VB, CT_X, CT_GB, CT_GC, CT_ZG = 0, 4, 8, 12, 16, 17, 18, 22, 26, 30
V_BADA, V_N1, V_N2, V_BGATE, V_CONV, V_FINAL, V_C, V_CC, V_END = 0, 48, 56, 64, 88, 100, 108, 116, 124
SH1, SC1, G1, SH2, SC2, G2 = range(6)

BAND0, BAND_END, CTX_END, SINK = 128, 512, 768, 768


class Stage:

    def __init__(self, name, layer, trips, blocks, ada, counts):
        self.name, self.layer, self.trips = name, layer, trips
        self.tags = [tag for tag, _ in blocks]
        self.slots = [slot for _, slot in blocks]
        self.dmas = [2 if tag in ("q0", "q1") or (tag == "m" and name == "mergeB") else 1 for tag in self.tags]
        self.per = len(blocks)
        self.ada = ada
        self.counts = counts
        self.base = {}

    def pos(self, tag):
        return self.tags.index(tag)


PRIMED = dict(ada_rows_copied=1, ada_cols_done=1, ada_cols_added=1, sq_added=2, bias_done=1, masked=1, o_lo=1,
              gate_ready=1, mix_done=1, mixed=1, u_done=1, c_done=1, x_updated=2, silu_done=1, act_done=1,
              h_lo_done=2, c_lo=1, act_lo=1)


def attention_tiles(kind, layer):
    tiles = []
    for j in range(SEQ // P):
        if kind == "A":
            tiles.append((P * j, P * j, 2 * P, [j, (j + 1) % 4], 0 if j == 0 else (2 if j == 3 else 1)))
        else:
            lo, hi = max(0, j - 1), min(3, j + 1)
            tiles.append((P * j, P * lo, P * (hi - lo + 1), list(range(lo, hi + 1)), None))
    if layer == 0:
        for j in range(CTX // P):
            tiles.append((SEQ + P * j, 0, 0, [], None))
    return tiles


def chunk_groups(tile):
    _, _, width, band, _ = tile
    cols = [(v, BAND_END - width - BAND0 + P * n) for n, v in enumerate(band)]
    cols += [(4, BAND_END - BAND0), (5, BAND_END - BAND0 + P)]
    return [cols[n:n + 2] for n in range(0, len(cols), 2)]


def plan():
    stages = []

    def add(name, layer, trips, blocks=(), ada=None, **counts):
        if ada:
            counts.update(ada_rows_copied=ada[2], ada_cols_done=ada[2], ada_cols_added=ada[2])
        stages.append(Stage(name, layer, trips, list(blocks), ada, counts))

    def with_ada(blocks):
        return [b for n, own in enumerate(blocks) for b in ((f"a{n}", 2), own)]

    add("load", 0, 1, x_cols_done=8, x_cols_copied=8, sq_ready=8, sq_added=8)
    add("ada", 0, 1, [(f"a{n}", n % 3) for n in range(2 * ADA_FIRST)], (0, 0, ADA_FIRST))
    for l in range(DEPTH):
        nt = len(attention_tiles("A", l))
        ga = sum(len(chunk_groups(t)) for t in attention_tiles("A", l))
        gb = sum(len(chunk_groups(t)) for t in attention_tiles("B", l))
        now, ahead = l == 0, l + 1 < DEPTH
        add("norm1", l, 4, normed=2, h_hi_done=2, h_lo_done=2)
        att = dict(scores_done=2 * nt, max_done=2 * nt, exp_done=2 * nt,
                   masked=8, inv_done=2 * nt, p_done=2 * nt, o_done=nt, o_hi=nt, o_lo=nt)
        qkv = [("q", 2), ("k", 0), ("v", 1)]
        made = dict(q_hi=1, q_lo=1, k_hi=1, k_lo=1, v_copied=1)
        used = dict(vt_done=1, v_hi=1, v_lo=1, pt_done=ga, pt_hi=ga, pt_lo=ga, **att)
        add("A0", l, 1, qkv, bias_done=1, **made)
        add("A", l, PAIRS - 1, qkv, bias_done=1, **made, **used)
        add("Az", l, 1, **used)
        merge = [("z", 0), ("m", 1)]
        add("mergeA", l, 8, with_ada(merge) if now else merge, (l, ADA_FIRST, 1) if now else None,
            gate_ready=1, mix_done=1)
        made = dict(q_hi=1, q_lo=1, swapped=1, rope_cos=1, rope_sin=1, rotated=1)
        used = dict(sunk=2, pt_done=gb, pt_hi=gb, pt_lo=gb, **att)
        add("B0", l, 1, [("k", 0), ("q0", 2), ("q1", 1), ("v", 0)], k_hi=1, k_lo=1, v_copied=1, vt_done=1,
            v_hi=1, v_lo=1, q_hi=1, q_lo=1, swapped=2, rope_cos=2, rope_sin=2, rotated=2)
        add("B", l, PAIRS - 1, [("q0", 2), ("q1", 1)], q_summed=1 if l == 0 else 0, **made, **used)
        add("Bz", l, 1, **used)
        add("mergeB", l, 8, with_ada(merge) if now else merge, (l, ADA_FIRST + 8, 1) if now else None,
            gate_ready=1, mix_done=1, mixed=1)
        add("C", l, 4, [("x", 2), ("c", 0), ("b", 1)], cx_copied=1, u_done=1,
            y_step=3, c_done=1, c_hi=1, c_lo=1)
        add("mergeC", l, 8, with_ada(merge) if ahead else merge, (l + 1, 0, 1) if ahead else None,
            gate_ready=1, mix_done=1, mixed=1)
        add("split", l, 4, h_hi_done=2, h_lo_done=2)
        add("out", l, 4, [("o0", 0), ("o1", 1)], x_updated=2, sq_ready=2, sq_added=2)
        add("norm2", l, 4, normed=2, h_hi_done=2, h_lo_done=2)
        for f in range(2):
            add(f"up{f}", l, HALF_FF, [("gate", 0), ("up", 1)], silu_done=1, act_done=1,
                act_hi=1, act_lo=1)
            down = [("d0", 0), ("e0", 1), ("d1", 0), ("e1", 1)]
            squares = dict(sq_ready=2, sq_added=2) if f == 1 else {}
            add(f"down{f}", l, 4, with_ada(down) if ahead else down,
                (l + 1, 8 + 8 * f, 2) if ahead else None, x_updated=2, **squares)
    add("final", DEPTH - 1, 1)

    totals = dict(PRIMED)
    block = 0
    for st in stages:
        st.block = block
        block += st.trips * st.per
        st.base = dict(totals)
        for name, n in st.counts.items():
            totals[name] = totals.get(name, 0) + n * st.trips
    return {(st.name, st.layer): st for st in stages}, stages, totals


def build(nc, x, c, ctx, c_ctx, w_ada, b_ada, norm1_g, norm2_g, w_in, b_gate, rpb, sw_sink, conv_w,
          w_br_a, w_br_b, w_br_c, w_o, w_up, w_down, final_g, ident_in, masks_a, masks_b, rope_in, comb_in,
          out):
    stage_of, stages, totals = plan()
    blocks = [(st, i, k) for st in stages for i in range(st.trips) for k in range(st.per)]
    by_vector = stage_of["ada", 0].per

    landed, per_slot = [], [0, 0, 0]
    for st, i, k in blocks:
        per_slot[st.slots[k]] += 16 * st.dmas[k]
        landed.append(per_slot[st.slots[k]])

    distance, user = [], {}
    for b, (st, i, k) in enumerate(blocks):
        distance.append(b - user.get(st.slots[k], -1000))
        user[st.slots[k]] = b
    assert min(distance) >= 2

    stack = ExitStack()
    with stack:
        def sb(where, name, shape, dt=F32):
            return where.enter_context(nc.sbuf_tensor(name, shape, dt))

        def sem(name):
            return stack.enter_context(nc.semaphore(name))

        x_t = sb(stack, "x_t", [P, KC, TALL])
        h_hi = sb(stack, "h_hi", [P, KC, TALL], F32R)
        h_lo = sb(stack, "h_lo", [P, KC, TALL], F32R)
        w_raw = sb(stack, "w_raw", [P, 3, KC * P])
        w_hi = sb(stack, "w_hi", [P, 3, KC * P], F32R)
        w_lo = sb(stack, "w_lo", [P, 3, KC * P], F32R)
        ident = sb(stack, "ident", [P, P])
        ones = sb(stack, "ones", [P, P])
        mask_b = sb(stack, "mask_b", [P, 2, P])
        rope = sb(stack, "rope", [P, 2, SEQ])
        comb = sb(stack, "comb", [4, 2])
        eps = sb(stack, "eps", [P, 1])
        warm_sb = sb(stack, "warm_sb", [P, 48])
        rows = sb(stack, "rows", [4, ADA_W])
        vec = sb(stack, "vec", [P, DEPTH, P])
        sink = sb(stack, "sink", [P, DEPTH, SW_HEADS])
        ada = sb(stack, "ada", [P, DEPTH, 2, 48])
        a_mod = sb(stack, "a_mod", [P, 2, 2, KC])
        cond = sb(stack, "cond", [P, KC, 2])
        cond4 = sb(stack, "cond4", [P, KC, 4], F32R)
        nmax = sb(stack, "nmax", [P, 2, 2])
        rsum = sb(stack, "rsum", [P, 2, 2])
        rinv = sb(stack, "rinv", [P, 2, 2])

        with ExitStack() as r:
            tok = sb(r, "tok", [P, TALL // P, D_MODEL])
            vec_rows = sb(r, "vec_rows", [P, DEPTH, P])
        with ExitStack() as r:
            rstd = sb(r, "rstd", [P, TALL])
            normed_t = sb(r, "normed_t", [P, 2, TALL])
        with ExitStack() as r:
            br_hi = sb(r, "br_hi", [P, PAIRS, TALL], F32R)
            br_lo = sb(r, "br_lo", [P, PAIRS, TALL], F32R)
            with ExitStack() as r2:
                rpb_seg = sb(r2, "rpb_seg", [P, NA_HEADS, SEG])
                mask_a = sb(r2, "mask_a", [P, 3, 2 * P])
                v_fm_a = sb(r2, "v_fm_a", [P, TALL])
                with ExitStack() as r3:
                    rpb_back = sb(r3, "rpb_back", [P, NA_HEADS, SEG])
                with ExitStack() as r3:
                    bias = sb(r3, "bias", [P, 3, 2, 2 * P])
            merged = sb(r, "merged", [P, KC, TALL])
            with ExitStack() as r2:
                q_hi = sb(r2, "q_hi_t", [P, TALL], F32R)
                q_lo = sb(r2, "q_lo_t", [P, TALL], F32R)
                k_hi = sb(r2, "k_hi_t", [P, 640 + CTX], F32R)
                k_lo = sb(r2, "k_lo_t", [P, 640 + CTX], F32R)
                v_hi = sb(r2, "v_hi_t", [P, TALL], F32R)
                v_lo = sb(r2, "v_lo_t", [P, TALL], F32R)
                pt_hi = sb(r2, "pt_hi_t", [P, 2, 4 * P], F32R)
                pt_lo = sb(r2, "pt_lo_t", [P, 2, 4 * P], F32R)
                swap = sb(r2, "swap", [P, SEQ])
                rc = sb(r2, "rc", [P, SEQ])
                with ExitStack() as r3:
                    probs = sb(r3, "probs", [P, 2, 2, 644])
                with ExitStack() as r3:
                    v_fm = sb(r3, "v_fm", [P, TALL])
            with ExitStack() as r2:
                gate = sb(r2, "gate", [P, TALL])
                mix = sb(r2, "mix", [P, TALL])
            with ExitStack() as r2:
                cx_sb = sb(r2, "cx_sb", [P, TALL])
                u_pad = sb(r2, "u_pad", [P, TALL + 4])
                y_a = sb(r2, "y_a", [P, TALL + 2])
                y_b = sb(r2, "y_b", [P, TALL + 2])
                c_out = sb(r2, "c_out", [P, TALL])
        with ExitStack() as r:
            a_hi = sb(r, "a_hi", [P, HALF_FF, TALL], F32R)
            a_lo = sb(r, "a_lo", [P, HALF_FF, TALL], F32R)
            silu_sb = sb(r, "silu_sb", [P, TALL])
            act_sb = sb(r, "act_sb", [P, TALL])
            sq = sb(r, "sq", [P, 2, TALL])
            ssum = sb(r, "ssum", [P, TALL])
        with ExitStack() as r:
            r.enter_context(nc.sbuf_tensor("under_y", [P, 3 * TALL], F32))
            y_fm = sb(r, "y_fm", [P, KC, SEQ])
            y_tok = sb(r, "y_tok", [P, 2, D_MODEL])

        psum = stack.enter_context(nc.psum_tensor("psum", [P, 8 * 512], F32))

        def bank(n, width=512):
            return psum[:, 512 * n:512 * n + width]

        s = {name: sem(name) for name in totals}
        s_const = sem("const_loaded")
        s_load = [sem(f"w_loaded{n}") for n in range(3)]
        s_whi = sem("w_hi_done")
        s_wlo = sem("w_lo_done")
        s_block = sem("block_done")
        s_vecT = sem("vec_transposed")
        s_vec = sem("vec_copied")
        s_ones = sem("ones_set")
        s_zero = sem("pad_zeroed")
        s_cond = sem("cond_step")
        s_mod = sem("mod_ready")
        s_ms = sem("mean_square_step")
        s_rstd = sem("rstd_ready")
        s_yfm = sem("y_ready")
        s_yT = sem("y_transposed")
        s_ytok = sem("y_copied")
        s_out = [sem(f"out_stored{n}") for n in range(2)]
        s_rpb = sem("rpb_loaded")
        s_rpbf = sem("rpb_forward")
        s_wlov = sem("w_lo_done_by_vector")
        s_ssz = sem("sum_zeroed")
        s_sumsq = sem("squares_summed")

        CONSTS = 3 + DEPTH * 9 + 3

        WI = w_in.rearrange("l (kc p) (ct f) -> l ct p kc f", p=P, f=P)
        WI64 = w_in.rearrange("l (kc p) (ct f) -> l ct p kc f", p=P, f=HD)
        WADA = w_ada.rearrange("l (kc p) (g f) -> l g p kc f", p=P, f=ADA_W)
        WBR = {"A": w_br_a.rearrange("l (kc p) (d f) -> l d p kc f", p=P, f=P),
               "B": w_br_b.rearrange("l (e kc p) (d f) -> l d e p kc f", e=2, p=HD, f=P),
               "C": w_br_c.rearrange("l (kc p) (d f) -> l d p kc f", p=P, f=P)}
        WO = w_o.rearrange("l (kc p) (d f) -> l d p kc f", p=P, f=P)
        WUP = w_up.rearrange("l (kc p) (ct f) -> l ct p kc f", p=P, f=P)
        WDN = w_down.rearrange("l (kc p) (d f) -> l d p kc f", p=P, f=P)

        def block_source(st, i, k):
            l, name = st.layer, st.name
            slot = w_raw[:, st.slots[k], :]

            def cols(kc):
                return slot[:, 0:kc * P].rearrange("p (kc f) -> p kc f", f=P)

            tag = st.tags[k]
            if st.ada and tag[0] == "a":
                al, first, n = st.ada
                unit, half = int(tag[1:]) // 2, int(tag[1:]) % 2
                return [(slot.rearrange("p (kc f) -> p kc f", f=ADA_W),
                         WADA[al, i * n + (first + unit), :, 4 * half:4 * half + 4])]
            if name in ("A0", "A"):
                return [(cols(KC), WI[l, i + dict(q=CT_QA, k=CT_KA, v=CT_VA)[tag] + (1 if name == "A" else 0)])]
            if name == "B0" and tag in ("k", "v"):
                return [(cols(KC), WI[l, dict(k=CT_KB, v=CT_VB)[tag]])]
            if name in ("B0", "B"):
                j = i + (1 if name == "B" else 0)
                d = cols(KC // 2)
                first = KC // 2 * int(tag[1])
                return [(d[:, :, HD * e:HD * e + HD], WI64[l, j + 2 * CT_QB + 4 * e, :, first:first + KC // 2])
                        for e in range(2)]
            if name == "C":
                return [(cols(KC), WI[l, i + dict(x=CT_X, c=CT_GC, b=CT_GB)[tag]])]
            if name.startswith("merge"):
                kind = name[5]
                if tag == "z":
                    return [(cols(KC), WI[l, i + CT_ZG + 8 * "ABC".index(kind)])]
                if kind == "B":
                    return [(cols(4)[HD * e:HD * e + HD], WBR["B"][l, i, e]) for e in range(2)]
                return [(cols(4), WBR[kind][l, i])]
            if name == "out":
                return [(cols(KC), WO[l, i * 2 + k])]
            if name.startswith("up"):
                f = int(name[2])
                return [(cols(KC), WUP[l, i + HALF_FF * f + (0 if tag == "gate" else 2 * HALF_FF)])]
            f = int(name[4])
            first, n = (HALF_FF * f, KC) if tag[0] == "d" else (HALF_FF * f + KC, HALF_FF - KC)
            return [(cols(n), WDN[l, i * 2 + int(tag[1]), :, first:first + n])]

        def block_width(st, k):
            tag = st.tags[k]
            if tag in ("q0", "q1", "m"):
                return 4 * P
            return (HALF_FF - KC) * P if tag in ("e0", "e1") else KC * P

        def block_at(st, i, k):
            if isinstance(i, int):
                b = st.block + i * st.per + k
                if b >= len(blocks):
                    return None
                return (*blocks[b], b)
            assert k < 2 * st.per
            return (st, i + k // st.per, k % st.per, i * st.per + (st.block + k))

        def load_value(st, i, k):
            first = landed[st.block + k]
            if isinstance(i, int):
                return landed[st.block + i * st.per + k]
            if st.trips == 1:
                return first
            return i * (landed[st.block + st.per + k] - first) + first

        def passes(eng, st, body, first=0):
            for i in range(first):
                body(i)
            if st.trips > first + 1:
                with eng.Fori(first, st.trips - 1) as i:
                    body(i)
            body(st.trips - 1)

        def at(st, name, i, k):
            return i * st.counts[name] + (st.base.get(name, 0) + k)

        def wait(eng, st, name, i, k=None):
            v = at(st, name, i, st.counts[name] if k is None else k)
            if not (isinstance(v, int) and v <= 0):
                eng.wait_ge(s[name], v)

        def wait_block(eng, st, i, k):
            eng.wait_ge(s_block, block_at(st, i, k)[3] + 1)

        def wait_lo(eng, b):
            if isinstance(b, int) and b < by_vector:
                eng.wait_ge(s_wlov, b + 1)
            else:
                eng.wait_ge(s_wlo, b + 1)

        def slot_distance(blk):
            st, i, k, b = blk
            return distance[b] if isinstance(b, int) else distance[st.block + st.per + k]

        def h_ready(st):
            return lambda eng, kc: wait(eng, st, "h_lo_done", kc // 2, kc % 2 + 1)

        def wait_before(eng, st, name, i):
            if name in st.counts:
                wait(eng, st, name, i, 0)
            else:
                wait_total(eng, st, name)

        def prime(eng, *names):
            for name in names:
                eng.sem_inc(s[name], PRIMED[name])

        def wait_total(eng, st, name):
            v = st.base.get(name, 0)
            if v > 0:
                eng.wait_ge(s[name], v)

        def segs(width):
            return [(0, 0, SEQ)] + ([(1, SEQ, TALL)] if width == TALL else [])

        def width_of(l):
            return TALL if l == 0 else SEQ

        def perm(ap):
            return ap.rearrange("p (r c) -> p c r", c=GRID_W)

        def grid(ap):
            return ap.rearrange("p (c r) -> p c r", r=ROWS)

        def chunk(t, i, k, n=2):
            if isinstance(i, int):
                return t[:, n * i + k, :]
            return t[:, :, :].rearrange("p (c k) t -> p c k t", k=n)[:, i, k, :]

        def x_chunk(i, k, n):
            return chunk(x_t, i, k, n)

        def pair_of(st, i):
            return PAIRS - 1 if st.name in ("Az", "Bz") else i

        def tile_of(t, i):
            return t[:, i, :]

        pair = tile_of

        def ada_col(l, e, piece, i, k):
            return ada[:, l, e, KC * piece:KC * piece + KC].rearrange("p (c k) -> p c k", k=2)[:, i, k:k + 1]

        def mod_col(which, e, i, k):
            return a_mod[:, which, e, :].rearrange("p (c k) -> p c k", k=2)[:, i, k:k + 1]

        def vec_col(l, first, i):
            if isinstance(i, int):
                return vec[:, l, first + i:first + i + 1]
            return vec[:, l, first:P].rearrange("p (a b) -> p a b", b=1)[:, i, :]

        def sink_col(l, e, i):
            return sink[:, l, 4 * e:4 * e + 4].rearrange("p (a b) -> p a b", b=1)[:, i, :]

        def rpb_runs(i, e):
            seg = rpb_seg[:, :, :].rearrange("p (i e) w -> p i e w", e=2)[:, i, e, :]
            return bass.AP(seg.tensor, seg.offset, [list(seg.ap[0]), [1, 32], [RPB_W, ROWS]])

        def score_base(kind, e):
            return 768 + 512 * e if kind == "A" else 1024 * (1 + e)

        def turn_bank(kind, g):
            return (6, 4 if kind == "A" else 0)[g % 2]

        def out_bank(kind, n):
            return 7

        def q_pieces_b(dst, layer):
            return [(dst[:, 0:SEQ], rc[:])] + ([(dst[:, SEQ:TALL], bank(2, CTX))] if layer == 0 else [])

        def q_pieces_a(dst, width, b):
            out_ = [(grid(dst[:, 0:SEQ]), perm(bank(b)))]
            return out_ + ([(dst[:, SEQ:TALL], bank(b + 1, CTX))] if width == TALL else [])

        def k_pieces_a(dst):
            src = perm(bank(2))
            return [(grid(dst[:, 64:64 + SEQ]), src), (grid(dst[:, 0:64]), src[:, 56:64, :]),
                    (grid(dst[:, 576:640]), src[:, 0:8, :]), (dst[:, 640:640 + CTX], bank(3, CTX))]

        def v_pieces_a():
            src = perm(bank(0))
            return [(grid(v_fm_a[:, 64:SEQ]), src[:, 0:56, :]), (grid(v_fm_a[:, 0:64]), src[:, 56:64, :]),
                    (v_fm_a[:, SEQ:TALL], bank(1, CTX))]

        def out_pieces(dst, kind, i, n, q0):
            pieces = []
            for e in range(2):
                part = slice(HD * e, HD * e + HD)
                src = bank(out_bank(kind, n))[part, P * e:P * e + P]
                d = dst[part, i, :]
                if kind == "A" and q0 < SEQ:
                    c0 = q0 // ROWS
                    pieces.append((perm(d[:, 0:SEQ])[:, c0:c0 + P // ROWS, :], grid(src)))
                else:
                    pieces.append((d[:, q0:q0 + P], src))
            return pieces

        block = stack.enter_context(nc.Block())

        @block.sync
        def _(sp):
            def const(dst, src):
                sp.dma_start(dst, src).then_inc(s_const, 16)

            const(tok[:, 0:4, :], x.rearrange("b (t p) d -> p (b t) d", p=P))
            const(tok[:, 4:6, :], ctx.rearrange("b (t p) d -> p (b t) d", p=P))
            const(ident[:], ident_in)
            for l in range(DEPTH):
                def vrow(first, src):
                    n = src.shape[0]
                    const(vec_rows[first:first + n, l, :], src)
                vrow(V_BADA, b_ada[l].rearrange("(a b) -> a b", b=P))
                vrow(V_N1, norm1_g[l].rearrange("(a b) -> a b", b=P))
                vrow(V_N2, norm2_g[l].rearrange("(a b) -> a b", b=P))
                vrow(V_BGATE, b_gate[l].rearrange("(a b) -> a b", b=P))
                vrow(V_CONV, conv_w[l].rearrange("k (a b) -> (k a) b", b=P))
                vrow(V_FINAL, final_g.rearrange("(a b) -> a b", b=P))
                vrow(V_C, c.rearrange("o (a b) -> (o a) b", b=P))
                vrow(V_CC, c_ctx.rearrange("(a b) -> a b", b=P))
                const(sink[:, l, :], bass.AP(sw_sink.tensor, l * SW_HEADS, [[0, P], [1, SW_HEADS]]))
            const(mask_b[:], masks_b)
            const(rope[:], rope_in)
            const(comb[:], comb_in)

            def load(blk):
                if blk is None:
                    return
                st, i, k, b = blk
                last = b - slot_distance(blk)
                if not (isinstance(last, int) and last < 0):
                    sp.wait_ge(s_whi, last + 1)
                    wait_lo(sp, last)
                for dst, src in block_source(st, i, k):
                    sp.dma_start(dst, src).then_inc(s_load[st.slots[k]], 16)

            first = stage_of["ada", 0]
            load(block_at(first, 0, 0))
            load(block_at(first, 0, 1))
            for st in stages:
                def body(i, st=st):
                    for k in range(st.per):
                        load(block_at(st, i, k + 2))
                if st.per:
                    passes(sp, st, body)
                if st.name == "A0":
                    if st.layer:
                        wait_total(sp, st, "x_updated")
                    else:
                        sp.wait_ge(s_vec, DEPTH)
                    for h in range(NA_HEADS):
                        off = RPB_PAD + (st.layer * NA_HEADS + h) * RPB - 8
                        src = bass.AP(rpb.tensor, off, [[1, P // ROWS], [RPB_W, ROWS], [1, SEG]])
                        sp.dma_start(rpb_back[:, h, :], src).then_inc(s_rpb, 16)
                    sp.dma_start(mask_a[:], masks_a).then_inc(s_rpb, 16)

            for t in range(SEQ // P):
                sp.wait_ge(s_ytok, t + 1)
                sp.dma_start(out[0, t * P:(t + 1) * P, :], y_tok[:, t % 2, :]).then_inc(s_out[t % 2], 16)
            for n in range(2):
                sp.wait_ge(s_out[n], 16 * (SEQ // P // 2))

        @block.gpsimd
        def _(pool):
            prime(pool, "bias_done", "sq_added")
            pool.sem_inc(s_wlo, by_vector)
            pool.memset(eps[:], EPS)
            pool.memset(ones[:], 1.0).then_inc(s_ones, 1)

            def new_sum(number):
                pool.memset(ssum[:], 0.0).then_inc(s_ssz, 1)
                pool.wait_ge(s_ssz, number)

            def add_squares(st, i, n):
                for k in range(n):
                    wait(pool, st, "sq_ready", i, k + 1)
                    wait(pool, st, "sq_added", i, k)
                    w = TALL if st.name == "load" else width_of(st.layer)
                    pool.tensor_tensor(ssum[:, 0:w], ssum[:, 0:w], sq[:, k % 2, 0:w], ALU.add)\
                        .then_inc(s["sq_added"], 1)

            def split_lo(blk):
                if blk is None:
                    return
                st, i, k, b = blk
                if isinstance(b, int) and b < by_vector:
                    return
                slot, w = st.slots[k], block_width(st, k)
                pool.wait_ge(s_whi, b + 1)
                last = b - slot_distance(blk)
                pool.wait_ge(s_block, last + 1)
                pool.tensor_tensor(w_lo[:, slot, 0:w], w_raw[:, slot, 0:w], w_hi[:, slot, 0:w].bitcast(F32),
                                   ALU.subtract).then_inc(s_wlo, 1)

            def rotate(st, i, n):
                wait(pool, st, "swapped", i, n + 1)
                pool.tensor_tensor(swap[:], swap[:], rope[:, 1, :], ALU.mult).then_inc(s["rope_sin"], 1)
                wait(pool, st, "rope_sin", i, n + 1)
                wait(pool, st, "rope_cos", i, n + 1)
                pool.tensor_tensor(rc[:], rc[:], swap[:], ALU.add).then_inc(s["rotated"], 1)

            def forward_runs(l):
                pool.wait_ge(s_rpb, 16 * (NA_HEADS + 1) * (l + 1))
                back = rpb_back[:, :, :]
                pool.tensor_copy(rpb_seg[:, :, :],
                                 bass.AP(back.tensor, back.offset + SEG - 1,
                                         [list(back.ap[0]), [SEG, NA_HEADS], [-1, SEG]])).then_inc(s_rpbf, 1)
                pool.wait_ge(s_rpbf, l + 1)

            def bias_tables(pair_):
                for v in range(3):
                    for e in range(2):
                        ins = pool.tensor_tensor(bias[:, v, e, :].rearrange("p (b r) -> p b r", r=8),
                                                 rpb_runs(pair_, e),
                                                 mask_a[:, v, :].rearrange("p (b r) -> p b r", r=8), ALU.add)
                ins.then_inc(s["bias_done"], 1)

            new_sum(1)
            number = 1
            for st in stages:
                if st.name == "out" or (st.name == "down1"):
                    number += 1
                    if st.name == "out":
                        wait(pool, stage_of["split", st.layer], "h_lo_done", 3)
                    else:
                        wait(pool, stage_of["up1", st.layer], "act_lo", HALF_FF - 1)
                    new_sum(number)
                if st.name == "load":
                    add_squares(st, 0, 8)
                def body(i, st=st):
                    if st.name == "B":
                        rotate(st, i, 0)
                    for k in range(st.per):
                        split_lo(block_at(st, i, k + 2))
                        if k == 1 and st.name == "B0":
                            rotate(st, 0, 0)
                            rotate(st, 0, 1)
                        if k == 0 and st.name == "A0":
                            forward_runs(st.layer)
                            bias_tables(0)
                        if k == 0 and st.name == "A":
                            wait(pool, st, "masked", i)
                            bias_tables(i + 1)
                    if st.name in ("out", "down1"):
                        add_squares(st, i, 2)
                if st.per:
                    passes(pool, st, body)

        @block.tensor
        def _(pe):
            def steps(st, i, k, dst, rhs_hi, rhs_lo, nk, width, first=True, last=True, kc0=0, ready=None):
                b = block_at(st, i, k)[3]
                pe.wait_ge(s_whi, b + 1)
                wait_lo(pe, b)
                slot = st.slots[k]
                for kc in range(nk):
                    if ready:
                        ready(pe, kc)
                    cols = slice(kc * P, kc * P + P)
                    for n, (w, r) in enumerate(((w_hi, rhs_hi), (w_hi, rhs_lo), (w_lo, rhs_hi))):
                        for _, t0, t1 in segs(width):
                            ins = pe.matmul(psum[:, dst * 512 + t0:dst * 512 + t1], w[:, slot, cols],
                                            r[:, kc0 + kc, t0:t1], start=first and kc == 0 and n == 0,
                                            stop=last and kc == nk - 1 and n == 2)
                    if kc == nk - 1:
                        ins.then_inc(s_block, 1)
                    yield

            def project(*args, **kw):
                for _ in steps(*args, **kw):
                    pass

            def together(*parts):
                for _ in zip(*parts):
                    pass
                for part in parts:
                    for _ in part:
                        pass

            def ada_half(st, i, n):
                k = st.pos(f"a{n}")
                b = block_at(st, i, k)[3]
                if n % 2 == 0:
                    wait(pe, st, "ada_rows_copied", i, n // 2)
                pe.wait_ge(s_whi, b + 1)
                wait_lo(pe, b)
                for kk in range(4):
                    for w in (w_hi, w_lo):
                        ins = pe.matmul(bank(4)[0:4, 0:ADA_W], cond4[:, 4 * (n % 2) + kk, :],
                                        w[:, st.slots[k], kk * ADA_W:(kk + 1) * ADA_W],
                                        start=n % 2 == 0 and kk == 0 and w is w_hi,
                                        stop=n % 2 == 1 and kk == 3 and w is w_lo)
                ins.then_inc(s_block, 1)

            def ada_turn(st, i, u):
                wait(pe, st, "ada_rows_copied", i, u + 1)
                wait(pe, st, "ada_cols_added", i, u)
                for j in range(2):
                    ins = pe.matmul(bank(5)[:, 2 * j:2 * j + 2], rows[:, P * j:P * j + P], comb[:, :],
                                    start=True, stop=True)
                ins.then_inc(s["ada_cols_done"], 1)

            sums = {(st.name, st.layer): st.base.get("sq_added", 0) + st.trips * st.counts["sq_added"]
                    for st in stages if "sq_added" in st.counts}
            prime(pe, "ada_cols_done")
            pe.wait_ge(s_const, 16 * CONSTS)
            ld = stage_of["load", 0]
            for l in range(DEPTH):
                pe.transpose(bank(4 + l, P)[:, 0:V_END], vec_rows[0:V_END, l, :],
                             ident[0:V_END, 0:V_END]).then_inc(s_vecT, 1)
            for ch in range(KC):
                if ch >= 2:
                    wait(pe, ld, "x_cols_copied", 0, ch - 1)
                for t in range(TALL // P):
                    ins = pe.transpose(psum[:, 1024 * (ch % 2) + t * P:1024 * (ch % 2) + (t + 1) * P],
                                       tok[:, t, ch * P:(ch + 1) * P], ident[:])
                ins.then_inc(s["x_cols_done"], 1)
            wait(pe, ld, "x_cols_copied", 0)
            pe.wait_ge(s_vec, DEPTH)

            def stage_ada(st):
                pe.wait_ge(s_cond, 4)
                n = st.ada[2]
                for u in range(n):
                    ada_half(st, 0, 2 * u)
                    ada_half(st, 0, 2 * u + 1)
                    if u:
                        ada_turn(st, 0, u - 1)
                ada_turn(st, 0, n - 1)

            def stage_norm(st, width, number):
                if number % 2 == 0:
                    before = "out"
                else:
                    before = "load" if number == 1 else "down1"
                pe.wait_ge(s["sq_added"], sums[before, (number - 1) // 2 if number == 1 else (number - 2) // 2])
                for _, t0, t1 in segs(width):
                    ins = pe.matmul(psum[:, t0:t1], ones[:], ssum[:, t0:t1], start=True, stop=True)
                ins.then_inc(s_sumsq, 1)

            def values_turn(st, i, v_fm_, b):
                for t in range(6):
                    ins = pe.transpose(psum[:, b * 512 + t * P:b * 512 + (t + 1) * P], v_fm_[:, t * P:(t + 1) * P],
                                       ident[:])
                ins.then_inc(s["vt_done"], 1)

            def attention(st, kind, i, ahead=None, tail=None):
                tiles = attention_tiles(kind, st.layer)
                N = len(tiles)

                def scores(n):
                    q0, k0, width, _, _ = tiles[n]
                    for e in range(2):
                        base = score_base(kind, e)
                        rows_ = slice(HD * e, HD * e + HD)
                        if n > 0:
                            wait(pe, st, "exp_done", i, 2 * (n - 1) + e + 1)
                        for first, keys, count in ((BAND_END - width, k0, width), (BAND_END, 640, CTX)):
                            for m, (q, kk) in enumerate(((q_hi, k_hi), (q_hi, k_lo), (q_lo, k_hi))):
                                if count:
                                    ins = pe.matmul(psum[:, base + first:base + first + count],
                                                    q[rows_, q0:q0 + P], kk[rows_, keys:keys + count],
                                                    start=m == 0, stop=m == 2)
                        ins.then_inc(s["scores_done"], 1)

                def fill(part, count):
                    for _ in range(count if part else 0):
                        next(part, None)

                M = N - 1 if kind == "A" else N - 2
                share = [KC * (n + 1) // M - KC * n // M for n in range(M)][::-1]
                share += [0] if kind == "A" else [KC, 0]
                wait_before(pe, st, "q_lo", i)
                wait_before(pe, st, "k_lo", i)
                scores(0)
                if kind == "A":
                    wait_before(pe, st, "v_copied", i)
                    values_turn(st, i, v_fm_a, 0)
                g0 = 0
                for n, tile in enumerate(tiles):
                    if n + 1 < N:
                        scores(n + 1)
                    groups = chunk_groups(tile)
                    if n == 0:
                        wait(pe, st, "v_lo", i) if kind == "A" else wait_total(pe, st, "v_lo")
                    if n == 0:
                        fill(ahead, 1)
                    wait(pe, st, "p_done", i, 2 * n + 2)

                    def turn(g):
                        gg = g0 + g
                        if gg >= 2:
                            wait(pe, st, "pt_lo", i, gg - 1)
                        for m, (_, col) in enumerate(groups[g]):
                            for e in range(2):
                                ins = pe.transpose(
                                    bank(turn_bank(kind, gg))[:, (2 * m + e) * P:(2 * m + e + 1) * P],
                                    probs[:, n % 2, e, col:col + P], ident[:])
                        ins.then_inc(s["pt_done"], 1)

                    def values(g):
                        gg = g0 + g
                        wait(pe, st, "pt_lo", i, gg + 1)
                        if g == 0:
                            wait(pe, st, "o_lo", i, n)
                        for m, (v, _) in enumerate(groups[g]):
                            cols = slice(2 * m * P, 2 * m * P + 2 * P)
                            for w, (vv, pp) in enumerate(((v_hi, pt_hi), (v_hi, pt_lo), (v_lo, pt_hi))):
                                ins = pe.matmul(bank(out_bank(kind, n), 2 * P), vv[:, v * P:(v + 1) * P],
                                                pp[:, gg % 2, cols],
                                                start=g == 0 and m == 0 and w == 0,
                                                stop=g == len(groups) - 1 and m == len(groups[g]) - 1 and w == 2)
                        if g == len(groups) - 1:
                            ins.then_inc(s["o_done"], 1)

                    turn(0)
                    for g in range(len(groups)):
                        if g + 1 < len(groups):
                            turn(g + 1)
                        if g == 0:
                            fill(ahead, share[n] - (n == 0))
                        if n == N - 1:
                            fill(tail, KC // 2 if g == 0 else 2)
                        values(g)
                    if n == N - 1:
                        fill(tail, KC)
                    g0 += len(groups)

            def stage_a0(st):
                width = width_of(st.layer)
                ready = h_ready(stage_of["norm1", st.layer])
                pe.wait_ge(s_ms, 2 * st.layer + 1)
                together(*[steps(st, 0, st.pos(tag), b, h_hi, h_lo, KC, w, ready=ready)
                           for tag, b, w in (("q", 4, width), ("k", 2, TALL), ("v", 0, TALL))])

            def stage_a(st):
                width = width_of(st.layer)

                def body(i):
                    attention(st, "A", i, ahead=steps(st, i, st.pos("q"), 0, h_hi, h_lo, KC, width),
                              tail=steps(st, i, st.pos("k"), 2, h_hi, h_lo, KC, TALL))
                    wait(pe, st, "q_lo", i)
                    project(st, i, st.pos("v"), 0, h_hi, h_lo, KC, TALL)
                passes(pe, st, body)

            def after_merge(name, l):
                merge = stage_of[name, l]
                wait(pe, merge, "mix_done", 7)
                if merge.ada:
                    wait(pe, merge, "ada_cols_added", 7)

            def q_steps(st, i, part):
                t0, t1 = ((0, SEQ), (SEQ, TALL))[part]
                done = part == 1 or width_of(st.layer) == SEQ
                for half in range(2):
                    k = st.pos(f"q{half}")
                    b = block_at(st, i, k)[3]
                    pe.wait_ge(s_whi, b + 1)
                    wait_lo(pe, b)
                    for kc in range(KC // 2):
                        for n, (w, r) in enumerate(((w_hi, h_hi), (w_hi, h_lo), (w_lo, h_hi))):
                            ins = pe.matmul(bank(1 + part, t1 - t0), w[:, st.slots[k], kc * P:kc * P + P],
                                            r[:, KC // 2 * half + kc, t0:t1],
                                            start=half == 0 and kc == 0 and n == 0,
                                            stop=half == 1 and kc == KC // 2 - 1 and n == 2)
                        if done and kc == KC // 2 - 1:
                            ins.then_inc(s_block, 1)
                        elif st.name == "B" and half == 1 and kc == KC // 2 - 1:
                            ins.then_inc(s["q_summed"], 1)
                        yield

            def q_all(st, i):
                yield from q_steps(st, i, 0)
                if width_of(st.layer) == TALL:
                    yield from q_steps(st, i, 1)

            def stage_b0(st):
                after_merge("mergeA", st.layer)
                project(st, 0, st.pos("k"), 2, h_hi, h_lo, KC, TALL)
                for _ in q_steps(st, 0, 0):
                    pass
                if width_of(st.layer) == TALL:
                    wait(pe, st, "k_lo", 0)
                    for _ in q_steps(st, 0, 1):
                        pass
                project(st, 0, st.pos("v"), 4, h_hi, h_lo, KC, TALL)
                wait(pe, st, "v_copied", 0)
                values_turn(st, 0, v_fm, 6)

            def stage_b(st):
                passes(pe, st, lambda i: attention(st, "B", i, ahead=q_all(st, i)))

            def stage_merge(st):
                width = width_of(st.layer)
                kind = st.name[5]
                prev, done = {"A": ("Az", "o_lo"), "B": ("Bz", "o_lo"), "C": ("C", "c_lo")}[kind]
                prev = stage_of[prev, st.layer]
                wait(pe, prev, done, prev.trips - 1)

                def body(i):
                    if st.ada:
                        ada_half(st, i, 0)
                    wait(pe, st, "gate_ready", i, 0)
                    project(st, i, st.pos("z"), 0, h_hi, h_lo, KC, width)
                    if st.ada:
                        ada_half(st, i, 1)
                    wait(pe, st, "mix_done", i, 0)
                    project(st, i, st.pos("m"), 2, br_hi, br_lo, 4, width)
                    if st.ada:
                        ada_turn(st, i, 0)
                passes(pe, st, body)

            def stage_c(st):
                width = width_of(st.layer)
                after_merge("mergeB", st.layer)

                def body(i):
                    wait(pe, st, "c_done", i, 0)
                    for k in range(3):
                        project(st, i, k, 2 * k, h_hi, h_lo, KC, width)
                passes(pe, st, body)

            def stage_out(st):
                width = width_of(st.layer)
                wait(pe, stage_of["mergeC", st.layer], "mix_done", 7)
                ready = h_ready(stage_of["split", st.layer])

                def body(i):
                    for k in range(2):
                        wait(pe, st, "x_updated", i, k - 1)
                        project(st, i, k, 2 * k, h_hi, h_lo, KC, width,
                                ready=ready if isinstance(i, int) and i == 0 and k == 0 else None)
                passes(pe, st, body, first=1)

            def stage_up(st):
                width = width_of(st.layer)
                ready = None
                if st.name == "up0":
                    ready = h_ready(stage_of["norm2", st.layer])
                    pe.wait_ge(s_ms, 2 * st.layer + 2)
                else:
                    wait(pe, stage_of["down0", st.layer], "x_updated", 3)

                def body(i):
                    wait(pe, st, "silu_done", i, 0)
                    if isinstance(i, int) and i == 0 and ready:
                        together(steps(st, i, 0, 0, h_hi, h_lo, KC, width, ready=ready),
                                 steps(st, i, 1, 2, h_hi, h_lo, KC, width, ready=ready))
                        return
                    project(st, i, 0, 0, h_hi, h_lo, KC, width)
                    wait(pe, st, "act_done", i, 0)
                    project(st, i, 1, 2, h_hi, h_lo, KC, width)
                passes(pe, st, body, first=1 if ready else 0)

            def stage_down(st):
                width = width_of(st.layer)
                up = stage_of[f"up{st.name[4]}", st.layer]
                wait(pe, up, "act_lo", up.trips - 1)

                def body(i):
                    for d in range(2):
                        wait(pe, st, "x_updated", i, d - 1)
                        if st.ada:
                            ada_half(st, i, 2 * d)
                        project(st, i, st.pos(f"d{d}"), 2 * d, a_hi, a_lo, KC, width, last=False)
                        if st.ada:
                            ada_half(st, i, 2 * d + 1)
                        project(st, i, st.pos(f"e{d}"), 2 * d, a_hi, a_lo, HALF_FF - KC, width, first=False,
                                kc0=KC)
                        if st.ada:
                            ada_turn(st, i, d)
                passes(pe, st, body)

            pe.wait_ge(s_ones, 1)
            for l in range(DEPTH):
                if l == 0:
                    stage_ada(stage_of["ada", l])
                stage_norm(stage_of["norm1", l], TALL, 2 * l + 1)
                stage_a0(stage_of["A0", l])
                stage_a(stage_of["A", l])
                attention(stage_of["Az", l], "A", 0)
                stage_merge(stage_of["mergeA", l])
                stage_b0(stage_of["B0", l])
                stage_b(stage_of["B", l])
                attention(stage_of["Bz", l], "B", 0)
                stage_merge(stage_of["mergeB", l])
                stage_c(stage_of["C", l])
                stage_merge(stage_of["mergeC", l])
                stage_out(stage_of["out", l])
                stage_norm(stage_of["norm2", l], width_of(l), 2 * l + 2)
                for f in range(2):
                    stage_up(stage_of[f"up{f}", l])
                    stage_down(stage_of[f"down{f}", l])
            stage_norm(stage_of["final", DEPTH - 1], SEQ, 2 * DEPTH + 1)
            for t in range(SEQ // P):
                pe.wait_ge(s_yfm, KC)
                if t >= 2:
                    pe.wait_ge(s_ytok, t - 1)
                for ch in range(KC):
                    ins = pe.transpose(psum[:, 1024 * (1 + t % 2) + ch * P:1024 * (1 + t % 2) + (ch + 1) * P],
                                       y_fm[:, ch, t * P:(t + 1) * P], ident[:])
                ins.then_inc(s_yT, 1)

        @block.scalar
        def _(act):
            prime(act, "ada_rows_copied", "gate_ready", "silu_done")

            def split_hi(blk):
                if blk is None:
                    return
                st, i, k, b = blk
                slot, w = st.slots[k], block_width(st, k)
                act.wait_ge(s_load[slot], load_value(st, i, k))
                last = b - slot_distance(blk)
                if not (isinstance(last, int) and last < 0):
                    act.wait_ge(s_block, last + 1)
                act.activation(w_hi[:, slot, 0:w], w_raw[:, slot, 0:w], ACT.Identity).then_inc(s_whi, 1)

            def copy(dst, src, scale=1.0):
                return act.activation(dst, src, ACT.Identity, scale=scale)

            warmed = [0]

            def warm(function):
                n = warmed[0]
                warmed[0] += 1
                act.activation(warm_sb[:, n:n + 1], ones[:, 0:1], function)

            def ada_rows(st, i, u):
                wait_block(act, st, i, st.pos(f"a{2 * u + 1}"))
                wait(act, st, "ada_cols_done", i, u)
                copy(rows[:, :], bank(4)[0:4, 0:ADA_W]).then_inc(s["ada_rows_copied"], 1)

            first = stage_of["ada", 0]
            act.wait_ge(s_ones, 1)
            split_hi(block_at(first, 0, 0))
            split_hi(block_at(first, 0, 1))
            split_hi(block_at(first, 0, 2))

            act.wait_ge(s_vec, DEPTH)
            act.activation(cond[:, :, 0], vec[:, 0, V_C:V_C + KC], ACT.Silu).then_inc(s_cond, 1)
            act.activation(cond[:, :, 1], vec[:, 0, V_CC:V_CC + KC], ACT.Silu).then_inc(s_cond, 1)
            act.wait_ge(s_cond, 2)
            copy(cond4[:, :, 0:4:2], cond[:]).then_inc(s_cond, 1)

            def squares(st, i, n, ready):
                w = TALL if st.name == "load" else width_of(st.layer)
                for k in range(n):
                    wait(act, st, "sq_added", i, k - 1)
                    wait(act, st, ready, i, k + 1)
                    act.activation(sq[:, k % 2, 0:w], x_chunk(i, k, n)[:, 0:w], ACT.Square)\
                       .then_inc(s["sq_ready"], 1)

            def stage_ada(st):
                load_st = stage_of["load", 0]
                for u in range(st.ada[2]):
                    split_hi(block_at(st, 0, 2 * u + 3))
                    wait(act, load_st, "sq_added", 0, u - 1)
                    wait(act, load_st, "x_cols_copied", 0, u + 1)
                    act.activation(sq[:, u % 2, :], x_t[:, u, :], ACT.Square).then_inc(s["sq_ready"], 1)
                    ada_rows(st, 0, u)
                    if 2 * u + 4 < st.per + 2:
                        split_hi(block_at(st, 0, 2 * u + 4))

            def root(width, number):
                act.wait_ge(s_sumsq, number)
                act.activation(rstd[:, 0:width], psum[:, 0:width], ACT.Sqrt, scale=1.0 / D_MODEL,
                               bias=eps[:, 0:1]).then_inc(s_rstd, 1)

            def stage_norm(st, width, number, shift):
                root(width, number)

                def body(i):
                    for k in range(2):
                        wait(act, st, "normed", i, k + 1)
                        for e, t0, t1 in segs(width):
                            ins = act.activation(chunk(h_hi, i, k)[:, t0:t1], normed_t[:, k, t0:t1], ACT.Identity,
                                                 bias=ada_col(st.layer, e, shift, i, k))
                        ins.then_inc(s["h_hi_done"], 1)
                passes(act, st, body)

            def qk_hi(pieces, name, scale):
                for dst, src in pieces:
                    ins = copy(dst, src, scale)
                ins.then_inc(s[name], 1)

            def values_hi(st, i, b):
                wait(act, st, "vt_done", i)
                copy(v_hi[:], psum[:, b * 512:b * 512 + TALL]).then_inc(s["v_hi"], 1)

            def attention(st, kind, i, first_done=None, before_last=None, before_two=None):
                tiles = attention_tiles(kind, st.layer)

                def exps(n, e):
                    if n >= len(tiles):
                        return
                    wait(act, st, "max_done", i, 2 * n + e + 1)
                    c0, c1 = BAND_END - tiles[n][2], SINK + (kind == "B")
                    act.activation(probs[:, n % 2, e, c0 - BAND0:c1 - BAND0],
                                   psum[:, score_base(kind, e) + c0:score_base(kind, e) + c1], ACT.Exp,
                                   bias=nmax[:, n % 2, e:e + 1],
                                   accum_out=rsum[:, n % 2, e:e + 1]).then_inc(s["exp_done"], 1)

                exps(0, 0)
                if kind == "A":
                    values_hi(st, i, 0)
                exps(0, 1)
                g0 = 0
                for n, tile in enumerate(tiles):
                    groups = chunk_groups(tile)

                    def turned(g):
                        wait(act, st, "pt_done", i, g0 + g + 1)
                        w = 2 * P * len(groups[g])
                        copy(pt_hi[:, (g0 + g) % 2, 0:w], bank(turn_bank(kind, g0 + g), w)).then_inc(s["pt_hi"], 1)

                    if n == len(tiles) - 1 and before_last:
                        before_last()
                    if n == len(tiles) - 2 and before_two:
                        before_two()
                    turned(0)
                    exps(n + 1, 0)
                    if len(groups) > 1:
                        turned(1)
                    exps(n + 1, 1)
                    if len(groups) > 2:
                        turned(2)
                    g0 += len(groups)
                    wait(act, st, "o_done", i, n + 1)
                    for dst, src in out_pieces(br_hi, kind, pair_of(st, i), n, tile[0]):
                        ins = copy(dst, src)
                    ins.then_inc(s["o_hi"], 1)
                    if n == 0 and first_done:
                        first_done()

            def v_out(st, i):
                wait_block(act, st, i, st.pos("v"))
                for dst, src in v_pieces_a():
                    ins = copy(dst, src)
                ins.then_inc(s["v_copied"], 1)

            def stage_a0(st):
                wait(act, stage_of["norm1", st.layer], "h_lo_done", 3)
                wait_block(act, st, 0, st.pos("q"))
                qk_hi(q_pieces_a(q_hi, width_of(st.layer), 4), "q_hi", QSCALE)
                wait_block(act, st, 0, st.pos("k"))
                qk_hi(k_pieces_a(k_hi), "k_hi", 1.0)
                v_out(st, 0)
                split_hi(block_at(st, 0, 3))
                split_hi(block_at(st, 0, 4))

            def stage_a(st):
                width = width_of(st.layer)

                def body(i):
                    def next_q():
                        wait_block(act, st, i, st.pos("q"))
                        qk_hi(q_pieces_a(q_hi, width, 0), "q_hi", QSCALE)

                    attention(st, "A", i, lambda: split_hi(block_at(st, i, 2)), next_q)
                    wait_block(act, st, i, st.pos("k"))
                    qk_hi(k_pieces_a(k_hi), "k_hi", 1.0)
                    split_hi(block_at(st, i, 3))
                    v_out(st, i)
                    split_hi(block_at(st, i, 4))
                warm(ACT.Exp)
                passes(act, st, body)

            def swap_halves(src):
                for e in range(2):
                    for half in range(2):
                        to, frm = HD * e + 32 * half, HD * e + 32 * (1 - half)
                        ins = copy(swap[to:to + 32, :], src[frm:frm + 32, 0:SEQ])
                ins.then_inc(s["swapped"], 1)

            def stage_b0(st):
                wait(act, stage_of["mergeA", st.layer], "mix_done", 7)
                split_hi(block_at(st, 0, 2))
                wait_block(act, st, 0, st.pos("k"))
                swap_halves(bank(2))
                split_hi(block_at(st, 0, 3))
                wait(act, st, "rotated", 0, 1)
                qk_hi([(k_hi[:, 0:SEQ], rc[:]), (k_hi[:, 640:640 + CTX], bank(3, CTX))], "k_hi", 1.0)
                wait_block(act, st, 0, st.pos("q1"))
                swap_halves(bank(1))
                split_hi(block_at(st, 0, 4))
                wait(act, st, "rotated", 0, 2)
                qk_hi(q_pieces_b(q_hi, st.layer), "q_hi", QSCALE)
                split_hi(block_at(st, 0, 5))
                wait_block(act, st, 0, st.pos("v"))
                copy(v_fm[:, :], psum[:, 2048:2048 + TALL]).then_inc(s["v_copied"], 1)
                values_hi(st, 0, 6)

            def stage_b(st):
                def body(i):
                    def turn_q():
                        if st.layer:
                            wait_block(act, st, i, st.pos("q1"))
                        else:
                            wait(act, st, "q_summed", i)
                        swap_halves(bank(1))

                    def next_q():
                        wait(act, st, "rotated", i)
                        wait_block(act, st, i, st.pos("q1"))
                        qk_hi(q_pieces_b(q_hi, st.layer), "q_hi", QSCALE)

                    attention(st, "B", i, None, next_q, turn_q)
                    split_hi(block_at(st, i, 2))
                    split_hi(block_at(st, i, 3))
                warm(ACT.Exp)
                passes(act, st, body)

            def stage_merge(st):
                width = width_of(st.layer)
                number = "ABC".index(st.name[5])

                def body(i):
                    if st.ada:
                        split_hi(block_at(st, i, 2))
                        split_hi(block_at(st, i, 3))
                    else:
                        split_hi(block_at(st, i, 2))
                    wait_block(act, st, i, st.pos("z"))
                    wait(act, st, "mix_done", i, 0)
                    act.activation(gate[:, 0:width], psum[:, 0:width], ACT.Sigmoid,
                                   bias=vec_col(st.layer, V_BGATE + KC * number, i)).then_inc(s["gate_ready"], 1)
                    if st.ada:
                        split_hi(block_at(st, i, 4))
                        ada_rows(st, i, 0)
                        split_hi(block_at(st, i, 5))
                    else:
                        split_hi(block_at(st, i, 3))
                warm(ACT.Sigmoid)
                passes(act, st, body)

            def stage_c(st):
                width = width_of(st.layer)
                wait(act, stage_of["mergeB", st.layer], "mixed", 7)

                def body(i):
                    split_hi(block_at(st, i, 2))
                    wait_block(act, st, i, 0)
                    wait(act, st, "u_done", i, 0)
                    copy(cx_sb[:, 0:width], psum[:, 0:width]).then_inc(s["cx_copied"], 1)
                    split_hi(block_at(st, i, 3))
                    split_hi(block_at(st, i, 4))
                    wait(act, st, "c_done", i)
                    copy(pair(br_hi, i)[:, 0:width], c_out[:, 0:width]).then_inc(s["c_hi"], 1)
                passes(act, st, body)

            def stage_split(st):
                width = width_of(st.layer)
                wait(act, stage_of["mergeC", st.layer], "mixed", 7)

                def body(i):
                    for k in range(2):
                        copy(chunk(h_hi, i, k)[:, 0:width], chunk(merged, i, k)[:, 0:width])\
                            .then_inc(s["h_hi_done"], 1)
                passes(act, st, body)

            def stage_tiles(st):
                def body(i):
                    half = st.per // 2
                    for k in range(st.per):
                        split_hi(block_at(st, i, k + 2))
                        if st.ada and st.tags[k][0] == "a" and int(st.tags[k][1:]) % 2:
                            ada_rows(st, i, int(st.tags[k][1:]) // 2)
                    if "sq_ready" in st.counts:
                        squares(st, i, 2, "x_updated")
                passes(act, st, body)

            def stage_up(st):
                width = width_of(st.layer)

                warm(ACT.Silu)

                def body(i):
                    split_hi(block_at(st, i, 2))
                    wait_block(act, st, i, 0)
                    wait(act, st, "act_done", i, 0)
                    act.activation(silu_sb[:, 0:width], psum[:, 0:width], ACT.Silu).then_inc(s["silu_done"], 1)
                    split_hi(block_at(st, i, 3))
                    wait(act, st, "act_done", i)
                    copy(tile_of(a_hi, i)[:, 0:width], act_sb[:, 0:width]).then_inc(s["act_hi"], 1)
                passes(act, st, body)

            stage_ada(stage_of["ada", 0])
            for l in range(DEPTH):
                split_hi(block_at(stage_of["A0", l], 0, 2))
                stage_norm(stage_of["norm1", l], TALL, 2 * l + 1, SH1)
                stage_a0(stage_of["A0", l])
                stage_a(stage_of["A", l])
                attention(stage_of["Az", l], "A", 0)
                stage_merge(stage_of["mergeA", l])
                stage_b0(stage_of["B0", l])
                stage_b(stage_of["B", l])
                attention(stage_of["Bz", l], "B", 0)
                stage_merge(stage_of["mergeB", l])
                stage_c(stage_of["C", l])
                stage_merge(stage_of["mergeC", l])
                stage_split(stage_of["split", l])
                stage_tiles(stage_of["out", l])
                stage_norm(stage_of["norm2", l], width_of(l), 2 * l + 2, SH2)
                for f in range(2):
                    stage_up(stage_of[f"up{f}", l])
                    stage_tiles(stage_of[f"down{f}", l])
            root(SEQ, 2 * DEPTH + 1)
            for t in range(SEQ // P):
                act.wait_ge(s_yT, t + 1)
                if t >= 2:
                    act.wait_ge(s_out[t % 2], 16 * (t // 2))
                copy(y_tok[:, t % 2, :], psum[:, 1024 * (1 + t % 2):1024 * (2 + t % 2)]).then_inc(s_ytok, 1)

        @block.vector
        def _(dve):
            prime(dve, "ada_cols_added", "masked", "o_lo", "mix_done", "mixed", "u_done", "c_done", "x_updated",
                  "act_done", "h_lo_done", "c_lo", "act_lo")

            def rest(dst, src, hi, scale=1.0):
                return dve.scalar_tensor_tensor(dst, src, scale, hi.bitcast(F32), ALU.mult, ALU.subtract)

            for l in range(DEPTH):
                dve.wait_ge(s_vecT, l + 1)
                dve.tensor_copy(vec[:, l, 0:V_END], bank(4 + l, V_END)).then_inc(s_vec, 1)
            ld = stage_of["load", 0]
            for ch in range(KC):
                wait(dve, ld, "x_cols_done", 0, ch + 1)
                dve.tensor_copy(x_t[:, ch, :], psum[:, 1024 * (ch % 2):1024 * (ch % 2) + TALL])\
                   .then_inc(s["x_cols_copied"], 1)
            def split_lo(b):
                st, i, k = blocks[b]
                slot = st.slots[k]
                dve.wait_ge(s_whi, b + 1)
                last = b - distance[b]
                if last >= 0:
                    dve.wait_ge(s_block, last + 1)
                dve.tensor_tensor(w_lo[:, slot, :], w_raw[:, slot, :], w_hi[:, slot, :].bitcast(F32),
                                  ALU.subtract).then_inc(s_wlov, 1)

            def ada_cols(st, i, u):
                al, first, n = st.ada
                wait(dve, st, "ada_cols_done", i, u + 1)
                ada_v = ada[:, al, :, 2 * first:48].rearrange("p s (g j) -> p s g j", j=2)
                add_v = vec[:, al, V_BADA + 2 * first:V_BADA + 48].rearrange("p (g j) -> p g j", j=2)
                g = i * n + u
                for e in range(2):
                    ins = dve.tensor_tensor(ada_v[:, e, g, :], bank(5, 4)[:, e:4:2], add_v[:, g, :], ALU.add)
                ins.then_inc(s["ada_cols_added"], 1)

            dve.wait_ge(s_cond, 3)
            dve.tensor_tensor(cond4[:, :, 1:4:2], cond[:], cond4[:, :, 0:4:2].bitcast(F32), ALU.subtract)\
               .then_inc(s_cond, 1)

            def stage_ada(st):
                for u in range(st.ada[2]):
                    split_lo(2 * u)
                    split_lo(2 * u + 1)
                    if u:
                        ada_cols(st, 0, u - 1)
                ada_cols(st, 0, st.ada[2] - 1)

            def modulation(st, which, scale, g, number):
                wait_total(dve, st, "ada_cols_added")
                for e in range(2):
                    ins = dve.scalar_tensor_tensor(a_mod[:, which, e, :],
                                                   ada[:, st.layer, e, KC * scale:KC * scale + KC], 1.0,
                                                   vec[:, st.layer, g:g + KC], ALU.add, ALU.mult)
                ins.then_inc(s_mod, 1)
                dve.wait_ge(s_mod, number)

            def inverse(width, number):
                dve.wait_ge(s_rstd, number)
                dve.reciprocal(rstd[:, 0:width], rstd[:, 0:width]).then_inc(s_ms, 1)
                dve.wait_ge(s_ms, number)

            def stage_norm(st, width, number, which, shift):
                modulation(st, which, (SC1, SC2)[which], (V_N1, V_N2)[which], number)
                inverse(width, number)

                def body(i):
                    for k in range(2):
                        wait(dve, st, "h_lo_done", i, k - 1)
                        for e, t0, t1 in segs(width):
                            ins = dve.scalar_tensor_tensor(normed_t[:, k, t0:t1], chunk(x_t, i, k)[:, t0:t1],
                                                           mod_col(which, e, i, k), rstd[:, t0:t1], ALU.mult,
                                                           ALU.mult)
                        ins.then_inc(s["normed"], 1)
                    for k in range(2):
                        wait(dve, st, "h_hi_done", i, k + 1)
                        for e, t0, t1 in segs(width):
                            ins = dve.scalar_tensor_tensor(chunk(h_lo, i, k)[:, t0:t1], normed_t[:, k, t0:t1],
                                                           ada_col(st.layer, e, shift, i, k),
                                                           chunk(h_hi, i, k)[:, t0:t1].bitcast(F32), ALU.add,
                                                           ALU.subtract)
                        ins.then_inc(s["h_lo_done"], 1)
                passes(dve, st, body)

            def qk_lo(st, i, his, pieces, name, scale):
                wait(dve, st, name + "_hi", i)
                for (dst, src), (hi, _) in zip(pieces, his):
                    ins = rest(dst, src, hi, scale)
                ins.then_inc(s[name + "_lo"], 1)

            def values_lo(st, i, b):
                wait(dve, st, "v_hi", i)
                rest(v_lo[:], psum[:, b * 512:b * 512 + TALL], v_hi[:]).then_inc(s["v_lo"], 1)

            def attention(st, kind, i, before_last=None, before_two=None):
                tiles = attention_tiles(kind, st.layer)
                marks = [0]

                def front(n, e):
                    if n >= len(tiles):
                        return
                    q0, _, width, band, variant = tiles[n]
                    base = score_base(kind, e)
                    wait(dve, st, "scores_done", i, 2 * n + e + 1)
                    if kind == "B" and n == 0:
                        dve.tensor_copy(psum[:, base + SINK:base + SINK + 1], sink_col(st.layer, e, pair_of(st, i)))\
                           .then_inc(s["sunk"], 1)
                        wait(dve, st, "sunk", i, e + 1)
                    if width:
                        if kind == "A":
                            at_ = psum[:, base + BAND_END - width:base + BAND_END]
                            by = bias[:, variant, e, :]
                        elif q0 == 0:
                            at_, by = psum[:, base + 3 * P:base + 4 * P], mask_b[:, 1, :]
                        elif q0 == SEQ - P:
                            at_, by = psum[:, base + 2 * P:base + 3 * P], mask_b[:, 0, :]
                        else:
                            at_ = psum[:, base + P:base + 5 * P].rearrange("p (a b) -> p a b", b=2 * P)[:, :, 0:P]
                            by = mask_b[:, :, :]
                        dve.tensor_tensor(at_, at_, by, ALU.add).then_inc(s["masked"], 1)
                        wait(dve, st, "masked", i, 2 * n + e + 1)
                    c0, c1 = BAND_END - width, SINK + (kind == "B")
                    dve.tensor_reduce(nmax[:, n % 2, e:e + 1], psum[:, base + c0:base + c1], AX.X, ALU.max,
                                      negate=True).then_inc(s["max_done"], 1)

                def normalise(n):
                    for e in range(2):
                        wait(dve, st, "exp_done", i, 2 * n + e + 1)
                        dve.reciprocal(rinv[:, n % 2, e:e + 1], rsum[:, n % 2, e:e + 1]).then_inc(s["inv_done"], 1)
                    for e in range(2):
                        wait(dve, st, "inv_done", i, 2 * n + e + 1)
                        c0 = BAND_END - tiles[n][2] - BAND0
                        part = probs[:, n % 2, e, c0:CTX_END - BAND0]
                        dve.tensor_scalar(part, part, rinv[:, n % 2, e:e + 1], None, ALU.mult)\
                           .then_inc(s["p_done"], 1)

                if kind == "A":
                    wait_before(dve, st, "bias_done", i)
                front(0, 0)
                front(0, 1)
                if kind == "A":
                    values_lo(st, i, 0)
                normalise(0)
                g0 = 0
                for n, tile in enumerate(tiles):
                    groups = chunk_groups(tile)

                    def turned(g):
                        wait(dve, st, "pt_hi", i, g0 + g + 1)
                        par, w = (g0 + g) % 2, 2 * P * len(groups[g])
                        rest(pt_lo[:, par, 0:w], bank(turn_bank(kind, par), w), pt_hi[:, par, 0:w]).then_inc(s["pt_lo"], 1)

                    if n == len(tiles) - 1 and before_last:
                        before_last()
                    if n == len(tiles) - 2 and before_two:
                        before_two()
                    front(n + 1, 0)
                    turned(0)
                    front(n + 1, 1)
                    for g in range(1, len(groups)):
                        turned(g)
                    g0 += len(groups)
                    if n + 1 < len(tiles):
                        normalise(n + 1)
                    wait(dve, st, "o_hi", i, n + 1)
                    for (dst, src), (hi, _) in zip(out_pieces(br_lo, kind, pair_of(st, i), n, tile[0]),
                                                   out_pieces(br_hi, kind, pair_of(st, i), n, tile[0])):
                        ins = rest(dst, src, hi)
                    ins.then_inc(s["o_lo"], 1)

            def stage_a0(st):
                width = width_of(st.layer)
                qk_lo(st, 0, q_pieces_a(q_hi, width, 4), q_pieces_a(q_lo, width, 4), "q", QSCALE)
                qk_lo(st, 0, k_pieces_a(k_hi), k_pieces_a(k_lo), "k", 1.0)

            def stage_a(st):
                width = width_of(st.layer)

                def body(i):
                    attention(st, "A", i, lambda: qk_lo(st, i, q_pieces_a(q_hi, width, 0),
                                                        q_pieces_a(q_lo, width, 0), "q", QSCALE))
                    qk_lo(st, i, k_pieces_a(k_hi), k_pieces_a(k_lo), "k", 1.0)
                passes(dve, st, body)

            def rotate(st, i, n, src):
                wait(dve, st, "swapped", i, n + 1)
                dve.tensor_tensor(rc[:], src, rope[:, 0, :], ALU.mult).then_inc(s["rope_cos"], 1)

            def stage_b0(st):
                rotate(st, 0, 0, bank(2))
                qk_lo(st, 0, [(k_hi[:, 0:SEQ], None), (k_hi[:, 640:640 + CTX], None)],
                      [(k_lo[:, 0:SEQ], rc[:]), (k_lo[:, 640:640 + CTX], bank(3, CTX))], "k", 1.0)
                wait(dve, st, "k_lo", 0)
                rotate(st, 0, 1, bank(1))
                qk_lo(st, 0, q_pieces_b(q_hi, st.layer), q_pieces_b(q_lo, st.layer), "q", QSCALE)
                values_lo(st, 0, 6)

            def stage_b(st):
                def body(i):
                    attention(st, "B", i, lambda: qk_lo(st, i, q_pieces_b(q_hi, st.layer),
                                                        q_pieces_b(q_lo, st.layer), "q", QSCALE),
                              lambda: rotate(st, i, 0, bank(1)))
                passes(dve, st, body)

            def stage_merge(st):
                width = width_of(st.layer)

                def body(i):
                    wait_block(dve, st, i, st.pos("m"))
                    wait(dve, st, "gate_ready", i)
                    m = tile_of(merged, i)[:, 0:width]
                    if st.name == "mergeA":
                        dve.tensor_tensor(m, psum[:, 1024:1024 + width], gate[:, 0:width], ALU.mult)\
                           .then_inc(s["mix_done"], 1)
                    else:
                        wait(dve, st, "mixed", i, 0)
                        dve.tensor_tensor(mix[:, 0:width], psum[:, 1024:1024 + width], gate[:, 0:width], ALU.mult)\
                           .then_inc(s["mix_done"], 1)
                        wait(dve, st, "mix_done", i)
                        dve.tensor_tensor(m, m, mix[:, 0:width], ALU.add).then_inc(s["mixed"], 1)
                    if st.ada:
                        ada_cols(st, i, 0)
                passes(dve, st, body)

            def stage_c(st):
                width = width_of(st.layer)
                span = width + (2 if width == TALL else 0)

                def body(i):
                    wait_block(dve, st, i, 1)
                    wait(dve, st, "cx_copied", i)
                    for e, t0, t1 in segs(width):
                        ins = dve.tensor_tensor(u_pad[:, t0 + 1 + 2 * e:t1 + 1 + 2 * e], psum[:, 1024 + t0:1024 + t1],
                                                cx_sb[:, t0:t1], ALU.mult)
                    ins.then_inc(s["u_done"], 1)
                    wait(dve, st, "u_done", i)
                    dve.tensor_scalar(y_a[:, 0:span], u_pad[:, 1:span + 1], vec_col(st.layer, V_CONV + 4, i), None,
                                      ALU.mult).then_inc(s["y_step"], 1)
                    wait(dve, st, "y_step", i, 1)
                    dve.scalar_tensor_tensor(y_b[:, 0:span], u_pad[:, 0:span], vec_col(st.layer, V_CONV, i),
                                             y_a[:, 0:span], ALU.mult, ALU.add).then_inc(s["y_step"], 1)
                    wait(dve, st, "y_step", i, 2)
                    dve.scalar_tensor_tensor(y_a[:, 0:span], u_pad[:, 2:span + 2], vec_col(st.layer, V_CONV + 8, i),
                                             y_b[:, 0:span], ALU.mult, ALU.add).then_inc(s["y_step"], 1)
                    wait(dve, st, "y_step", i, 3)
                    wait_block(dve, st, i, 2)
                    wait(dve, st, "c_lo", i, 0)
                    for e, t0, t1 in segs(width):
                        ins = dve.tensor_tensor(c_out[:, t0:t1], psum[:, 2048 + t0:2048 + t1],
                                                y_a[:, t0 + 2 * e:t1 + 2 * e], ALU.mult)
                    ins.then_inc(s["c_done"], 1)
                    wait(dve, st, "c_hi", i)
                    rest(pair(br_lo, i)[:, 0:width], c_out[:, 0:width], pair(br_hi, i)[:, 0:width])\
                        .then_inc(s["c_lo"], 1)

                wait(dve, stage_of["mergeB", st.layer], "mixed", 7)
                dve.memset(u_pad[:, 0:1], 0.0)
                dve.memset(u_pad[:, SEQ + 1:SEQ + 3], 0.0)
                dve.memset(u_pad[:, TALL + 3:TALL + 4], 0.0).then_inc(s_zero, 1)
                dve.wait_ge(s_zero, st.layer + 1)
                passes(dve, st, body)

            def stage_split(st):
                width = width_of(st.layer)
                wait(dve, stage_of["mergeC", st.layer], "mixed", 7)

                def body(i):
                    for k in range(2):
                        wait(dve, st, "h_hi_done", i, k + 1)
                        rest(chunk(h_lo, i, k)[:, 0:width], chunk(merged, i, k)[:, 0:width],
                             chunk(h_hi, i, k)[:, 0:width]).then_inc(s["h_lo_done"], 1)
                passes(dve, st, body)

            def stage_residual(st, piece, last_blocks):
                width = width_of(st.layer)

                def body(i):
                    for k in range(2):
                        wait_block(dve, st, i, st.pos(last_blocks[k]))
                        for e, t0, t1 in segs(width):
                            xs = chunk(x_t, i, k)[:, t0:t1]
                            ins = dve.scalar_tensor_tensor(xs, psum[:, 1024 * k + t0:1024 * k + t1],
                                                           ada_col(st.layer, e, piece, i, k), xs, ALU.mult, ALU.add)
                        ins.then_inc(s["x_updated"], 1)
                        if st.ada:
                            ada_cols(st, i, k)
                passes(dve, st, body)

            def stage_up(st):
                width = width_of(st.layer)

                def body(i):
                    wait_block(dve, st, i, 1)
                    wait(dve, st, "silu_done", i)
                    wait(dve, st, "act_lo", i, 0)
                    dve.tensor_tensor(act_sb[:, 0:width], psum[:, 1024:1024 + width], silu_sb[:, 0:width], ALU.mult)\
                       .then_inc(s["act_done"], 1)
                    wait(dve, st, "act_hi", i)
                    rest(tile_of(a_lo, i)[:, 0:width], act_sb[:, 0:width], tile_of(a_hi, i)[:, 0:width])\
                        .then_inc(s["act_lo"], 1)
                passes(dve, st, body)

            stage_ada(stage_of["ada", 0])
            for l in range(DEPTH):
                stage_norm(stage_of["norm1", l], TALL, 2 * l + 1, 0, SH1)
                stage_a0(stage_of["A0", l])
                stage_a(stage_of["A", l])
                attention(stage_of["Az", l], "A", 0)
                stage_merge(stage_of["mergeA", l])
                stage_b0(stage_of["B0", l])
                stage_b(stage_of["B", l])
                attention(stage_of["Bz", l], "B", 0)
                stage_merge(stage_of["mergeB", l])
                stage_c(stage_of["C", l])
                stage_merge(stage_of["mergeC", l])
                stage_split(stage_of["split", l])
                stage_residual(stage_of["out", l], G1, ("o0", "o1"))
                stage_norm(stage_of["norm2", l], width_of(l), 2 * l + 2, 1, SH2)
                for f in range(2):
                    stage_up(stage_of[f"up{f}", l])
                    wait(dve, stage_of[f"up{f}", l], "act_lo", HALF_FF - 1)
                    stage_residual(stage_of[f"down{f}", l], G2, ("e0", "e1"))
            inverse(SEQ, 2 * DEPTH + 1)
            for ch in range(KC):
                dve.scalar_tensor_tensor(y_fm[:, ch, :], x_t[:, ch, 0:SEQ], vec[:, 0, V_FINAL + ch:V_FINAL + ch + 1],
                                         rstd[:, 0:SEQ], ALU.mult, ALU.mult).then_inc(s_yfm, 1)


_INS = ["x", "c", "ctx", "c_ctx", "w_ada", "b_ada", "norm1_g", "norm2_g", "w_in", "b_gate", "na_rpb", "sw_sink",
        "conv_w", "w_br_a", "w_br_b", "w_br_c", "w_o", "w_ffn_up", "w_ffn_down", "final_norm_g"]


def shape_constants():
    import numpy as np

    ident = np.eye(P, dtype=np.float32)
    a = np.arange(P)[:, None] // ROWS
    b = np.arange(2 * P)[None, :] // ROWS
    starts = [np.maximum(a, 8), a, np.minimum(a, 8)]
    masks_a = np.stack([np.where((b >= st) & (b < st + WIN_COLS), 0.0, NEG) for st in starts], 1)
    q, k = np.arange(P)[:, None], np.arange(P)[None, :]
    masks_b = np.stack([np.where(k >= q, 0.0, NEG), np.where(k <= q, 0.0, NEG)], 1)
    t = np.arange(SEQ)
    inv = np.float32(ROPE_THETA) ** (-np.arange(HD // 4, dtype=np.float32) / np.float32(HD // 4))
    ang = np.concatenate([(t // GRID_W).astype(np.float32)[:, None] * inv,
                          (t % GRID_W).astype(np.float32)[:, None] * inv], -1)
    f = np.arange(P) % HD
    cos = np.cos(ang).T[f % 32]
    sin = np.sin(ang).T[f % 32] * np.where(f < 32, -1.0, 1.0)[:, None]
    comb = np.array([[1, 0], [1, 0], [0, 1], [0, 1]])
    return {"ident": ident, "masks_a": masks_a.astype(np.float32), "masks_b": masks_b.astype(np.float32),
            "rope": np.stack([cos, sin], 1).astype(np.float32), "comb": comb.astype(np.float32)}


def kernel(**inputs):
    import numpy as np
    import concourse.bacc as bacc
    from concourse.bass_utils import run_bass_kernel_spmd as run

    nc = bacc.Bacc("TRN2", target_bir_lowering=False, num_devices=1)
    arrays, args = {}, []

    def give(name, a):
        a = np.ascontiguousarray(a)
        arrays[f"in_{name}"] = a
        args.append(nc.dram_tensor(f"in_{name}", a.shape, mybir.dt.from_np(a.dtype), kind="ExternalInput").ap())

    for name in _INS:
        a = np.asarray(inputs[name])
        if name == "na_rpb":
            edge = np.zeros(RPB_PAD, a.dtype)
            a = np.concatenate([edge, a[:, :, ::-1, ::-1].reshape(-1), edge])
        give(name, a)
    for name, a in shape_constants().items():
        give(name, a)
    out = nc.dram_tensor("out_0", (1, SEQ, D_MODEL), F32, kind="ExternalOutput").ap()
    build(nc, *args, out)
    r = run(nc, [arrays], core_ids=[0])
    return r.results[0]["out_0"]
```

```python
from contextlib import ExitStack

import concourse.bass as bass
from concourse import mybir

F32 = mybir.dt.float32
F32R = mybir.dt.float32r
ALU = mybir.AluOpType
ACT = mybir.ActivationFunctionType
AX = mybir.AxisListType

P = 128
D_MODEL = 1024
KC = D_MODEL // P
SEQ = 512
CTX = 256
TALL = SEQ + CTX
DEPTH = 2
GRID_W = 64
ROWS = SEQ // GRID_W
HD = 64
NA_HEADS = 8
WIN_ROWS, WIN_COLS = 8, 16
RPB = (2 * WIN_ROWS - 1) * (2 * WIN_COLS - 1)
RPB_W = 2 * WIN_COLS - 1
SW_HEADS = 8
PAIRS = 4
ADA_W = 256
RING = 3
SLOTS = 9
ADA_FIRST = 2 * D_MODEL // ADA_W
BR = 512
D_FF = 2816
HALF_FF = D_FF // P // 2
DOWN_D = 6
SPLIT_EARLY = 3
MERGE_Z = 6
EPS = 1e-6
ROPE_THETA = 10000.0
NEG = -1e30
QSCALE = HD ** -0.5
RPB_PAD = 8
SEG = (WIN_ROWS - 1) * RPB_W + 32

CT_QA, CT_KA, CT_VA, CT_QB, CT_KB, CT_VB, CT_X, CT_GB, CT_GC, CT_ZG = 0, 4, 8, 12, 16, 17, 18, 22, 26, 30
V_BADA, V_N1, V_N2, V_BGATE, V_CONV, V_FINAL, V_C, V_CC, V_END = 0, 48, 56, 64, 88, 100, 108, 116, 124
SH1, SC1, G1, SH2, SC2, G2 = range(6)

BAND0, BAND_END, CTX_END, SINK = 128, 512, 768, 768


class Stage:

    def __init__(self, name, layer, trips, blocks, ada, counts):
        self.name, self.layer, self.trips = name, layer, trips
        self.tags = [tag for tag, _ in blocks]
        self.slots = [slot for _, slot in blocks]
        self.dmas = [{"q0": 2, "q1": 2, "m": 3 if name == "mergeB" else 2}.get(tag, 1) for tag in self.tags]
        self.per = len(blocks)
        self.ada = ada
        self.counts = counts
        self.base = {}

    def pos(self, tag):
        return self.tags.index(tag)


PRIMED = dict(ada_rows_copied=1, ada_cols_done=1, ada_cols_added=1, sq_added=2, bias_done=1, masked=1, o_lo=1,
              gate_ready=1, mix_done=1, mixed=1, u_done=1, c_done=1, x_updated=2, silu_done=1, act_done=1,
              h_lo_done=2, c_lo=1, act_lo=1)


def attention_tiles(kind, layer):
    tiles = []
    for j in range(SEQ // P):
        if kind == "A":
            tiles.append((P * j, P * j, 2 * P, [j, (j + 1) % 4], 0 if j == 0 else (2 if j == 3 else 1)))
        else:
            lo, hi = max(0, j - 1), min(3, j + 1)
            tiles.append((P * j, P * lo, P * (hi - lo + 1), list(range(lo, hi + 1)), None))
    if layer == 0:
        for j in range(CTX // P):
            tiles.append((SEQ + P * j, 0, 0, [], None))
    return tiles


def chunk_groups(tile):
    _, _, width, band, _ = tile
    cols = [(v, BAND_END - width - BAND0 + P * n) for n, v in enumerate(band)]
    cols += [(4, BAND_END - BAND0), (5, BAND_END - BAND0 + P)]
    return [cols[n:n + 2] for n in range(0, len(cols), 2)]


def plan():
    stages = []

    def add(name, layer, trips, blocks=(), ada=None, **counts):
        if ada:
            counts.update(ada_rows_copied=ada[2], ada_cols_done=ada[2], ada_cols_added=ada[2])
        stages.append(Stage(name, layer, trips, list(blocks), ada, counts))

    def with_ada(blocks):
        return [b for n, own in enumerate(blocks) for b in ((f"a{n}", 2), own)]

    add("load", 0, 1, x_cols_done=8, x_cols_copied=8, sq_ready=8, sq_added=8)
    add("ada", 0, 1, [(f"a{n}", n % SLOTS) for n in range(2 * ADA_FIRST)], (0, 0, ADA_FIRST))
    for l in range(DEPTH):
        nt = len(attention_tiles("A", l))
        ga = sum(len(chunk_groups(t)) for t in attention_tiles("A", l))
        gb = sum(len(chunk_groups(t)) for t in attention_tiles("B", l))
        now, ahead = l == 0, l + 1 < DEPTH
        add("norm1", l, 4, normed=2, h_hi_done=2, h_lo_done=2)
        att = dict(scores_done=2 * nt, max_done=2 * nt, exp_done=2 * nt,
                   inv_done=2 * nt, p_done=2 * nt, o_done=nt, o_hi=nt, o_lo=nt)
        qkv = [("q", 2), ("k", 0), ("v", 1)]
        made = dict(q_hi=1, q_lo=1, k_hi=1, k_lo=1, v_copied=1)
        used = dict(masked=8, vt_done=1, v_hi=1, v_lo=1, pt_done=ga, pt_hi=ga, pt_lo=ga, **att)
        add("A0", l, 1, qkv, bias_done=1, **made)
        add("A", l, PAIRS - 1, qkv, bias_done=1, **made, **used)
        add("Az", l, 1, **used)
        merge = [("z", 0), ("m", 1)]
        add("mergeA", l, 8, with_ada(merge) if now else merge, (l, ADA_FIRST, 1) if now else None,
            z_summed=1, gate_ready=1, mix_done=1)
        made = dict(q_hi=1, q_lo=1, swapped=1, rope_cos=1, rope_sin=1, rotated=1)
        used = dict(sunk=2, pt_done=gb, pt_hi=gb, pt_lo=gb, **att)
        add("B0", l, 1, [("k", 0), ("q0", 2), ("q1", 1), ("v", 0)], k_hi=1, k_lo=1, v_copied=1, vt_done=1,
            v_hi=1, v_lo=1, q_hi=1, q_lo=1, swapped=2, rope_cos=2, rope_sin=2, rotated=2)
        add("B", l, PAIRS - 1, [("q0", 2), ("q1", 1)], q_summed=1 if l == 0 else 0, **made, **used)
        add("Bz", l, 1, **used)
        add("mergeB", l, 8, with_ada(merge) if now else merge, (l, ADA_FIRST + 8, 1) if now else None,
            z_summed=1, gate_ready=1, mix_done=1, mixed=1)
        add("C", l, 4, [("x", 2), ("c", 0), ("b", 1)], cx_copied=1, u_done=1,
            y_step=3, c_done=1, c_hi=1, c_lo=1)
        add("mergeC", l, 8, with_ada(merge) if ahead else merge, (l + 1, 0, 1) if ahead else None,
            z_summed=1, gate_ready=1, mix_done=1, mixed=1)
        add("split", l, 4, h_hi_done=2, h_lo_done=2)
        add("out", l, 4, [("o0", 0), ("o1", 1)], x_updated=2, sq_ready=2, sq_added=2)
        add("norm2", l, 4, normed=2, h_hi_done=2, h_lo_done=2)
        for f in range(2):
            add(f"up{f}", l, HALF_FF, [("gate", 0), ("up", 1)], silu_done=1, act_done=1,
                act_hi=1, act_lo=1)
            down = [("d0", 0), ("e0", 1), ("d1", 0), ("e1", 1)]
            squares = dict(sq_ready=2, sq_added=2) if f == 1 else {}
            add(f"down{f}", l, 4, with_ada(down) if ahead else down,
                (l + 1, 8 + 8 * f, 2) if ahead else None, x_updated=2, **squares)
    add("final", DEPTH - 1, 1)

    totals = dict(PRIMED)
    block = 0
    for st in stages:
        st.block = block
        block += st.trips * st.per
        st.base = dict(totals)
        for name, n in st.counts.items():
            totals[name] = totals.get(name, 0) + n * st.trips
    return {(st.name, st.layer): st for st in stages}, stages, totals


def build(nc, x, c, ctx, c_ctx, w_ada, b_ada, norm1_g, norm2_g, w_in, b_gate, rpb, sw_sink, conv_w,
          w_br_a, w_br_b, w_br_c, w_o, w_up, w_down, final_g, ident_in, masks_a, masks_b, rope_in, comb_in,
          out):
    stage_of, stages, totals = plan()
    blocks = [(st, i, k) for st in stages for i in range(st.trips) for k in range(st.per)]
    by_vector = stage_of["ada", 0].per

    landed, per_slot = [], [0] * SLOTS
    for st, i, k in blocks:
        per_slot[st.slots[k]] += 16 * st.dmas[k]
        landed.append(per_slot[st.slots[k]])

    distance, user = [], {}
    for b, (st, i, k) in enumerate(blocks):
        distance.append(b - user.get(st.slots[k], -1000))
        user[st.slots[k]] = b
    assert min(distance) >= 2

    stack = ExitStack()
    with stack:
        def sb(where, name, shape, dt=F32):
            return where.enter_context(nc.sbuf_tensor(name, shape, dt))

        def sem(name):
            return stack.enter_context(nc.semaphore(name))

        x_t = sb(stack, "x_t", [P, KC, TALL])
        h_hi = sb(stack, "h_hi", [P, KC, TALL], F32R)
        h_lo = sb(stack, "h_lo", [P, KC, TALL], F32R)
        w_raw = sb(stack, "w_raw", [P, 3, KC * P])
        w_hi = sb(stack, "w_hi", [P, 3, KC * P], F32R)
        w_lo = sb(stack, "w_lo", [P, 3, KC * P], F32R)
        ident = sb(stack, "ident", [P, P])
        ones = sb(stack, "ones", [P, P])
        mask_b = sb(stack, "mask_b", [P, 2, P], F32R)
        ident_r = sb(stack, "ident_r", [P, P], F32R)
        rope = sb(stack, "rope", [P, 2, SEQ])
        comb = sb(stack, "comb", [4, 2])
        eps = sb(stack, "eps", [P, 1])
        rstd = sb(stack, "rstd", [P, TALL // P])
        warm_sb = sb(stack, "warm_sb", [P, 48])
        rows = sb(stack, "rows", [4, ADA_W])
        vec = sb(stack, "vec", [P, DEPTH, P])
        sink = sb(stack, "sink", [P, DEPTH, SW_HEADS])
        ada = sb(stack, "ada", [P, DEPTH, 2, 48])
        a_mod = sb(stack, "a_mod", [P, 2, 2, KC])
        cond = sb(stack, "cond", [P, KC, 2])
        cond4 = sb(stack, "cond4", [P, KC, 4], F32R)
        nmax = sb(stack, "nmax", [P, 2, 2])
        rsum = sb(stack, "rsum", [P, 2, 2])
        rinv = sb(stack, "rinv", [P, 2, 2])

        with ExitStack() as r:
            tok = sb(r, "tok", [P, TALL // P, D_MODEL])
            vec_rows = sb(r, "vec_rows", [P, DEPTH, P])
            mask_in = sb(r, "mask_in", [P, 2, P])
            more_raw = sb(r, "more_raw", [P, SLOTS - RING, KC * P])
        with ExitStack() as r:
            normed_t = sb(r, "normed_t", [P, 2, TALL])
        with ExitStack() as r:
            br_hi = sb(r, "br_hi", [P, PAIRS, TALL], F32R)
            br_lo = sb(r, "br_lo", [P, PAIRS, TALL], F32R)
            with ExitStack() as r2:
                rpb_seg = sb(r2, "rpb_seg", [P, NA_HEADS, SEG])
                mask_a = sb(r2, "mask_a", [P, 3, 2 * P])
                v_fm_a = sb(r2, "v_fm_a", [P, TALL])
                with ExitStack() as r3:
                    rpb_back = sb(r3, "rpb_back", [P, NA_HEADS, SEG])
                with ExitStack() as r3:
                    bias = sb(r3, "bias", [P, 3, 2, 2 * P])
            merged = sb(r, "merged", [P, KC, TALL])
            with ExitStack() as r2:
                q_hi = sb(r2, "q_hi_t", [P, TALL], F32R)
                q_lo = sb(r2, "q_lo_t", [P, TALL], F32R)
                k_hi = sb(r2, "k_hi_t", [P, 640 + CTX], F32R)
                k_lo = sb(r2, "k_lo_t", [P, 640 + CTX], F32R)
                v_hi = sb(r2, "v_hi_t", [P, TALL], F32R)
                v_lo = sb(r2, "v_lo_t", [P, TALL], F32R)
                pt_hi = sb(r2, "pt_hi_t", [P, 2, 4 * P], F32R)
                pt_lo = sb(r2, "pt_lo_t", [P, 2, 4 * P], F32R)
                swap = sb(r2, "swap", [P, SEQ])
                rc = sb(r2, "rc", [P, SEQ])
                with ExitStack() as r3:
                    probs = sb(r3, "probs", [P, 2, 2, 644])
                with ExitStack() as r3:
                    v_fm = sb(r3, "v_fm", [P, TALL])
            with ExitStack() as r2:
                gate = sb(r2, "gate", [P, TALL])
                mix = sb(r2, "mix", [P, TALL])
            with ExitStack() as r2:
                cx_sb = sb(r2, "cx_sb", [P, TALL])
                u_pad = sb(r2, "u_pad", [P, TALL + 4])
                y_a = sb(r2, "y_a", [P, TALL + 2])
                y_b = sb(r2, "y_b", [P, TALL + 2])
                c_out = sb(r2, "c_out", [P, TALL])
        with ExitStack() as r:
            a_hi = sb(r, "a_hi", [P, HALF_FF, TALL], F32R)
            a_lo = sb(r, "a_lo", [P, HALF_FF, TALL], F32R)
            silu_sb = sb(r, "silu_sb", [P, TALL])
            act_sb = sb(r, "act_sb", [P, TALL])
            sq = sb(r, "sq", [P, 2, TALL])
            ssum = sb(r, "ssum", [P, TALL])
        with ExitStack() as r:
            r.enter_context(nc.sbuf_tensor("under_y", [P, 2 * TALL], F32))
            y_fm = sb(r, "y_fm", [P, KC, SEQ])
            y_tok = sb(r, "y_tok", [P, 2, D_MODEL])

        psum = stack.enter_context(nc.psum_tensor("psum", [P, 8 * 512], F32))

        def raw_slot(slot):
            return w_raw[:, slot, :] if slot < RING else more_raw[:, slot - RING, :]

        def part_slot(part, slot):
            if slot < RING:
                return part[:, slot, :]
            more = (h_hi if part is w_hi else h_lo)[:, :, :].rearrange("p c t -> p (c t)")
            return more[:, (slot - RING) * KC * P:(slot - RING + 1) * KC * P]

        def bank(n, width=512):
            return psum[:, 512 * n:512 * n + width]

        s = {name: sem(name) for name in totals}
        s_const = sem("const_loaded")
        s_load = [sem(f"w_loaded{n}") for n in range(SLOTS)]
        s_whi = sem("w_hi_done")
        s_wlo = sem("w_lo_done")
        s_block = sem("block_done")
        s_vecT = sem("vec_transposed")
        s_vec = sem("vec_copied")
        s_ones = sem("ones_set")
        s_zero = sem("pad_zeroed")
        s_cond = sem("cond_step")
        s_mod = sem("mod_ready")
        s_ms = sem("mean_square_step")
        s_rstd = sem("rstd_ready")
        s_yfm = sem("y_ready")
        s_yT = sem("y_transposed")
        s_ytok = sem("y_copied")
        s_out = [sem(f"out_stored{n}") for n in range(2)]
        s_rpb = sem("rpb_loaded")
        s_rpbf = sem("rpb_forward")
        s_wlov = sem("w_lo_done_by_vector")
        s_ssz = sem("sum_zeroed")
        s_maskb = sem("mask_for_products")
        s_sumsq = sem("squares_summed")
        s_spread = sem("scales_spread")
        s_first = sem("vectors_loaded")
        s_tok = [sem(f"tokens_loaded{n}") for n in range(2)]

        FIRST = 2 + 8
        CONSTS = DEPTH + 2

        WI = w_in.rearrange("l (kc p) (ct f) -> l ct p kc f", p=P, f=P)
        WI64 = w_in.rearrange("l (kc p) (ct f) -> l ct p kc f", p=P, f=HD)
        WADA = w_ada.rearrange("l (kc p) (g f) -> l g p kc f", p=P, f=ADA_W)
        WBR = {"A": w_br_a.rearrange("l (kc p) (d f) -> l d p kc f", p=P, f=P),
               "B": w_br_b.rearrange("l (e kc p) (d f) -> l d e p kc f", e=2, p=HD, f=P),
               "C": w_br_c.rearrange("l (kc p) (d f) -> l d p kc f", p=P, f=P)}
        WO = w_o.rearrange("l (kc p) (d f) -> l d p kc f", p=P, f=P)
        WUP = w_up.rearrange("l (kc p) (ct f) -> l ct p kc f", p=P, f=P)
        WDN = w_down.rearrange("l (kc p) (d f) -> l d p kc f", p=P, f=P)

        def block_source(st, i, k):
            l, name = st.layer, st.name
            slot = raw_slot(st.slots[k])

            def cols(kc):
                return slot[:, 0:kc * P].rearrange("p (kc f) -> p kc f", f=P)

            tag = st.tags[k]
            if st.ada and tag[0] == "a":
                al, first, n = st.ada
                unit, half = int(tag[1:]) // 2, int(tag[1:]) % 2
                return [(slot.rearrange("p (kc f) -> p kc f", f=ADA_W),
                         WADA[al, i * n + (first + unit), :, 4 * half:4 * half + 4])]
            if name in ("A0", "A"):
                return [(cols(KC), WI[l, i + dict(q=CT_QA, k=CT_KA, v=CT_VA)[tag] + (1 if name == "A" else 0)])]
            if name == "B0" and tag in ("k", "v"):
                return [(cols(KC), WI[l, dict(k=CT_KB, v=CT_VB)[tag]])]
            if name in ("B0", "B"):
                j = i + (1 if name == "B" else 0)
                d = cols(KC // 2)
                first = KC // 2 * int(tag[1])
                return [(d[:, :, HD * e:HD * e + HD], WI64[l, j + 2 * CT_QB + 4 * e, :, first:first + KC // 2])
                        for e in range(2)]
            if name == "C":
                return [(cols(KC), WI[l, i + dict(x=CT_X, c=CT_GC, b=CT_GB)[tag]])]
            if name.startswith("merge"):
                kind = name[5]
                z = WI[l, i + CT_ZG + 8 * "ABC".index(kind)]
                if tag == "z":
                    return [(cols(MERGE_Z), z[:, 0:MERGE_Z])]
                d = cols(KC - MERGE_Z + 4)
                rest_z, m = (d[:, 0:KC - MERGE_Z], z[:, MERGE_Z:KC]), d[:, KC - MERGE_Z:]
                if kind == "B":
                    return [rest_z] + [(m[HD * e:HD * e + HD], WBR["B"][l, i, e]) for e in range(2)]
                return [rest_z, (m, WBR[kind][l, i])]
            if name == "out":
                return [(cols(KC), WO[l, i * 2 + k])]
            if name.startswith("up"):
                f = int(name[2])
                return [(cols(KC), WUP[l, i + HALF_FF * f + (0 if tag == "gate" else 2 * HALF_FF)])]
            f = int(name[4])
            first, n = (HALF_FF * f, DOWN_D) if tag[0] == "d" else (HALF_FF * f + DOWN_D, HALF_FF - DOWN_D)
            return [(cols(n), WDN[l, i * 2 + int(tag[1]), :, first:first + n])]

        def block_width(st, k):
            tag = st.tags[k]
            if tag in ("q0", "q1"):
                return KC // 2 * P
            chunks = {"z": MERGE_Z, "m": KC - MERGE_Z + 4, "d": DOWN_D, "e": HALF_FF - DOWN_D}
            return chunks.get(tag[0], KC) * P

        def block_at(st, i, k):
            if isinstance(i, int):
                b = st.block + i * st.per + k
                if b >= len(blocks):
                    return None
                return (*blocks[b], b)
            assert k < 2 * st.per
            return (st, i + k // st.per, k % st.per, i * st.per + (st.block + k))

        def load_value(st, i, k):
            first = landed[st.block + k]
            if isinstance(i, int):
                return landed[st.block + i * st.per + k]
            if st.trips == 1:
                return first
            return i * (landed[st.block + st.per + k] - first) + first

        def passes(eng, st, body, first=0):
            for i in range(first):
                body(i)
            if st.trips > first + 1:
                with eng.Fori(first, st.trips - 1) as i:
                    body(i)
            body(st.trips - 1)

        def at(st, name, i, k):
            return i * st.counts[name] + (st.base.get(name, 0) + k)

        def wait(eng, st, name, i, k=None):
            v = at(st, name, i, st.counts[name] if k is None else k)
            if not (isinstance(v, int) and v <= 0):
                eng.wait_ge(s[name], v)

        def wait_block(eng, st, i, k):
            eng.wait_ge(s_block, block_at(st, i, k)[3] + 1)

        def wait_lo(eng, b):
            if isinstance(b, int) and b < by_vector:
                eng.wait_ge(s_wlov, b + 1)
            else:
                eng.wait_ge(s_wlo, b + 1)

        def slot_distance(blk):
            st, i, k, b = blk
            return distance[b] if isinstance(b, int) else distance[st.block + st.per + k]

        def h_ready(st):
            return lambda eng, kc: wait(eng, st, "h_lo_done", kc // 2, kc % 2 + 1)

        def wait_before(eng, st, name, i):
            if name in st.counts:
                wait(eng, st, name, i, 0)
            else:
                wait_total(eng, st, name)

        def prime(eng, *names):
            for name in names:
                eng.sem_inc(s[name], PRIMED[name])

        def wait_total(eng, st, name):
            v = st.base.get(name, 0)
            if v > 0:
                eng.wait_ge(s[name], v)

        def segs(width):
            return [(0, 0, SEQ)] + ([(1, SEQ, TALL)] if width == TALL else [])

        def width_of(l):
            return TALL if l == 0 else SEQ

        def spreads(number):
            widths = [w for l in range(DEPTH) for w in (TALL, width_of(l))]
            return sum(1 if w == SEQ else 2 for w in widths[:number - 1]) + 1

        def perm(ap):
            return ap.rearrange("p (r c) -> p c r", c=GRID_W)

        def grid(ap):
            return ap.rearrange("p (c r) -> p c r", r=ROWS)

        def chunk(t, i, k, n=2):
            if isinstance(i, int):
                return t[:, n * i + k, :]
            return t[:, :, :].rearrange("p (c k) t -> p c k t", k=n)[:, i, k, :]

        def x_chunk(i, k, n):
            return chunk(x_t, i, k, n)

        def pair_of(st, i):
            return PAIRS - 1 if st.name in ("Az", "Bz") else i

        def tile_of(t, i):
            return t[:, i, :]

        pair = tile_of

        def ada_col(l, e, piece, i, k):
            return ada[:, l, e, KC * piece:KC * piece + KC].rearrange("p (c k) -> p c k", k=2)[:, i, k:k + 1]

        def mod_col(which, e, i, k):
            return a_mod[:, which, e, :].rearrange("p (c k) -> p c k", k=2)[:, i, k:k + 1]

        def vec_col(l, first, i):
            if isinstance(i, int):
                return vec[:, l, first + i:first + i + 1]
            return vec[:, l, first:P].rearrange("p (a b) -> p a b", b=1)[:, i, :]

        def sink_col(l, e, i):
            return sink[:, l, 4 * e:4 * e + 4].rearrange("p (a b) -> p a b", b=1)[:, i, :]

        def rpb_runs(i, e):
            seg = rpb_seg[:, :, :].rearrange("p (i e) w -> p i e w", e=2)[:, i, e, :]
            return bass.AP(seg.tensor, seg.offset, [list(seg.ap[0]), [1, 32], [RPB_W, ROWS]])

        def score_base(kind, e):
            return 768 + 512 * e if kind == "A" else 1024 * (1 + e)

        def turn_bank(kind, g):
            return (6, 4 if kind == "A" else 0)[g % 2]

        def out_bank(kind, n):
            return 7

        def context_bank(st):
            return 0 if st.name == "B0" else 2

        def q_pieces_b(dst, st):
            context = [(dst[:, SEQ:TALL], bank(context_bank(st), CTX))] if st.layer == 0 else []
            return [(dst[:, 0:SEQ], rc[:])] + context

        def q_pieces_a(dst, width, b):
            out_ = [(grid(dst[:, 0:SEQ]), perm(bank(b)))]
            return out_ + ([(dst[:, SEQ:TALL], bank(b + 1, CTX))] if width == TALL else [])

        def k_pieces_a(dst):
            src = perm(bank(2))
            return [(grid(dst[:, 64:64 + SEQ]), src), (grid(dst[:, 0:64]), src[:, 56:64, :]),
                    (grid(dst[:, 576:640]), src[:, 0:8, :]), (dst[:, 640:640 + CTX], bank(3, CTX))]

        def v_pieces_a():
            src = perm(bank(0))
            return [(grid(v_fm_a[:, 64:SEQ]), src[:, 0:56, :]), (grid(v_fm_a[:, 0:64]), src[:, 56:64, :]),
                    (v_fm_a[:, SEQ:TALL], bank(1, CTX))]

        def out_pieces(dst, kind, i, n, q0):
            pieces = []
            for e in range(2):
                part = slice(HD * e, HD * e + HD)
                src = bank(out_bank(kind, n))[part, P * e:P * e + P]
                d = dst[part, i, :]
                if kind == "A" and q0 < SEQ:
                    c0 = q0 // ROWS
                    pieces.append((perm(d[:, 0:SEQ])[:, c0:c0 + P // ROWS, :], grid(src)))
                else:
                    pieces.append((d[:, q0:q0 + P], src))
            return pieces

        block = stack.enter_context(nc.Block())

        @block.sync
        def _(sp):
            def const(dst, src):
                sp.dma_start(dst, src).then_inc(s_const, 16)

            def first_const(dst, src):
                sp.dma_start(dst, src).then_inc(s_first, 16)

            first_const(ident[:], ident_in)
            first_const(comb[:], comb_in)
            def vrow(first, src):
                if len(src.shape) == 3:
                    first_const(vec_rows[first:first + src.shape[0], :, :], src)
                else:
                    first_const(vec_rows[first:first + src.shape[0], 0, :], src)
            vrow(V_C, c.rearrange("o (a b) -> (o a) b", b=P))
            vrow(V_CC, c_ctx.rearrange("(a b) -> a b", b=P))
            vrow(V_BADA, b_ada.rearrange("l (a b) -> a l b", b=P))
            vrow(V_N1, norm1_g.rearrange("l (a b) -> a l b", b=P))
            vrow(V_N2, norm2_g.rearrange("l (a b) -> a l b", b=P))
            vrow(V_BGATE, b_gate.rearrange("l (a b) -> a l b", b=P))
            vrow(V_CONV, conv_w.rearrange("l k (a b) -> (k a) l b", b=P))
            vrow(V_FINAL, final_g.rearrange("(a b) -> a b", b=P))

            def load(blk):
                if blk is None:
                    return
                st, i, k, b = blk
                last = b - slot_distance(blk)
                if not (isinstance(last, int) and last < 0):
                    sp.wait_ge(s_whi, last + 1)
                    wait_lo(sp, last)
                for dst, src in block_source(st, i, k):
                    sp.dma_start(dst, src).then_inc(s_load[st.slots[k]], 16)

            first = stage_of["ada", 0]
            for k in range(4):
                load(block_at(first, 0, k))
            for half in range(2):
                f = slice(half * D_MODEL // 2, (half + 1) * D_MODEL // 2)
                sp.dma_start(tok[:, 0:4, f], x.rearrange("b (t p) d -> p (b t) d", p=P)[:, :, f])\
                  .then_inc(s_tok[half], 16)
                sp.dma_start(tok[:, 4:6, f], ctx.rearrange("b (t p) d -> p (b t) d", p=P)[:, :, f])\
                  .then_inc(s_tok[half], 16)
                for k in ((4, 5, 6, 7), (8,))[half]:
                    load(block_at(first, 0, k))
            for l in range(DEPTH):
                const(sink[:, l, :], bass.AP(sw_sink.tensor, l * SW_HEADS, [[0, P], [1, SW_HEADS]]))
            const(mask_in[:], masks_b)
            const(rope[:], rope_in)
            for st in stages:
                def body(i, st=st):
                    for k in range(SLOTS - 2 if st.name == "ada" else 0, st.per):
                        load(block_at(st, i, k + 2))
                if st.per:
                    passes(sp, st, body)
                if st.name == "A0":
                    if st.layer:
                        wait_total(sp, st, "x_updated")
                    else:
                        sp.wait_ge(s_vec, DEPTH)
                        sp.wait_ge(s_wlov, by_vector)
                    for h in range(NA_HEADS):
                        off = RPB_PAD + (st.layer * NA_HEADS + h) * RPB - 8
                        src = bass.AP(rpb.tensor, off, [[1, P // ROWS], [RPB_W, ROWS], [1, SEG]])
                        sp.dma_start(rpb_back[:, h, :], src).then_inc(s_rpb, 16)
                    sp.dma_start(mask_a[:], masks_a).then_inc(s_rpb, 16)

            for t in range(SEQ // P):
                sp.wait_ge(s_ytok, t + 1)
                sp.dma_start(out[0, t * P:(t + 1) * P, :], y_tok[:, t % 2, :]).then_inc(s_out[t % 2], 16)
            for n in range(2):
                sp.wait_ge(s_out[n], 16 * (SEQ // P // 2))

        @block.gpsimd
        def _(pool):
            prime(pool, "bias_done", "sq_added")
            pool.sem_inc(s_wlo, by_vector)
            pool.memset(eps[:], EPS)
            pool.memset(ones[:], 1.0).then_inc(s_ones, 1)

            def new_sum(number):
                pool.memset(ssum[:], 0.0).then_inc(s_ssz, 1)
                pool.wait_ge(s_ssz, number)

            def split_lo(blk):
                if blk is None:
                    return
                st, i, k, b = blk
                if isinstance(b, int) and b < by_vector:
                    return
                slot, w = st.slots[k], block_width(st, k)
                pool.wait_ge(s_whi, b + 1)
                last = b - slot_distance(blk)
                pool.wait_ge(s_block, last + 1)
                pool.tensor_tensor(w_lo[:, slot, 0:w], w_raw[:, slot, 0:w], w_hi[:, slot, 0:w].bitcast(F32),
                                   ALU.subtract).then_inc(s_wlo, 1)

            def rotate(st, i, n):
                pool.wait_ge(s_const, 16 * CONSTS)
                wait(pool, st, "swapped", i, n + 1)
                pool.tensor_tensor(swap[:], swap[:], rope[:, 1, :], ALU.mult).then_inc(s["rope_sin"], 1)
                wait(pool, st, "rope_sin", i, n + 1)
                wait(pool, st, "rope_cos", i, n + 1)
                pool.tensor_tensor(rc[:], rc[:], swap[:], ALU.add).then_inc(s["rotated"], 1)

            def forward_runs(l):
                pool.wait_ge(s_rpb, 16 * (NA_HEADS + 1) * (l + 1))
                pool.wait_ge(s_maskb, 2)
                back = rpb_back[:, :, :]
                pool.tensor_copy(rpb_seg[:, :, :],
                                 bass.AP(back.tensor, back.offset + SEG - 1,
                                         [list(back.ap[0]), [SEG, NA_HEADS], [-1, SEG]])).then_inc(s_rpbf, 1)
                pool.wait_ge(s_rpbf, l + 1)

            def bias_tables(pair_):
                for v in range(3):
                    for e in range(2):
                        ins = pool.tensor_tensor(bias[:, v, e, :].rearrange("p (b r) -> p b r", r=8),
                                                 rpb_runs(pair_, e),
                                                 mask_a[:, v, :].rearrange("p (b r) -> p b r", r=8), ALU.add)
                ins.then_inc(s["bias_done"], 1)

            new_sum(1)
            number = 1
            for st in stages:
                if st.name in ("out", "down1"):
                    number += 1
                    if st.name == "out":
                        wait(pool, stage_of["split", st.layer], "h_lo_done", 3)
                    else:
                        wait(pool, stage_of["up1", st.layer], "act_lo", HALF_FF - 1)
                    new_sum(number)
                if st.name == "load":
                    for ch in range(KC):
                        wait(pool, st, "sq_ready", 0, ch + 1)
                        wait(pool, st, "sq_added", 0, ch)
                        pool.tensor_tensor(ssum[:], ssum[:], sq[:, ch % 2, :], ALU.add).then_inc(s["sq_added"], 1)

                def body(i, st=st):
                    if st.name == "B":
                        rotate(st, i, 0)
                    for k in range(st.per):
                        split_lo(block_at(st, i, k + 2))
                        if k == 1 and st.name == "B0":
                            rotate(st, 0, 0)
                            rotate(st, 0, 1)
                        if k == 0 and st.name == "A0":
                            forward_runs(st.layer)
                            bias_tables(0)
                        if k == 0 and st.name == "A":
                            wait(pool, st, "masked", i)
                            bias_tables(i + 1)
                if st.per:
                    passes(pool, st, body)

        @block.tensor
        def _(pe):
            def steps(st, i, k, dst, rhs_hi, rhs_lo, nk, width, first=True, last=True, kc0=0, ready=None, w0=0,
                      signal=s_block):
                b = block_at(st, i, k)[3]
                pe.wait_ge(s_whi, b + 1)
                wait_lo(pe, b)
                slot = st.slots[k]
                for kc in range(nk):
                    if ready:
                        ready(pe, kc)
                    cols = slice((w0 + kc) * P, (w0 + kc + 1) * P)
                    for n, (w, r) in enumerate(((w_hi, rhs_hi), (w_hi, rhs_lo), (w_lo, rhs_hi))):
                        for _, t0, t1 in segs(width):
                            ins = pe.matmul(psum[:, dst * 512 + t0:dst * 512 + t1], w[:, slot, cols],
                                            r[:, kc0 + kc, t0:t1], start=first and kc == 0 and n == 0,
                                            stop=last and kc == nk - 1 and n == 2)
                    if kc == nk - 1:
                        ins.then_inc(signal, 1)
                    yield

            def project(*args, **kw):
                for _ in steps(*args, **kw):
                    pass

            def together(*parts):
                for _ in zip(*parts):
                    pass
                for part in parts:
                    for _ in part:
                        pass

            def ada_half(st, i, n):
                k = st.pos(f"a{n}")
                b = block_at(st, i, k)[3]
                if n % 2 == 0:
                    wait(pe, st, "ada_rows_copied", i, n // 2)
                pe.wait_ge(s_whi, b + 1)
                wait_lo(pe, b)
                for kk in range(4):
                    for w in (w_hi, w_lo):
                        ins = pe.matmul(bank(4)[0:4, 0:ADA_W], cond4[:, 4 * (n % 2) + kk, :],
                                        part_slot(w, st.slots[k])[:, kk * ADA_W:(kk + 1) * ADA_W],
                                        start=n % 2 == 0 and kk == 0 and w is w_hi,
                                        stop=n % 2 == 1 and kk == 3 and w is w_lo)
                ins.then_inc(s_block, 1)

            def ada_turn(st, i, u):
                wait(pe, st, "ada_rows_copied", i, u + 1)
                wait(pe, st, "ada_cols_added", i, u)
                for j in range(2):
                    ins = pe.matmul(bank(5)[:, 2 * j:2 * j + 2], rows[:, P * j:P * j + P], comb[:, :],
                                    start=True, stop=True)
                ins.then_inc(s["ada_cols_done"], 1)

            sums = {(st.name, st.layer): st.base.get("sq_added", 0) + st.trips * st.counts["sq_added"]
                    for st in stages if "sq_added" in st.counts}
            prime(pe, "ada_cols_done")
            pe.wait_ge(s_first, 16 * FIRST)
            for l in range(DEPTH):
                n = V_END if l == 0 else V_FINAL
                pe.transpose(bank(4 + l, n), vec_rows[0:n, l, :], ident[0:n, 0:n]).then_inc(s_vecT, 1)
            pe.wait_ge(s_vec, DEPTH)

            def x_columns(ch):
                ld = stage_of["load", 0]
                pe.wait_ge(s_tok[ch // 4], 32)
                if ch >= 2:
                    wait(pe, ld, "x_cols_copied", 0, ch - 1)
                for t in range(TALL // P):
                    ins = pe.transpose(psum[:, 1024 * (ch % 2) + t * P:1024 * (ch % 2) + (t + 1) * P],
                                       tok[:, t, ch * P:(ch + 1) * P], ident[:])
                ins.then_inc(s["x_cols_done"], 1)

            def stage_ada(st):
                pe.wait_ge(s_cond, 4)
                n = st.ada[2]
                for u in range(n):
                    ada_half(st, 0, 2 * u)
                    if u:
                        ada_turn(st, 0, u - 1)
                    ada_half(st, 0, 2 * u + 1)
                    x_columns(u)
                ada_turn(st, 0, n - 1)

            def stage_norm(st, width, number):
                if number % 2 == 0:
                    before = "out", (number - 2) // 2
                else:
                    before = ("load", 0) if number == 1 else ("down1", (number - 3) // 2)
                pe.wait_ge(s["sq_added"], sums[before])
                wait_total(pe, st, "ada_cols_added")
                for t in range(width // P):
                    ins = pe.matmul(bank(5)[:, t:t + 1], ssum[:, t * P:(t + 1) * P], ones[:, 0:1], start=True,
                                    stop=True)
                ins.then_inc(s_sumsq, 1)
                pe.wait_ge(s_ms, number)
                for t in range(width // P):
                    ins = pe.matmul(psum[:, 3072 + t * P:3072 + (t + 1) * P],
                                    rstd[:, t:t + 1].broadcast_to([P, P]), ident[:], start=True, stop=True)
                    if (t + 1) * P in (SEQ, TALL):
                        ins.then_inc(s_spread, 1)

            def values_turn(st, i, v_fm_, b):
                for t in range(6):
                    ins = pe.transpose(psum[:, b * 512 + t * P:b * 512 + (t + 1) * P], v_fm_[:, t * P:(t + 1) * P],
                                       ident[:])
                ins.then_inc(s["vt_done"], 1)

            def attention(st, kind, i, ahead=None, tail=None):
                tiles = attention_tiles(kind, st.layer)
                N = len(tiles)

                def scores(n):
                    q0, k0, width, _, _ = tiles[n]
                    for e in range(2):
                        base = score_base(kind, e)
                        rows_ = slice(HD * e, HD * e + HD)
                        if n > 0:
                            wait(pe, st, "exp_done", i, 2 * (n - 1) + e + 1)
                        for first, keys, count in ((BAND_END - width, k0, width), (BAND_END, 640, CTX)):
                            for m, (q, kk) in enumerate(((q_hi, k_hi), (q_hi, k_lo), (q_lo, k_hi))):
                                if count:
                                    ins = pe.matmul(psum[:, base + first:base + first + count],
                                                    q[rows_, q0:q0 + P], kk[rows_, keys:keys + count],
                                                    start=m == 0, stop=m == 2)
                                if count and kind == "B" and m == 0 and first < BAND_END:
                                    if q0 == SEQ - P:
                                        edges = [(1, 0)]
                                    elif q0 == 0:
                                        edges = [(2, 1)]
                                    else:
                                        edges = [(0, 0), (2, 1)]
                                    for block_, side in edges:
                                        c0 = base + BAND0 + P * block_
                                        pe.matmul(psum[:, c0:c0 + P], ident_r[:], mask_b[:, side, :], start=False,
                                                  stop=False)
                        ins.then_inc(s["scores_done"], 1)

                def fill(part, count):
                    for _ in range(count if part else 0):
                        next(part, None)

                if kind == "A":
                    share = [KC * (n + 1) // (N - 1) - KC * n // (N - 1) for n in range(N - 1)][::-1] + [0]
                else:
                    later = [3] if N == 4 else [2] + [1] * (N - 4)
                    share = [KC - sum(later)] + later + [KC, 0]
                wait_before(pe, st, "q_lo", i)
                wait_before(pe, st, "k_lo", i)
                scores(0)
                if kind == "A":
                    wait_before(pe, st, "v_copied", i)
                    values_turn(st, i, v_fm_a, 0)
                g0 = 0
                for n, tile in enumerate(tiles):
                    if n == 0 and kind == "B":
                        fill(ahead, share[0] - 2)
                    if n + 1 < N:
                        scores(n + 1)
                    groups = chunk_groups(tile)
                    if n == 0:
                        wait(pe, st, "v_lo", i) if kind == "A" else wait_total(pe, st, "v_lo")
                    if n == 0:
                        fill(ahead, 1)
                    wait(pe, st, "p_done", i, 2 * n + 2)

                    def turn(g):
                        gg = g0 + g
                        if gg >= 2:
                            wait(pe, st, "pt_lo", i, gg - 1)
                        for m, (_, col) in enumerate(groups[g]):
                            for e in range(2):
                                ins = pe.transpose(
                                    bank(turn_bank(kind, gg))[:, (2 * m + e) * P:(2 * m + e + 1) * P],
                                    probs[:, n % 2, e, col:col + P], ident[:])
                        ins.then_inc(s["pt_done"], 1)

                    def values(g):
                        gg = g0 + g
                        wait(pe, st, "pt_lo", i, gg + 1)
                        if g == 0:
                            wait(pe, st, "o_lo", i, n)
                        for m, (v, _) in enumerate(groups[g]):
                            cols = slice(2 * m * P, 2 * m * P + 2 * P)
                            for w, (vv, pp) in enumerate(((v_hi, pt_hi), (v_hi, pt_lo), (v_lo, pt_hi))):
                                ins = pe.matmul(bank(out_bank(kind, n), 2 * P), vv[:, v * P:(v + 1) * P],
                                                pp[:, gg % 2, cols],
                                                start=g == 0 and m == 0 and w == 0,
                                                stop=g == len(groups) - 1 and m == len(groups[g]) - 1 and w == 2)
                        if g == len(groups) - 1:
                            ins.then_inc(s["o_done"], 1)

                    turn(0)
                    for g in range(len(groups)):
                        if g + 1 < len(groups):
                            turn(g + 1)
                        if g == 0:
                            fill(ahead, share[n] - (0 if n else 1 if kind == "A" else share[0] - 1))
                        if n == N - 1:
                            fill(tail, KC // 2 if g == 0 else 2)
                        values(g)
                    if n == N - 1:
                        fill(tail, KC)
                    g0 += len(groups)

            def stage_a0(st):
                width = width_of(st.layer)
                ready = h_ready(stage_of["norm1", st.layer])
                pe.wait_ge(s_ms, 2 * st.layer + 1)
                together(*[steps(st, 0, st.pos(tag), b, h_hi, h_lo, KC, w, ready=ready)
                           for tag, b, w in (("q", 4, width), ("k", 2, TALL), ("v", 0, TALL))])

            def stage_a(st):
                width = width_of(st.layer)

                def body(i):
                    attention(st, "A", i, ahead=steps(st, i, st.pos("q"), 0, h_hi, h_lo, KC, width),
                              tail=steps(st, i, st.pos("k"), 2, h_hi, h_lo, KC, TALL))
                    wait(pe, st, "q_lo", i)
                    project(st, i, st.pos("v"), 0, h_hi, h_lo, KC, TALL)
                passes(pe, st, body)

            def after_merge(name, l):
                merge = stage_of[name, l]
                wait(pe, merge, "mix_done", 7)
                if merge.ada:
                    wait(pe, merge, "ada_cols_added", 7)

            def q_steps(st, i, part):
                t0, t1 = ((0, SEQ), (SEQ, TALL))[part]
                done = part == 1 or width_of(st.layer) == SEQ
                for half in range(2):
                    k = st.pos(f"q{half}")
                    b = block_at(st, i, k)[3]
                    pe.wait_ge(s_whi, b + 1)
                    wait_lo(pe, b)
                    for kc in range(KC // 2):
                        for n, (w, r) in enumerate(((w_hi, h_hi), (w_hi, h_lo), (w_lo, h_hi))):
                            ins = pe.matmul(bank(context_bank(st) if part else 1, t1 - t0), w[:, st.slots[k], kc * P:kc * P + P],
                                            r[:, KC // 2 * half + kc, t0:t1],
                                            start=half == 0 and kc == 0 and n == 0,
                                            stop=half == 1 and kc == KC // 2 - 1 and n == 2)
                        if done and kc == KC // 2 - 1:
                            ins.then_inc(s_block, 1)
                        elif st.name == "B" and half == 1 and kc == KC // 2 - 1:
                            ins.then_inc(s["q_summed"], 1)
                        yield

            def q_all(st, i):
                yield from q_steps(st, i, 0)
                if width_of(st.layer) == TALL:
                    yield from q_steps(st, i, 1)

            def stage_b0(st):
                after_merge("mergeA", st.layer)
                pe.wait_ge(s_maskb, 2)
                project(st, 0, st.pos("k"), 2, h_hi, h_lo, KC, TALL)
                for _ in q_all(st, 0):
                    pass
                project(st, 0, st.pos("v"), 4, h_hi, h_lo, KC, TALL)
                wait(pe, st, "v_copied", 0)
                values_turn(st, 0, v_fm, 6)

            def stage_b(st):
                passes(pe, st, lambda i: attention(st, "B", i, ahead=q_all(st, i)))

            def stage_merge(st):
                width = width_of(st.layer)
                kind = st.name[5]
                prev, done = {"A": ("Az", "o_lo"), "B": ("Bz", "o_lo"), "C": ("C", "c_lo")}[kind]
                prev = stage_of[prev, st.layer]
                if kind == "C":
                    wait(pe, prev, "c_done" if st.ada else "cx_copied", prev.trips - 1)

                def body(i):
                    if st.ada:
                        ada_half(st, i, 0)
                    wait(pe, st, "gate_ready", i, 0)
                    project(st, i, st.pos("z"), 0, h_hi, h_lo, MERGE_Z, width, last=False)
                    if st.ada:
                        ada_half(st, i, 1)
                    project(st, i, st.pos("m"), 0, h_hi, h_lo, KC - MERGE_Z, width, first=False, kc0=MERGE_Z,
                            signal=s["z_summed"])
                    if isinstance(i, int) and i == 0:
                        wait(pe, prev, done, prev.trips - 1)
                    wait(pe, st, "mix_done", i, 0)
                    project(st, i, st.pos("m"), 2, br_hi, br_lo, 4, width, w0=KC - MERGE_Z)
                    if st.ada:
                        ada_turn(st, i, 0)
                passes(pe, st, body, first=1)

            def stage_c(st):
                width = width_of(st.layer)
                after_merge("mergeB", st.layer)

                def body(i):
                    wait(pe, st, "c_done", i, 0)
                    for k in range(3):
                        project(st, i, k, 2 * k, h_hi, h_lo, KC, width)
                passes(pe, st, body)

            def stage_out(st):
                width = width_of(st.layer)
                merge = stage_of["mergeC", st.layer]
                wait(pe, merge, "gate_ready", 7)
                ready = h_ready(stage_of["split", st.layer])

                def body(i):
                    for k in range(2):
                        if isinstance(i, int) and i == 0 and k == 1:
                            wait(pe, merge, "mix_done", 7)
                        wait(pe, st, "x_updated", i, k - 1)
                        project(st, i, k, 2 * k, h_hi, h_lo, KC, width,
                                ready=ready if isinstance(i, int) and i == 0 and k == 0 else None)
                passes(pe, st, body, first=1)

            def stage_up(st):
                width = width_of(st.layer)
                ready = None
                if st.name == "up0":
                    ready = h_ready(stage_of["norm2", st.layer])
                    pe.wait_ge(s_ms, 2 * st.layer + 2)
                else:
                    wait(pe, stage_of["down0", st.layer], "x_updated", 3, 1)

                def body(i):
                    wait(pe, st, "silu_done", i, 0)
                    if isinstance(i, int) and i == 0 and ready:
                        together(steps(st, i, 0, 0, h_hi, h_lo, KC, width, ready=ready),
                                 steps(st, i, 1, 2, h_hi, h_lo, KC, width, ready=ready))
                        return
                    project(st, i, 0, 0, h_hi, h_lo, KC, width)
                    if isinstance(i, int) and i == 0:
                        wait(pe, stage_of["down0", st.layer], "x_updated", 3)
                    wait(pe, st, "act_done", i, 0)
                    project(st, i, 1, 2, h_hi, h_lo, KC, width)
                passes(pe, st, body, first=1)

            def stage_down(st):
                width = width_of(st.layer)
                up = stage_of[f"up{st.name[4]}", st.layer]
                wait(pe, up, "act_lo", up.trips - 2)
                wait(pe, up, "silu_done", up.trips - 1)

                def last_act(eng, kc):
                    if kc == HALF_FF - DOWN_D - 1:
                        wait(eng, up, "act_lo", up.trips - 1)

                def body(i):
                    for d in range(2):
                        wait(pe, st, "x_updated", i, d - 1)
                        if st.ada:
                            ada_half(st, i, 2 * d)
                        project(st, i, st.pos(f"d{d}"), 2 * d, a_hi, a_lo, DOWN_D, width, last=False)
                        if st.ada:
                            ada_half(st, i, 2 * d + 1)
                        project(st, i, st.pos(f"e{d}"), 2 * d, a_hi, a_lo, HALF_FF - DOWN_D, width, first=False,
                                kc0=DOWN_D, ready=last_act if isinstance(i, int) and i == d == 0 else None)
                        if st.ada:
                            ada_turn(st, i, d)
                passes(pe, st, body, first=1)

            pe.wait_ge(s_ones, 1)
            for l in range(DEPTH):
                if l == 0:
                    stage_ada(stage_of["ada", l])
                stage_norm(stage_of["norm1", l], TALL, 2 * l + 1)
                stage_a0(stage_of["A0", l])
                stage_a(stage_of["A", l])
                attention(stage_of["Az", l], "A", 0)
                stage_merge(stage_of["mergeA", l])
                stage_b0(stage_of["B0", l])
                stage_b(stage_of["B", l])
                attention(stage_of["Bz", l], "B", 0)
                stage_merge(stage_of["mergeB", l])
                stage_c(stage_of["C", l])
                stage_merge(stage_of["mergeC", l])
                stage_out(stage_of["out", l])
                stage_norm(stage_of["norm2", l], width_of(l), 2 * l + 2)
                for f in range(2):
                    stage_up(stage_of[f"up{f}", l])
                    stage_down(stage_of[f"down{f}", l])
            stage_norm(stage_of["final", DEPTH - 1], SEQ, 2 * DEPTH + 1)
            for t in range(SEQ // P):
                pe.wait_ge(s_yfm, KC)
                if t >= 2:
                    pe.wait_ge(s_ytok, t - 1)
                for ch in range(KC):
                    ins = pe.transpose(psum[:, 1024 * (1 + t % 2) + ch * P:1024 * (1 + t % 2) + (ch + 1) * P],
                                       y_fm[:, ch, t * P:(t + 1) * P], ident[:])
                ins.then_inc(s_yT, 1)

        @block.scalar
        def _(act):
            prime(act, "ada_rows_copied", "gate_ready", "silu_done")

            def split_hi(blk):
                if blk is None:
                    return
                st, i, k, b = blk
                slot, w = st.slots[k], block_width(st, k)
                act.wait_ge(s_load[slot], load_value(st, i, k))
                last = b - slot_distance(blk)
                if not (isinstance(last, int) and last < 0):
                    act.wait_ge(s_block, last + 1)
                act.activation(part_slot(w_hi, slot)[:, 0:w], raw_slot(slot)[:, 0:w], ACT.Identity)\
                   .then_inc(s_whi, 1)

            def copy(dst, src, scale=1.0):
                return act.activation(dst, src, ACT.Identity, scale=scale)

            AHEAD = 3
            warmed = [0]

            def warm(function):
                n = warmed[0]
                warmed[0] += 1
                act.activation(warm_sb[:, n:n + 1], ones[:, 0:1], function)

            def ada_rows(st, i, u):
                wait_block(act, st, i, st.pos(f"a{2 * u + 1}"))
                wait(act, st, "ada_cols_done", i, u)
                copy(rows[:, :], bank(4)[0:4, 0:ADA_W]).then_inc(s["ada_rows_copied"], 1)

            first = stage_of["ada", 0]
            act.wait_ge(s_ones, 1)
            act.wait_ge(s_vec, DEPTH)
            act.activation(cond[:, :, 0], vec[:, 0, V_C:V_C + KC], ACT.Silu).then_inc(s_cond, 1)
            act.activation(cond[:, :, 1], vec[:, 0, V_CC:V_CC + KC], ACT.Silu).then_inc(s_cond, 1)
            act.wait_ge(s_cond, 2)
            copy(cond4[:, :, 0:4:2], cond[:]).then_inc(s_cond, 1)
            for k in range(AHEAD):
                split_hi(block_at(first, 0, k))

            def square(st, i, k):
                w = width_of(st.layer)
                wait(act, st, "sq_added", i, k - 1)
                wait(act, st, "x_updated", i, k + 1)
                act.activation(sq[:, k, 0:w], x_chunk(i, k, 2)[:, 0:w], ACT.Square).then_inc(s["sq_ready"], 1)

            def stage_ada(st):
                def square_chunk(ch):
                    load_st = stage_of["load", 0]
                    wait(act, load_st, "sq_added", 0, ch - 1)
                    wait(act, load_st, "x_cols_copied", 0, ch + 1)
                    act.activation(sq[:, ch % 2, :], x_t[:, ch, :], ACT.Square).then_inc(s["sq_ready"], 1)

                for u in range(st.ada[2]):
                    for k in range(2 * u + AHEAD, min(2 * u + AHEAD + 2, st.per + 2)):
                        split_hi(block_at(st, 0, k))
                    ada_rows(st, 0, u)
                    if u > 1:
                        square_chunk(u - 2)
                square_chunk(KC - 2)
                square_chunk(KC - 1)

            def root(width, number):
                act.wait_ge(s_sumsq, number)
                act.activation(rstd[:, 0:width // P], bank(5, width // P), ACT.Sqrt, scale=1.0 / D_MODEL,
                               bias=eps[:, 0:1]).then_inc(s_rstd, 1)

            def stage_norm(st, width, number, shift):
                root(width, number)

                def body(i):
                    for k in range(2):
                        wait(act, st, "normed", i, k + 1)
                        for e, t0, t1 in segs(width):
                            ins = act.activation(chunk(h_hi, i, k)[:, t0:t1], normed_t[:, k, t0:t1], ACT.Identity,
                                                 bias=ada_col(st.layer, e, shift, i, k))
                        ins.then_inc(s["h_hi_done"], 1)
                passes(act, st, body)

            def qk_hi(pieces, name, scale):
                for dst, src in pieces:
                    ins = copy(dst, src, scale)
                ins.then_inc(s[name], 1)

            def values_hi(st, i, b):
                wait(act, st, "vt_done", i)
                copy(v_hi[:], psum[:, b * 512:b * 512 + TALL]).then_inc(s["v_hi"], 1)

            def attention(st, kind, i, first_done=None, next_q=None, aside=()):
                aside = list(aside)
                tiles = attention_tiles(kind, st.layer)

                def exps(n, e):
                    if n >= len(tiles):
                        return
                    wait(act, st, "max_done", i, 2 * n + e + 1)
                    c0, c1 = BAND_END - tiles[n][2], SINK + (kind == "B")
                    act.activation(probs[:, n % 2, e, c0 - BAND0:c1 - BAND0],
                                   psum[:, score_base(kind, e) + c0:score_base(kind, e) + c1], ACT.Exp,
                                   bias=nmax[:, n % 2, e:e + 1],
                                   accum_out=rsum[:, n % 2, e:e + 1]).then_inc(s["exp_done"], 1)

                exps(0, 0)
                if kind == "A":
                    values_hi(st, i, 0)
                exps(0, 1)
                g0 = 0
                for n, tile in enumerate(tiles):
                    groups = chunk_groups(tile)

                    def turned(g):
                        wait(act, st, "pt_done", i, g0 + g + 1)
                        w = 2 * P * len(groups[g])
                        copy(pt_hi[:, (g0 + g) % 2, 0:w], bank(turn_bank(kind, g0 + g), w)).then_inc(s["pt_hi"], 1)

                    def step_aside():
                        if n == len(tiles) - 2 and aside:
                            aside.pop(0)()

                    step_aside()
                    turned(0)
                    step_aside()
                    exps(n + 1, 0)
                    step_aside()
                    if len(groups) > 1:
                        turned(1)
                    exps(n + 1, 1)
                    step_aside()
                    if len(groups) > 2:
                        turned(2)
                    if n == len(tiles) - 1 and next_q:
                        next_q()
                    g0 += len(groups)
                    wait(act, st, "o_done", i, n + 1)
                    for dst, src in out_pieces(br_hi, kind, pair_of(st, i), n, tile[0]):
                        ins = copy(dst, src)
                    ins.then_inc(s["o_hi"], 1)
                    if n == 0 and first_done:
                        first_done()

            def v_out(st, i):
                wait_block(act, st, i, st.pos("v"))
                for dst, src in v_pieces_a():
                    ins = copy(dst, src)
                ins.then_inc(s["v_copied"], 1)

            def stage_a0(st):
                wait(act, stage_of["norm1", st.layer], "h_lo_done", 3)
                wait_block(act, st, 0, st.pos("q"))
                qk_hi(q_pieces_a(q_hi, width_of(st.layer), 4), "q_hi", QSCALE)
                wait_block(act, st, 0, st.pos("k"))
                qk_hi(k_pieces_a(k_hi), "k_hi", 1.0)
                v_out(st, 0)
                split_hi(block_at(st, 0, 3))
                split_hi(block_at(st, 0, 4))

            def stage_a(st):
                width = width_of(st.layer)

                def body(i):
                    def next_q():
                        wait_block(act, st, i, st.pos("q"))
                        qk_hi(q_pieces_a(q_hi, width, 0), "q_hi", QSCALE)

                    attention(st, "A", i, lambda: split_hi(block_at(st, i, 2)), next_q)
                    wait_block(act, st, i, st.pos("k"))
                    qk_hi(k_pieces_a(k_hi), "k_hi", 1.0)
                    split_hi(block_at(st, i, 3))
                    v_out(st, i)
                    split_hi(block_at(st, i, 4))
                warm(ACT.Exp)
                passes(act, st, body)

            def swap_quarter(src, n):
                to, frm = 32 * n, 32 * (n + 1 - 2 * (n % 2))
                ins = copy(swap[to:to + 32, :], src[frm:frm + 32, 0:SEQ])
                if n == 3:
                    ins.then_inc(s["swapped"], 1)

            def swap_halves(src):
                for n in range(4):
                    swap_quarter(src, n)

            def stage_b0(st):
                wait(act, stage_of["mergeA", st.layer], "mix_done", 7)
                split_hi(block_at(st, 0, 2))
                wait_block(act, st, 0, st.pos("k"))
                swap_halves(bank(2))
                split_hi(block_at(st, 0, 3))
                wait(act, st, "rotated", 0, 1)
                qk_hi([(k_hi[:, 0:SEQ], rc[:]), (k_hi[:, 640:640 + CTX], bank(3, CTX))], "k_hi", 1.0)
                wait_block(act, st, 0, st.pos("q1"))
                swap_halves(bank(1))
                split_hi(block_at(st, 0, 4))
                wait(act, st, "rotated", 0, 2)
                qk_hi(q_pieces_b(q_hi, st), "q_hi", QSCALE)
                split_hi(block_at(st, 0, 5))
                wait_block(act, st, 0, st.pos("v"))
                copy(v_fm[:, :], psum[:, 2048:2048 + TALL]).then_inc(s["v_copied"], 1)
                values_hi(st, 0, 6)

            def stage_b(st):
                def body(i):
                    def swap_step(n):
                        if n == 0 and st.layer:
                            wait_block(act, st, i, st.pos("q1"))
                        elif n == 0:
                            wait(act, st, "q_summed", i)
                        swap_quarter(bank(1), n)

                    def next_q():
                        wait(act, st, "rotated", i)
                        wait_block(act, st, i, st.pos("q1"))
                        qk_hi(q_pieces_b(q_hi, st), "q_hi", QSCALE)

                    attention(st, "B", i, next_q=next_q, aside=[lambda n=n: swap_step(n) for n in range(4)])
                    split_hi(block_at(st, i, 2))
                    split_hi(block_at(st, i, 3))
                warm(ACT.Exp)
                passes(act, st, body)

            def stage_merge(st):
                width = width_of(st.layer)
                number = "ABC".index(st.name[5])

                def body(i):
                    for k in range(4 if st.ada else 1):
                        split_hi(block_at(st, i, k + 2))
                    wait(act, st, "z_summed", i)
                    wait(act, st, "mix_done", i, 0)
                    act.activation(gate[:, 0:width], psum[:, 0:width], ACT.Sigmoid,
                                   bias=vec_col(st.layer, V_BGATE + KC * number, i)).then_inc(s["gate_ready"], 1)
                    if st.ada:
                        ada_rows(st, i, 0)
                    else:
                        split_hi(block_at(st, i, 3))
                warm(ACT.Sigmoid)
                passes(act, st, body)

            def stage_c(st):
                width = width_of(st.layer)
                wait(act, stage_of["mergeB", st.layer], "mixed", 7)

                def body(i):
                    split_hi(block_at(st, i, 2))
                    wait_block(act, st, i, 0)
                    wait(act, st, "u_done", i, 0)
                    copy(cx_sb[:, 0:width], psum[:, 0:width]).then_inc(s["cx_copied"], 1)
                    split_hi(block_at(st, i, 3))
                    split_hi(block_at(st, i, 4))
                    wait(act, st, "c_done", i)
                    copy(pair(br_hi, i)[:, 0:width], c_out[:, 0:width]).then_inc(s["c_hi"], 1)
                passes(act, st, body)

            def stage_split(st):
                width = width_of(st.layer)
                merge = stage_of["mergeC", st.layer]
                wait(act, merge, "z_summed", 7)
                for ch in range(KC):
                    wait(act, merge, "mixed", ch)
                    copy(h_hi[:, ch, 0:width], merged[:, ch, 0:width]).then_inc(s["h_hi_done"], 1)

            def stage_tiles(st):
                def body(i):
                    half = st.per // 2
                    for k in range(st.per):
                        split_hi(block_at(st, i, k + 2))
                        if st.ada and st.tags[k][0] == "a" and int(st.tags[k][1:]) % 2:
                            ada_rows(st, i, int(st.tags[k][1:]) // 2)
                        if "sq_ready" in st.counts and k % half == half - 1:
                            square(st, i, k // half)
                passes(act, st, body)

            def stage_up(st):
                width = width_of(st.layer)

                warm(ACT.Silu)

                def body(i):
                    split_hi(block_at(st, i, 2))
                    wait_block(act, st, i, 0)
                    wait(act, st, "act_done", i, 0)
                    act.activation(silu_sb[:, 0:width], psum[:, 0:width], ACT.Silu).then_inc(s["silu_done"], 1)
                    split_hi(block_at(st, i, 3))
                    wait(act, st, "act_done", i)
                    copy(tile_of(a_hi, i)[:, 0:width], act_sb[:, 0:width]).then_inc(s["act_hi"], 1)
                passes(act, st, body)

            stage_ada(stage_of["ada", 0])
            act.wait_ge(s_const, 16 * CONSTS)
            copy(mask_b[:], mask_in[:]).then_inc(s_maskb, 1)
            copy(ident_r[:], ident[:]).then_inc(s_maskb, 1)
            for l in range(DEPTH):
                split_hi(block_at(stage_of["A0", l], 0, 2))
                stage_norm(stage_of["norm1", l], TALL, 2 * l + 1, SH1)
                stage_a0(stage_of["A0", l])
                stage_a(stage_of["A", l])
                attention(stage_of["Az", l], "A", 0)
                stage_merge(stage_of["mergeA", l])
                stage_b0(stage_of["B0", l])
                stage_b(stage_of["B", l])
                attention(stage_of["Bz", l], "B", 0)
                stage_merge(stage_of["mergeB", l])
                stage_c(stage_of["C", l])
                stage_merge(stage_of["mergeC", l])
                stage_split(stage_of["split", l])
                stage_tiles(stage_of["out", l])
                stage_norm(stage_of["norm2", l], width_of(l), 2 * l + 2, SH2)
                for f in range(2):
                    stage_up(stage_of[f"up{f}", l])
                    stage_tiles(stage_of[f"down{f}", l])
            root(SEQ, 2 * DEPTH + 1)
            for t in range(SEQ // P):
                act.wait_ge(s_yT, t + 1)
                if t >= 2:
                    act.wait_ge(s_out[t % 2], 16 * (t // 2))
                copy(y_tok[:, t % 2, :], psum[:, 1024 * (1 + t % 2):1024 * (2 + t % 2)]).then_inc(s_ytok, 1)

        @block.vector
        def _(dve):
            prime(dve, "ada_cols_added", "masked", "o_lo", "mix_done", "mixed", "u_done", "c_done", "x_updated",
                  "act_done", "h_lo_done", "c_lo", "act_lo")

            def rest(dst, src, hi, scale=1.0):
                return dve.scalar_tensor_tensor(dst, src, scale, hi.bitcast(F32), ALU.mult, ALU.subtract)

            for l in range(DEPTH):
                dve.wait_ge(s_vecT, l + 1)
                n = V_END if l == 0 else V_FINAL
                dve.tensor_copy(vec[:, l, 0:n], bank(4 + l, n)).then_inc(s_vec, 1)

            def x_out(ch):
                wait(dve, stage_of["load", 0], "x_cols_done", 0, ch + 1)
                dve.tensor_copy(x_t[:, ch, :], psum[:, 1024 * (ch % 2):1024 * (ch % 2) + TALL])\
                   .then_inc(s["x_cols_copied"], 1)

            def split_lo(b):
                st, i, k = blocks[b]
                slot = st.slots[k]
                dve.wait_ge(s_whi, b + 1)
                last = b - distance[b]
                if last >= 0:
                    dve.wait_ge(s_block, last + 1)
                dve.tensor_tensor(part_slot(w_lo, slot), raw_slot(slot), part_slot(w_hi, slot).bitcast(F32),
                                  ALU.subtract).then_inc(s_wlov, 1)

            def ada_cols(st, i, u):
                al, first, n = st.ada
                wait(dve, st, "ada_cols_done", i, u + 1)
                ada_v = ada[:, al, :, 2 * first:48].rearrange("p s (g j) -> p s g j", j=2)
                add_v = vec[:, al, V_BADA + 2 * first:V_BADA + 48].rearrange("p (g j) -> p g j", j=2)
                g = i * n + u
                for e in range(2):
                    ins = dve.tensor_tensor(ada_v[:, e, g, :], bank(5, 4)[:, e:4:2], add_v[:, g, :], ALU.add)
                ins.then_inc(s["ada_cols_added"], 1)

            dve.wait_ge(s_cond, 3)
            dve.tensor_tensor(cond4[:, :, 1:4:2], cond[:], cond4[:, :, 0:4:2].bitcast(F32), ALU.subtract)\
               .then_inc(s_cond, 1)

            def stage_ada(st):
                split_lo(0)
                split_lo(1)
                for u in range(st.ada[2]):
                    if u + 1 < st.ada[2]:
                        split_lo(2 * u + 2)
                        split_lo(2 * u + 3)
                    if u:
                        ada_cols(st, 0, u - 1)
                        x_out(u - 1)
                x_out(KC - 1)
                ada_cols(st, 0, st.ada[2] - 1)

            def modulation(st, which, scale, g, number):
                wait_total(dve, st, "ada_cols_added")
                for e in range(2):
                    ins = dve.scalar_tensor_tensor(a_mod[:, which, e, :],
                                                   ada[:, st.layer, e, KC * scale:KC * scale + KC], 1.0,
                                                   vec[:, st.layer, g:g + KC], ALU.add, ALU.mult)
                ins.then_inc(s_mod, 1)
                dve.wait_ge(s_mod, number)

            def inverse(width, number):
                dve.wait_ge(s_rstd, number)
                dve.reciprocal(rstd[:, 0:width // P], rstd[:, 0:width // P]).then_inc(s_ms, 1)
                dve.wait_ge(s_spread, spreads(number))

            def stage_norm(st, width, number, which, shift):
                modulation(st, which, (SC1, SC2)[which], (V_N1, V_N2)[which], number)
                inverse(width, number)

                def body(i):
                    for k in range(2):
                        wait(dve, st, "h_lo_done", i, k - 1)
                        for e, t0, t1 in segs(width):
                            if e and k == 0 and isinstance(i, int) and i == 0:
                                dve.wait_ge(s_spread, spreads(number) + 1)
                            ins = dve.scalar_tensor_tensor(normed_t[:, k, t0:t1], chunk(x_t, i, k)[:, t0:t1],
                                                           mod_col(which, e, i, k),
                                                           psum[:, 3072 + t0:3072 + t1], ALU.mult,
                                                           ALU.mult)
                        ins.then_inc(s["normed"], 1)
                    for k in range(2):
                        wait(dve, st, "h_hi_done", i, k + 1)
                        for e, t0, t1 in segs(width):
                            ins = dve.scalar_tensor_tensor(chunk(h_lo, i, k)[:, t0:t1], normed_t[:, k, t0:t1],
                                                           ada_col(st.layer, e, shift, i, k),
                                                           chunk(h_hi, i, k)[:, t0:t1].bitcast(F32), ALU.add,
                                                           ALU.subtract)
                        ins.then_inc(s["h_lo_done"], 1)
                passes(dve, st, body, first=1)

            def qk_lo(st, i, his, pieces, name, scale):
                wait(dve, st, name + "_hi", i)
                for (dst, src), (hi, _) in zip(pieces, his):
                    ins = rest(dst, src, hi, scale)
                ins.then_inc(s[name + "_lo"], 1)

            def values_lo(st, i, b):
                wait(dve, st, "v_hi", i)
                rest(v_lo[:], psum[:, b * 512:b * 512 + TALL], v_hi[:]).then_inc(s["v_lo"], 1)

            def attention(st, kind, i, next_q=None, aside=None):
                tiles = attention_tiles(kind, st.layer)
                marks = [0]

                def front(n, e):
                    if n >= len(tiles):
                        return
                    q0, _, width, band, variant = tiles[n]
                    base = score_base(kind, e)
                    wait(dve, st, "scores_done", i, 2 * n + e + 1)
                    if kind == "B" and n == 0:
                        dve.tensor_copy(psum[:, base + SINK:base + SINK + 1], sink_col(st.layer, e, pair_of(st, i)))\
                           .then_inc(s["sunk"], 1)
                        wait(dve, st, "sunk", i, e + 1)
                    if width and kind == "A":
                        at_ = psum[:, base + BAND_END - width:base + BAND_END]
                        by = bias[:, variant, e, :]
                        dve.tensor_tensor(at_, at_, by, ALU.add).then_inc(s["masked"], 1)
                        wait(dve, st, "masked", i, 2 * n + e + 1)
                    c0, c1 = BAND_END - width, SINK + (kind == "B")
                    dve.tensor_reduce(nmax[:, n % 2, e:e + 1], psum[:, base + c0:base + c1], AX.X, ALU.max,
                                      negate=True).then_inc(s["max_done"], 1)

                def normalise(n):
                    for e in range(2):
                        wait(dve, st, "exp_done", i, 2 * n + e + 1)
                        dve.reciprocal(rinv[:, n % 2, e:e + 1], rsum[:, n % 2, e:e + 1]).then_inc(s["inv_done"], 1)
                    for e in range(2):
                        wait(dve, st, "inv_done", i, 2 * n + e + 1)
                        c0 = BAND_END - tiles[n][2] - BAND0
                        part = probs[:, n % 2, e, c0:CTX_END - BAND0]
                        dve.tensor_scalar(part, part, rinv[:, n % 2, e:e + 1], None, ALU.mult)\
                           .then_inc(s["p_done"], 1)

                if kind == "A":
                    wait_before(dve, st, "bias_done", i)
                front(0, 0)
                front(0, 1)
                if kind == "A":
                    values_lo(st, i, 0)
                normalise(0)
                g0 = 0
                for n, tile in enumerate(tiles):
                    groups = chunk_groups(tile)

                    def turned(g):
                        wait(dve, st, "pt_hi", i, g0 + g + 1)
                        par, w = (g0 + g) % 2, 2 * P * len(groups[g])
                        rest(pt_lo[:, par, 0:w], bank(turn_bank(kind, par), w), pt_hi[:, par, 0:w]).then_inc(s["pt_lo"], 1)

                    front(n + 1, 0)
                    front(n + 1, 1)
                    for g in range(len(groups)):
                        turned(g)
                    g0 += len(groups)
                    if n + 1 < len(tiles):
                        normalise(n + 1)
                    if n == len(tiles) - 2 and aside:
                        aside()
                    if n == len(tiles) - 1 and next_q:
                        next_q()
                    wait(dve, st, "o_hi", i, n + 1)
                    for (dst, src), (hi, _) in zip(out_pieces(br_lo, kind, pair_of(st, i), n, tile[0]),
                                                   out_pieces(br_hi, kind, pair_of(st, i), n, tile[0])):
                        ins = rest(dst, src, hi)
                    ins.then_inc(s["o_lo"], 1)

            def stage_a0(st):
                width = width_of(st.layer)
                qk_lo(st, 0, q_pieces_a(q_hi, width, 4), q_pieces_a(q_lo, width, 4), "q", QSCALE)
                qk_lo(st, 0, k_pieces_a(k_hi), k_pieces_a(k_lo), "k", 1.0)

            def stage_a(st):
                width = width_of(st.layer)

                def body(i):
                    attention(st, "A", i, lambda: qk_lo(st, i, q_pieces_a(q_hi, width, 0),
                                                        q_pieces_a(q_lo, width, 0), "q", QSCALE))
                    qk_lo(st, i, k_pieces_a(k_hi), k_pieces_a(k_lo), "k", 1.0)
                passes(dve, st, body)

            def rotate(st, i, n, src):
                wait(dve, st, "swapped", i, n + 1)
                dve.tensor_tensor(rc[:], src, rope[:, 0, :], ALU.mult).then_inc(s["rope_cos"], 1)

            def stage_b0(st):
                rotate(st, 0, 0, bank(2))
                qk_lo(st, 0, [(k_hi[:, 0:SEQ], None), (k_hi[:, 640:640 + CTX], None)],
                      [(k_lo[:, 0:SEQ], rc[:]), (k_lo[:, 640:640 + CTX], bank(3, CTX))], "k", 1.0)
                wait(dve, st, "k_lo", 0)
                rotate(st, 0, 1, bank(1))
                qk_lo(st, 0, q_pieces_b(q_hi, st), q_pieces_b(q_lo, st), "q", QSCALE)
                values_lo(st, 0, 6)

            def stage_b(st):
                def body(i):
                    attention(st, "B", i, lambda: qk_lo(st, i, q_pieces_b(q_hi, st),
                                                        q_pieces_b(q_lo, st), "q", QSCALE),
                              lambda: rotate(st, i, 0, bank(1)))
                passes(dve, st, body)

            def stage_merge(st):
                width = width_of(st.layer)

                def body(i):
                    if st.name == "mergeC" and isinstance(i, int) and i == st.trips - 1:
                        split_rest(st.layer, range(SPLIT_EARLY))
                    wait_block(dve, st, i, st.pos("m"))
                    wait(dve, st, "gate_ready", i)
                    m = tile_of(merged, i)[:, 0:width]
                    if st.name == "mergeA":
                        dve.tensor_tensor(m, psum[:, 1024:1024 + width], gate[:, 0:width], ALU.mult)\
                           .then_inc(s["mix_done"], 1)
                    else:
                        wait(dve, st, "mixed", i, 0)
                        dve.tensor_tensor(mix[:, 0:width], psum[:, 1024:1024 + width], gate[:, 0:width], ALU.mult)\
                           .then_inc(s["mix_done"], 1)
                        wait(dve, st, "mix_done", i)
                        dve.tensor_tensor(m, m, mix[:, 0:width], ALU.add).then_inc(s["mixed"], 1)
                    if st.ada:
                        ada_cols(st, i, 0)
                passes(dve, st, body)

            def stage_c(st):
                width = width_of(st.layer)
                span = width + (2 if width == TALL else 0)

                def body(i):
                    wait_block(dve, st, i, 1)
                    wait(dve, st, "cx_copied", i)
                    for e, t0, t1 in segs(width):
                        ins = dve.tensor_tensor(u_pad[:, t0 + 1 + 2 * e:t1 + 1 + 2 * e], psum[:, 1024 + t0:1024 + t1],
                                                cx_sb[:, t0:t1], ALU.mult)
                    ins.then_inc(s["u_done"], 1)
                    wait(dve, st, "u_done", i)
                    dve.tensor_scalar(y_a[:, 0:span], u_pad[:, 1:span + 1], vec_col(st.layer, V_CONV + 4, i), None,
                                      ALU.mult).then_inc(s["y_step"], 1)
                    wait(dve, st, "y_step", i, 1)
                    dve.scalar_tensor_tensor(y_b[:, 0:span], u_pad[:, 0:span], vec_col(st.layer, V_CONV, i),
                                             y_a[:, 0:span], ALU.mult, ALU.add).then_inc(s["y_step"], 1)
                    wait(dve, st, "y_step", i, 2)
                    dve.scalar_tensor_tensor(y_a[:, 0:span], u_pad[:, 2:span + 2], vec_col(st.layer, V_CONV + 8, i),
                                             y_b[:, 0:span], ALU.mult, ALU.add).then_inc(s["y_step"], 1)
                    wait(dve, st, "y_step", i, 3)
                    wait_block(dve, st, i, 2)
                    wait(dve, st, "c_lo", i, 0)
                    for e, t0, t1 in segs(width):
                        ins = dve.tensor_tensor(c_out[:, t0:t1], psum[:, 2048 + t0:2048 + t1],
                                                y_a[:, t0 + 2 * e:t1 + 2 * e], ALU.mult)
                    ins.then_inc(s["c_done"], 1)
                    wait(dve, st, "c_hi", i)
                    rest(pair(br_lo, i)[:, 0:width], c_out[:, 0:width], pair(br_hi, i)[:, 0:width])\
                        .then_inc(s["c_lo"], 1)

                wait(dve, stage_of["mergeB", st.layer], "mixed", 7)
                dve.memset(u_pad[:, 0:1], 0.0)
                dve.memset(u_pad[:, SEQ + 1:SEQ + 3], 0.0)
                dve.memset(u_pad[:, TALL + 3:TALL + 4], 0.0).then_inc(s_zero, 1)
                dve.wait_ge(s_zero, st.layer + 1)
                passes(dve, st, body)

            def split_rest(l, chunks):
                st, width = stage_of["split", l], width_of(l)
                for ch in chunks:
                    wait(dve, st, "h_hi_done", ch // 2, ch % 2 + 1)
                    rest(h_lo[:, ch, 0:width], merged[:, ch, 0:width], h_hi[:, ch, 0:width])\
                        .then_inc(s["h_lo_done"], 1)

            def stage_residual(st, piece, last_blocks):
                width = width_of(st.layer)

                def body(i):
                    for k in range(2):
                        wait_block(dve, st, i, st.pos(last_blocks[k]))
                        for e, t0, t1 in segs(width):
                            xs = chunk(x_t, i, k)[:, t0:t1]
                            ins = dve.scalar_tensor_tensor(xs, psum[:, 1024 * k + t0:1024 * k + t1],
                                                           ada_col(st.layer, e, piece, i, k), xs, ALU.mult, ALU.add)
                        ins.then_inc(s["x_updated"], 1)
                        if st.ada:
                            ada_cols(st, i, k)
                        if "sq_ready" in st.counts:
                            wait(dve, st, "sq_ready", i, k + 1)
                            wait(dve, st, "sq_added", i, k)
                            dve.tensor_tensor(ssum[:, 0:width], ssum[:, 0:width], sq[:, k, 0:width], ALU.add)\
                               .then_inc(s["sq_added"], 1)
                if "sq_ready" in st.counts:
                    dve.wait_ge(s_ssz, 2 * st.layer + (2 if st.name == "out" else 3))
                passes(dve, st, body)

            def stage_up(st):
                width = width_of(st.layer)

                def body(i):
                    wait_block(dve, st, i, 1)
                    wait(dve, st, "silu_done", i)
                    wait(dve, st, "act_lo", i, 0)
                    dve.tensor_tensor(act_sb[:, 0:width], psum[:, 1024:1024 + width], silu_sb[:, 0:width], ALU.mult)\
                       .then_inc(s["act_done"], 1)
                    wait(dve, st, "act_hi", i)
                    rest(tile_of(a_lo, i)[:, 0:width], act_sb[:, 0:width], tile_of(a_hi, i)[:, 0:width])\
                        .then_inc(s["act_lo"], 1)
                passes(dve, st, body)

            stage_ada(stage_of["ada", 0])
            dve.wait_ge(s_const, 16 * CONSTS)
            for l in range(DEPTH):
                stage_norm(stage_of["norm1", l], TALL, 2 * l + 1, 0, SH1)
                stage_a0(stage_of["A0", l])
                stage_a(stage_of["A", l])
                attention(stage_of["Az", l], "A", 0)
                stage_merge(stage_of["mergeA", l])
                stage_b0(stage_of["B0", l])
                stage_b(stage_of["B", l])
                attention(stage_of["Bz", l], "B", 0)
                stage_merge(stage_of["mergeB", l])
                stage_c(stage_of["C", l])
                stage_merge(stage_of["mergeC", l])
                split_rest(l, range(SPLIT_EARLY, KC))
                stage_residual(stage_of["out", l], G1, ("o0", "o1"))
                stage_norm(stage_of["norm2", l], width_of(l), 2 * l + 2, 1, SH2)
                for f in range(2):
                    stage_up(stage_of[f"up{f}", l])
                    wait(dve, stage_of[f"up{f}", l], "act_lo", HALF_FF - 1)
                    stage_residual(stage_of[f"down{f}", l], G2, ("e0", "e1"))
            inverse(SEQ, 2 * DEPTH + 1)
            for ch in range(KC):
                dve.scalar_tensor_tensor(y_fm[:, ch, :], x_t[:, ch, 0:SEQ], vec[:, 0, V_FINAL + ch:V_FINAL + ch + 1],
                                         psum[:, 3072:3072 + SEQ], ALU.mult, ALU.mult).then_inc(s_yfm, 1)


_INS = ["x", "c", "ctx", "c_ctx", "w_ada", "b_ada", "norm1_g", "norm2_g", "w_in", "b_gate", "na_rpb", "sw_sink",
        "conv_w", "w_br_a", "w_br_b", "w_br_c", "w_o", "w_ffn_up", "w_ffn_down", "final_norm_g"]


def shape_constants():
    import numpy as np

    ident = np.eye(P, dtype=np.float32)
    a = np.arange(P)[:, None] // ROWS
    b = np.arange(2 * P)[None, :] // ROWS
    starts = [np.maximum(a, 8), a, np.minimum(a, 8)]
    masks_a = np.stack([np.where((b >= st) & (b < st + WIN_COLS), 0.0, NEG) for st in starts], 1)
    q, k = np.arange(P)[:, None], np.arange(P)[None, :]
    masks_b = np.stack([np.where(k >= q, 0.0, NEG), np.where(k <= q, 0.0, NEG)], 1)
    t = np.arange(SEQ)
    inv = np.float32(ROPE_THETA) ** (-np.arange(HD // 4, dtype=np.float32) / np.float32(HD // 4))
    ang = np.concatenate([(t // GRID_W).astype(np.float32)[:, None] * inv,
                          (t % GRID_W).astype(np.float32)[:, None] * inv], -1)
    f = np.arange(P) % HD
    cos = np.cos(ang).T[f % 32]
    sin = np.sin(ang).T[f % 32] * np.where(f < 32, -1.0, 1.0)[:, None]
    comb = np.array([[1, 0], [1, 0], [0, 1], [0, 1]])
    return {"ident": ident, "masks_a": masks_a.astype(np.float32), "masks_b": masks_b.astype(np.float32),
            "rope": np.stack([cos, sin], 1).astype(np.float32), "comb": comb.astype(np.float32)}


def kernel(**inputs):
    import numpy as np
    import concourse.bacc as bacc
    from concourse.bass_utils import run_bass_kernel_spmd as run

    nc = bacc.Bacc("TRN2", target_bir_lowering=False, num_devices=1)
    arrays, args = {}, []

    def give(name, a):
        a = np.ascontiguousarray(a)
        arrays[f"in_{name}"] = a
        args.append(nc.dram_tensor(f"in_{name}", a.shape, mybir.dt.from_np(a.dtype), kind="ExternalInput").ap())

    for name in _INS:
        a = np.asarray(inputs[name])
        if name == "na_rpb":
            edge = np.zeros(RPB_PAD, a.dtype)
            a = np.concatenate([edge, a[:, :, ::-1, ::-1].reshape(-1), edge])
        give(name, a)
    for name, a in shape_constants().items():
        give(name, a)
    out = nc.dram_tensor("out_0", (1, SEQ, D_MODEL), F32, kind="ExternalOutput").ap()
    build(nc, *args, out)
    r = run(nc, [arrays], core_ids=[0])
    return r.results[0]["out_0"]
```
